# Optimizing a Trainium2 kernel written in Bass

```python
import math
import jax, jax.numpy as jnp
from jax import lax
import numpy as np

D_MODEL = 2048
BATCH = 1
SEQ = 256
DEPTH = 2
DEC_BATCH = 8
DEC_SEQ = 8
PAST_LEN = 2048
PAGE_SIZE = 128

N_META = 16
EPS = 1e-6
MLSTM_HEADS = 4
MLSTM_DV = D_MODEL // MLSTM_HEADS
MLSTM_DK = MLSTM_DV // 2
MLSTM_CHUNK = 64
QK_WIDTH = MLSTM_HEADS * MLSTM_DK
V_WIDTH = MLSTM_HEADS * MLSTM_DV
MLSTM_IN_WIDTH = 2 * QK_WIDTH + 2 * V_WIDTH + 2 * MLSTM_HEADS
POOL_WINDOWS = (2, 4, 8, 16)
POOL_GROUPS = len(POOL_WINDOWS)
POOL_GROUP_DIM = D_MODEL // POOL_GROUPS
POOL_PAD = max(POOL_WINDOWS) - 1
D_FF = (8 * D_MODEL // 3 + 127) // 128 * 128
CONV_WIDTH = 3
CONV_PAD = CONV_WIDTH - 1
N_MLSTM_LAYERS = (DEPTH + 1) // 2
N_POOL_LAYERS = DEPTH // 2

kernel_name = 'mlstm_pool_hybrid_decode_step'

def rms_norm(x, g):
    xf = x.astype(jnp.float32)
    y = xf * lax.rsqrt(jnp.mean(xf * xf, axis=-1, keepdims=True) + EPS)
    return (y * g.astype(jnp.float32)).astype(x.dtype)

def mlstm_chunk(carry, inp):
    C, n, m = carry
    q, k, v, ig, lf = inp
    L = q.shape[2]
    b = jnp.cumsum(lf, axis=-1)
    causal = jnp.tril(jnp.ones((L, L), dtype=bool))
    d = jnp.where(causal, b[..., :, None] - b[..., None, :] + ig[..., None, :], -jnp.inf)
    inter = b + m[..., None]
    m_t = jnp.maximum(inter, jnp.max(d, axis=-1))
    w_inter = jnp.exp(inter - m_t)
    s = jnp.einsum('bhtk,bhsk->bhts', q, k) * jnp.exp(d - m_t[..., None])
    num = w_inter[..., None] * jnp.einsum('bhtk,bhkv->bhtv', q, C) + jnp.einsum('bhts,bhsv->bhtv', s, v)
    den = w_inter * jnp.einsum('bhtk,bhk->bht', q, n) + jnp.sum(s, axis=-1)
    h = num / jnp.maximum(jnp.abs(den), jnp.exp(-m_t))[..., None]
    m_new = m_t[..., -1]
    decay_prev = jnp.exp(b[..., -1] + m - m_new)
    w_k = jnp.exp(b[..., -1:] - b + ig - m_new[..., None])
    wk = w_k[..., None] * k
    C_new = decay_prev[..., None, None] * C + jnp.einsum('bhsk,bhsv->bhkv', wk, v)
    n_new = decay_prev[..., None] * n + jnp.sum(wk, axis=2)
    return (C_new, n_new, m_new), h

def mlstm_scan(q, k, v, ig, lf, state):
    B, H, S, _ = q.shape
    L = math.gcd(S, MLSTM_CHUNK)
    nc = S // L

    def split(a):
        a = a.reshape(a.shape[:2] + (nc, L) + a.shape[3:])
        return jnp.moveaxis(a, 2, 0)

    state, h = lax.scan(mlstm_chunk, state, (split(q), split(k), split(v), split(ig), split(lf)))
    h = jnp.moveaxis(h, 0, 2).reshape(B, H, S, MLSTM_DV)
    return h, state

def mlstm_mixer(u, w_in, b_gate, g_out, w_out, state, lead):
    B, S, _ = u.shape
    f32 = jnp.float32
    proj = u @ w_in
    q, k, v, o, gates = jnp.split(proj, [QK_WIDTH, 2 * QK_WIDTH, 2 * QK_WIDTH + V_WIDTH, 2 * QK_WIDTH + 2 * V_WIDTH], axis=-1)

    def heads(a, dh):
        return a.reshape(B, S, MLSTM_HEADS, dh).transpose(0, 2, 1, 3).astype(f32)

    q = heads(q, MLSTM_DK) * (MLSTM_DK ** -0.5)
    k = heads(k, MLSTM_DK)
    v = heads(v, MLSTM_DV)
    gates = (gates.astype(f32) + b_gate.astype(f32)).transpose(0, 2, 1)
    ig = gates[:, :MLSTM_HEADS]
    lf = jax.nn.log_sigmoid(gates[:, MLSTM_HEADS:])
    state = tuple(s.astype(f32) for s in state)
    if lead > 0:
        h0, state = mlstm_scan(q[:, :, :lead], k[:, :, :lead], v[:, :, :lead], ig[:, :, :lead], lf[:, :, :lead], state)
        h1, state = mlstm_scan(q[:, :, lead:], k[:, :, lead:], v[:, :, lead:], ig[:, :, lead:], lf[:, :, lead:], state)
        h = jnp.concatenate([h0, h1], axis=2)
    else:
        h, state = mlstm_scan(q, k, v, ig, lf, state)
    h = h * lax.rsqrt(jnp.mean(h * h, axis=-1, keepdims=True) + EPS)
    h = h.transpose(0, 2, 1, 3).reshape(B, S, V_WIDTH) * g_out.astype(f32)
    h = h * jax.nn.sigmoid(o.astype(f32))
    return h.astype(u.dtype) @ w_out, state

def pool_mixer(u, buf, pos0, w_pool, scale):
    B, S, D = u.shape
    f32 = jnp.float32
    ext = jnp.concatenate([buf.astype(f32), u.astype(f32)], axis=1)
    cs = jnp.concatenate([jnp.zeros((B, 1, D), f32), jnp.cumsum(ext, axis=1)], axis=1)
    end = cs[:, POOL_PAD + 1:]
    pos = pos0 + jnp.arange(S)
    groups = []
    for gi, w in enumerate(POOL_WINDOWS):
        sl = slice(gi * POOL_GROUP_DIM, (gi + 1) * POOL_GROUP_DIM)
        start = cs[:, POOL_PAD + 1 - w:POOL_PAD + 1 - w + S, sl]
        cnt = jnp.minimum(w, pos + 1).astype(f32)[None, :, None]
        groups.append((end[..., sl] - start) / cnt)
    pooled = jnp.concatenate(groups, axis=-1) - ext[:, POOL_PAD:]
    y = jnp.einsum('bsgc,gcd->bsgd', pooled.reshape(B, S, POOL_GROUPS, POOL_GROUP_DIM), w_pool.astype(f32))
    y = y.reshape(B, S, D) * scale.astype(f32)
    return y.astype(u.dtype), ext[:, -POOL_PAD:].astype(u.dtype)

def conv_ffn(u, buf, w_up, conv_w, conv_b, w_down):
    S = u.shape[1]
    g, a = jnp.split(u @ w_up, 2, axis=-1)
    ext = jnp.concatenate([buf.astype(g.dtype), g], axis=1)
    gc = conv_b + sum(conv_w[j] * ext[:, j:j + S] for j in range(CONV_WIDTH))
    h = jax.nn.silu(gc) * a
    return h @ w_down, ext[:, -CONV_PAD:]

def trunk(x, st_C, st_n, st_m, st_pool, st_conv, lead, pos0, norm_mix, norm_ffn, norm_final,
          w_mlstm_in, b_mlstm_gate, g_mlstm_out, w_mlstm_out, w_pool, pool_scale, w_up, conv_w, conv_b, w_down):
    new_C, new_n, new_m, new_pool, new_conv = [], [], [], [], []
    for layer in range(DEPTH):
        j = layer // 2
        u = rms_norm(x, norm_mix[layer])
        if layer % 2 == 0:
            y, (C, n, m) = mlstm_mixer(u, w_mlstm_in[j], b_mlstm_gate[j], g_mlstm_out[j], w_mlstm_out[j],
                                       (st_C[j], st_n[j], st_m[j]), lead)
            new_C.append(C)
            new_n.append(n)
            new_m.append(m)
        else:
            y, pbuf = pool_mixer(u, st_pool[j], pos0, w_pool[j], pool_scale[j])
            new_pool.append(pbuf)
        x = x + y.astype(x.dtype)
        u = rms_norm(x, norm_ffn[layer])
        y, cbuf = conv_ffn(u, st_conv[layer], w_up[layer], conv_w[layer], conv_b[layer], w_down[layer])
        new_conv.append(cbuf)
        x = x + y.astype(x.dtype)
    out = rms_norm(x, norm_final)
    return (out, jnp.stack(new_C), jnp.stack(new_n), jnp.stack(new_m), jnp.stack(new_pool), jnp.stack(new_conv))

def setup_inputs(seed: int = 0) -> dict:
    key = jax.random.key(seed)
    ks = jax.random.split(key, 24)
    nrm = jax.random.normal
    H = MLSTM_HEADS
    x_prompt = nrm(ks[0], (BATCH, SEQ, D_MODEL), jnp.float32)
    x_sample = nrm(ks[1], (DEC_BATCH, DEC_SEQ, D_MODEL), jnp.float32)
    state_mlstm_C = 0.5 * nrm(ks[2], (N_MLSTM_LAYERS, DEC_BATCH, H, MLSTM_DK, MLSTM_DV), jnp.float32)
    state_mlstm_n = nrm(ks[3], (N_MLSTM_LAYERS, DEC_BATCH, H, MLSTM_DK), jnp.float32)
    state_mlstm_m = nrm(ks[4], (N_MLSTM_LAYERS, DEC_BATCH, H), jnp.float32)
    state_pool = nrm(ks[5], (N_POOL_LAYERS, DEC_BATCH, POOL_PAD, D_MODEL), jnp.float32)
    state_ffn_conv = nrm(ks[6], (DEPTH, DEC_BATCH, CONV_PAD, D_FF), jnp.float32)
    meta_tokens = nrm(ks[7], (N_META, D_MODEL), jnp.float32)
    norm_mix = 1.0 + 0.02 * nrm(ks[8], (DEPTH, D_MODEL), jnp.float32)
    norm_ffn = 1.0 + 0.02 * nrm(ks[9], (DEPTH, D_MODEL), jnp.float32)
    norm_final = 1.0 + 0.02 * nrm(ks[10], (D_MODEL,), jnp.float32)
    w_mlstm_in = nrm(ks[11], (N_MLSTM_LAYERS, D_MODEL, MLSTM_IN_WIDTH), jnp.float32) * D_MODEL ** -0.5
    f_bias = jnp.linspace(3.0, 6.0, H, dtype=jnp.float32)
    b_mlstm_gate = jnp.concatenate([0.1 * nrm(ks[12], (N_MLSTM_LAYERS, H), jnp.float32),
                                    f_bias + 0.1 * nrm(ks[13], (N_MLSTM_LAYERS, H), jnp.float32)], axis=-1)
    g_mlstm_out = 1.0 + 0.02 * nrm(ks[14], (N_MLSTM_LAYERS, V_WIDTH), jnp.float32)
    w_mlstm_out = nrm(ks[15], (N_MLSTM_LAYERS, V_WIDTH, D_MODEL), jnp.float32) * V_WIDTH ** -0.5
    w_pool = nrm(ks[16], (N_POOL_LAYERS, POOL_GROUPS, POOL_GROUP_DIM, POOL_GROUP_DIM), jnp.float32) * POOL_GROUP_DIM ** -0.5
    pool_scale = 1.0 + 0.02 * nrm(ks[17], (N_POOL_LAYERS, D_MODEL), jnp.float32)
    w_up = nrm(ks[18], (DEPTH, D_MODEL, 2 * D_FF), jnp.float32) * D_MODEL ** -0.5
    conv_w = nrm(ks[19], (DEPTH, CONV_WIDTH, D_FF), jnp.float32) * CONV_WIDTH ** -0.5
    conv_b = 0.01 * nrm(ks[20], (DEPTH, D_FF), jnp.float32)
    w_down = nrm(ks[21], (DEPTH, D_FF, D_MODEL), jnp.float32) * D_FF ** -0.5
    return {'x_prompt': x_prompt, 'x_sample': x_sample,
            'state_mlstm_C': state_mlstm_C, 'state_mlstm_n': state_mlstm_n, 'state_mlstm_m': state_mlstm_m,
            'state_pool': state_pool, 'state_ffn_conv': state_ffn_conv,
            'meta_tokens': meta_tokens, 'norm_mix': norm_mix, 'norm_ffn': norm_ffn, 'norm_final': norm_final,
            'w_mlstm_in': w_mlstm_in, 'b_mlstm_gate': b_mlstm_gate, 'g_mlstm_out': g_mlstm_out,
            'w_mlstm_out': w_mlstm_out, 'w_pool': w_pool, 'pool_scale': pool_scale,
            'w_up': w_up, 'conv_w': conv_w, 'conv_b': conv_b, 'w_down': w_down}

def reference(x_prompt, x_sample, state_mlstm_C, state_mlstm_n, state_mlstm_m, state_pool, state_ffn_conv,
              meta_tokens, norm_mix, norm_ffn, norm_final, w_mlstm_in, b_mlstm_gate, g_mlstm_out, w_mlstm_out,
              w_pool, pool_scale, w_up, conv_w, conv_b, w_down):
    f32 = jnp.float32
    B = x_prompt.shape[0]
    H = MLSTM_HEADS
    weights = (norm_mix, norm_ffn, norm_final, w_mlstm_in, b_mlstm_gate, g_mlstm_out, w_mlstm_out,
               w_pool, pool_scale, w_up, conv_w, conv_b, w_down)
    meta = jnp.broadcast_to(meta_tokens.astype(x_prompt.dtype)[None], (B, N_META, D_MODEL))
    xp = jnp.concatenate([meta, x_prompt], axis=1)
    zC = jnp.zeros((N_MLSTM_LAYERS, B, H, MLSTM_DK, MLSTM_DV), f32)
    zn = jnp.zeros((N_MLSTM_LAYERS, B, H, MLSTM_DK), f32)
    zm = jnp.zeros((N_MLSTM_LAYERS, B, H), f32)
    zpool = jnp.zeros((N_POOL_LAYERS, B, POOL_PAD, D_MODEL), x_prompt.dtype)
    zconv = jnp.zeros((DEPTH, B, CONV_PAD, D_FF), x_prompt.dtype)
    yp, C_p, n_p, m_p, pool_p, conv_p = trunk(xp, zC, zn, zm, zpool, zconv, N_META, 0, *weights)
    y_prompt = yp[:, N_META:]
    y_sample, C_s, n_s, m_s, pool_s, conv_s = trunk(x_sample, state_mlstm_C, state_mlstm_n, state_mlstm_m,
                                                     state_pool, state_ffn_conv, 0, PAST_LEN, *weights)
    return (y_prompt, y_sample, C_p, n_p, m_p, pool_p, conv_p, C_s, n_s, m_s, pool_s, conv_s)


_drawn_inputs = setup_inputs


def setup_inputs(seed=0):
    import zlib

    import numpy as np

    out = dict(_drawn_inputs(seed))
    spreads = {}
    factors = {'norm_final': 8.175,
     'g_mlstm_out': 14.148,
     'pool_scale': 16.116,
     'conv_b': 23.887,
     'norm_ffn': 2.742}
    for name, (base, spread) in spreads.items():
        noise = np.random.default_rng([zlib.crc32(name.encode()), seed]).standard_normal(out[name].shape)
        drawn = base * np.exp(spread * noise) if base else spread * noise
        out[name] = __import__('jax').numpy.asarray(drawn.astype(out[name].dtype))
    for name, factor in factors.items():
        out[name] = (out[name] * factor).astype(out[name].dtype)
    return out
```

```python
from contextlib import ExitStack

import concourse.bass as bass
from concourse import mybir

F32 = mybir.dt.float32
F32R = mybir.dt.float32r
ALU = mybir.AluOpType
ACT = mybir.ActivationFunctionType

P = 128
D = 2048
KT = D // P
META, SEQ = 16, 256
NP = META + SEQ
NB, NS = 8, 8
T = NP + NB * NS
H, DK, DV = 4, 256, 512
QK_W = H * DK
V_W = H * DV
EPS = 1e-6
F = 5504
FT = F // P
TOK = [(0, 128), (128, 128), (256, T - 256)]
TL = TOK[2][1]
PADW = 15
CW = 512
SLOTS = 4
X0, X1, X2, XW = 0, NP, NP + NP - 128, NP + NP - 128 + TL
SEQW = PADW + NS
UW = PADW + NP + NB * SEQW
GW = 2 + NP + NB * (2 + NS)
BIG = -1.0e38

C_HEAD = 3 * (KT // 2) + 4 * 2
C_FFN0 = H * C_HEAD
PASS_T = 8
N_PASS = FT // PASS_T
C_PASS = 4 * (KT // 2) + 4 * (PASS_T // 2)
TAIL_T = FT - N_PASS * PASS_T
C_TAIL = 2 * (KT // 2) + 4 * 2
C_POOL = C_FFN0 + N_PASS * C_PASS + C_TAIL
C_FFN1 = C_POOL + 4 * 2
HB = 2 * N_PASS + 1
C_END = C_FFN1 + N_PASS * C_PASS + C_TAIL
E_HEAD = 12 + 16
E_FFN0 = H * E_HEAD
E_PASS = 16 + 16
E_TAIL = 2 * TAIL_T + 16
E_POOL = E_FFN0 + N_PASS * E_PASS + E_TAIL
E_FFN1 = E_POOL + 16
E_END = E_FFN1 + N_PASS * E_PASS + E_TAIL
G0 = [0, META - 2]
A0 = [0, META]


class Chain:

    def __init__(self, eng, sem):
        self.eng, self.sem, self.base, self.n = eng, sem, 0, 0

    def __call__(self, ins):
        ins.then_inc(self.sem, 1)
        self.n += 1
        self.eng.wait_ge(self.sem, self.base + self.n)

    def mark(self, ins):
        ins.then_inc(self.sem, 1)
        self.n += 1

    def sync(self):
        self.eng.wait_ge(self.sem, self.base + self.n)


def wait_apart(eng, passed, semaphore, value):
    eng.wait_ge(semaphore, value)
    eng.sem_inc(passed, 1)


def program(nc, I, O):
    with ExitStack() as ctx:
        def sb(name, shape, dt=F32):
            return ctx.enter_context(nc.sbuf_tensor(name, shape, dt))

        def sem(name):
            return ctx.enter_context(nc.semaphore(name))

        bank = [ctx.enter_context(nc.psum_tensor(f"bank{i}", [P, 512], F32)) for i in range(8)]
        SA, SB = bank[0:4], bank[4:8]
        YB = SB + [SA[2], SA[3], SA[0], SA[1]]

        x = sb("x", [P, KT, T])
        xh = sb("xh", [P, KT, T], F32R)
        xl = sb("xl", [P, KT, T], F32R)
        w_raw = sb("w_raw", [P, SLOTS, 2, CW])
        w_hi = sb("w_hi", [P, SLOTS, 2, CW], F32R)
        w_lo = sb("w_lo", [P, SLOTS, 2, CW], F32R)
        hh = sb("hh", [P, PASS_T, T], F32R)
        hl = sb("hl", [P, PASS_T, T], F32R)
        ident = sb("ident", [P, P])
        ones = sb("ones", [P, P])
        mask = sb("mask", [P, XW])
        par = sb("par", [P, 7 * KT])
        cpar = sb("cpar", [P, 2, 4, FT])
        cp = sb("cp", [P, 4, PASS_T])
        rbc = sb("rbc", [P, T])
        acc = sb("acc", [P, T])

        rt = sb("rt", [P, T])
        sq = rt
        eps = sb("eps", [P, 1])
        nT = sb("nT", [P, 2, NB, H])
        nP = sb("nP", [P, 2, H])
        mrow = sb("mrow", [H, T])
        mtrow = sb("mtrow", [H, T])
        mm = sb("mm", [H, T])
        negeye = sb("negeye", [H, H])
        gcol = sb("gcol", [P, 3, 2, H])
        hcol = sb("hcol", [P, 3, 2])
        mb = sb("mb", [P, NB, H])
        mbh = sb("mbh", [P, NB])
        nh = sb("nh", [P, 2, NB])
        gh = sb("gh", [P, 4])
        bg = sb("bg", [36, 1])
        rc = sb("rc", [P, 16])
        stat = sb("stat", [P, 8, 3])
        nt2 = sb("nt2", [P, 2, NB])
        AREA = 15700
        area = sb("area", [P, AREA])

        def view(at, n, parts=P):
            assert at + n <= AREA
            return area[0:parts, at:at + n]

        at = 0
        qk = view(0, 4 * T).rearrange("p (f t) -> p f t", t=T)
        v = view(1344, 4 * T).rearrange("p (f t) -> p f t", t=T)
        hn = view(1344, 3 * DV).rearrange("p (s n) -> p s n", n=DV)
        o = view(2880, 4 * T).rearrange("p (f t) -> p f t", t=T)
        ktok = view(4224, 3 * DK).rearrange("p (s n) -> p s n", n=DK)
        vtok = view(4992, 3 * DV).rearrange("p (s n) -> p s n", n=DV)
        X = view(6528, XW)
        PS0 = view(7024, T)
        PS1 = view(7360, T - 128)
        PS2 = view(7568, TL)
        qm = view(7648, 2 * 704).rearrange("p (k n) -> p k n", k=2)
        qn = view(9056, 2 * TL).rearrange("p (k n) -> p k n", k=2)
        WI = view(9216, NB * NS)
        wkp = view(9280, 3 * DK).rearrange("p (s n) -> p s n", n=DK)
        wkb = view(10048, 2 * DK).rearrange("p (s n) -> p s n", n=DK)
        Cst = view(10560, 2 * DV).rearrange("p (k n) -> p k n", n=DV)
        Cr = view(11584, 4 * 2 * DV).rearrange("p (s k n) -> p s k n", s=4, k=2)
        hf = view(0, 4 * T).rearrange("p (f t) -> p f t", t=T)
        junk = view(0, DV)
        xtok = view(0, 3 * D).rearrange("p (s n) -> p s n", n=D)
        ptok = view(6144, P, 7 * KT)
        ctok = view(6272, 4 * P, 86).rearrange("p (s n) -> p s n", n=P)
        ntok = view(6784, DK, NB * H)
        wgr = view(9280, KT * 8).rearrange("p (k n) -> p k n", n=8)
        wgg = view(9408, KT * 36).rearrange("p (k n) -> p k n", n=36)
        sqr = view(9984, 4 * T).rearrange("p (s n) -> p s n", n=T)
        row = [view(11584 + i * T, T, 36) for i in range(12)]
        E = view(0, 4 * GW).rearrange("p (f t) -> p f t", t=GW)
        Tt = view(1416, 4 * GW).rearrange("p (f t) -> p f t", t=GW)
        Sp = view(2832, 4 * T).rearrange("p (f t) -> p f t", t=T)
        fh = view(4176, 4 * T).rearrange("p (f t) -> p f t", t=T)
        hb = view(5520, 2 * CW, 2 * NB).rearrange("p (s n) -> p s n", n=CW)
        tst = view(6544, 2 * CW, 2 * NB + 2).rearrange("p (s n) -> p s n", n=CW)
        last = view(15104, 2 * 4 * 2 * (NB + 1)).rearrange("p (q f n) -> p q f n", q=2, f=4)
        hrow = view(5520, KT * NB * PADW).rearrange("p (f n) -> p f n", f=KT)
        U = view(7568, KT * UW).rearrange("p (f t) -> p f t", t=UW)
        Wa = view(1416, UW)
        Wb = view(1900, UW)
        pbuf = view(13632, D, NB * PADW)
        PD = view(4176, 4 * T).rearrange("p (f t) -> p f t", t=T)
        psto = view(7568, D, NB * PADW)
        pstp = view(9616, D, PADW)
        yT = view(4176, 4 * T).rearrange("p (f t) -> p f t", t=T)
        ytok = view(7568, 3 * D).rearrange("p (s n) -> p s n", n=D)
        nsto = view(5520, DK, NB * H)
        npst = view(5776, DK, H)

        def seqs(ap, pad=0):
            return ap.rearrange("p (b s) -> p b s", s=NS + pad)[:, :, pad:]

        raw_landed = [sem(f"raw_landed{s}") for s in range(SLOTS)]
        hi_done, lo_done, chunk_used = sem("hi_done"), sem("lo_done"), sem("chunk_used")
        evac = sem("accumulator_read")
        act_step, dve_step, pool_step = sem("act_step"), sem("dve_step"), sem("pool_step")
        in_par, in_x, in_gate, in_ntok = sem("in_par"), sem("in_x"), sem("in_gate"), sem("in_ntok")
        consts = sem("consts")
        pe_passed, pool_passed = sem("pe_passed"), sem("pool_passed")
        st_tr, st_ev = sem("start_transposed"), sem("start_read")
        st_sq, st_squ = sem("square_ready"), sem("square_used")
        xh_done, xl_done = sem("xh_done"), sem("xl_done")
        ssq_ready, rms_mm, rt_ready, r_ready = sem("ssq_ready"), sem("rms_mm"), sem("rt_ready"), sem("r_ready")
        wgg_ready, gates_mm = sem("wgg_ready"), sem("gates_mm")
        row_abs, row_exp, row_ln, rows_ready = sem("row_abs"), sem("row_exp"), sem("row_ln"), sem("rows_ready")
        gcol_mm, gcol_a, gcol_em = sem("gcol_mm"), sem("gcol_a"), sem("gcol_em")
        mrow_ready, mb_ready, mb_read = sem("mrow_ready"), sem("mb_ready"), sem("mb_read")
        x_exp, pm_ready, qm_ready = sem("x_exp"), sem("pm_ready"), sem("qm_ready")
        s_ready, kt_ready, ps_ready, ktok_ready = sem("s_ready"), sem("kt_ready"), sem("ps_ready"), sem("ktok_ready")
        sig_done, vt_ready, vtok_a, vtok_v = sem("sig_done"), sem("vt_ready"), sem("vtok_a"), sem("vtok_v")
        num_ready, den_ready, den_read = sem("num_ready"), sem("den_ready"), sem("den_read")
        c_landed = [sem(f"c_landed{s}") for s in range(4)]
        c_stored = [sem(f"c_stored{s}") for s in range(4)]
        wkp_ready, wkb_ready = sem("wkp_ready"), sem("wkb_ready")
        e_zero, cnew_ready, c_updated = sem("e_zero"), sem("cnew_ready"), sem("c_updated")
        cp_ready, cst_ready, cst_stored = sem("cp_ready"), sem("cst_ready"), sem("cst_stored")
        n_ready, n_read, nst_step = sem("n_ready"), sem("n_read"), sem("n_new")
        ss_done, z_ready, z_sqrt, hn_ready = sem("ss_done"), sem("z_ready"), sem("z_sqrt"), sem("hn_ready")
        ht_ready, hf_ready, hh_ready, hl_ready = sem("ht_ready"), sem("hf_ready"), sem("hh_ready"), sem("hl_ready")
        hb_landed = [sem(f"hb_landed{s}") for s in range(2)]
        hist_mm, hist_read, tail_mm, tail_read = sem("hist_mm"), sem("hist_read"), sem("tail_mm"), sem("tail_read")
        tail_stored = [sem(f"tail_stored{s}") for s in range(2)]
        tap0_ready, taps_ready, silu_ready = sem("tap0_ready"), sem("taps_ready"), sem("silu_ready")
        in_pool, ph_mm, ph_read, pd_ready = sem("in_pool"), sem("ph_mm"), sem("ph_read"), sem("pd_ready")
        last_ready, hrow_ready = sem("last_ready"), sem("hrow_ready")
        pt_mm, pt_read, u_zero = sem("pt_mm"), sem("pt_read"), sem("u_zero")
        y_ready, y_mm, y_read, no_mm, no_read = sem("y_ready"), sem("y_mm"), sem("y_read"), sem("no_mm"), sem("no_read")
        stored, pool_stored = sem("stored"), sem("pool_stored")

        block = ctx.enter_context(nc.Block())

        w_in = I["w_mlstm_in"][0].rearrange("(k p) n -> p k n", p=P)
        w_out = I["w_mlstm_out"][0].rearrange("(k p) n -> p k n", p=P)
        w_pool = [I["w_pool"][0, g].rearrange("(k p) n -> p k n", p=P) for g in range(4)]
        w_up = [I["w_up"][i].rearrange("(k p) n -> p k n", p=P) for i in range(2)]
        w_down = [I["w_down"][i].rearrange("(k p) n -> p k n", p=P) for i in range(2)]

        @block.sync
        def _(sp):
            def chunk(c, k, parts):
                s = k % SLOTS
                if not (isinstance(c, int) and c + k < SLOTS):
                    sp.wait_ge(lo_done, c + (k - SLOTS + 1))
                for to, src in parts:
                    sp.dma_start(to(w_raw[:, s]), src).then_inc(raw_landed[s], 16)

            def by_row(w, k0, c0, n=CW):
                return [(lambda r, j=j: r[:, j, 0:n], w[:, bass.ds(k0 + j, 1), bass.ds(c0, n)].rearrange("p a n -> p (a n)"))
                        for j in range(2)]

            def one_row(w, k0, c0):
                return [(lambda r, j=j: r[:, 0, j * 256:j * 256 + 256],
                         w[:, bass.ds(k0, 1), bass.ds(c0 + j * 256, 256)].rearrange("p a n -> p (a n)"))
                        for j in range(2)]

            sp.dma_start(xtok[0:META, 0, :], I["meta_tokens"]).then_inc(in_x, 16)
            sp.dma_start(xtok[META:P, 0, :], I["x_prompt"][0, 0:P - META]).then_inc(in_x, 16)
            sp.dma_start(xtok[:, 1, :], I["x_prompt"][0, P - META:2 * P - META]).then_inc(in_x, 16)
            sp.dma_start(xtok[0:META, 2, :], I["x_prompt"][0, 2 * P - META:SEQ]).then_inc(in_x, 16)
            sp.dma_start(xtok[META:TL, 2, :], I["x_sample"].rearrange("b s d -> (b s) d")).then_inc(in_x, 16)
            vecs = [I["norm_mix"][0], I["norm_mix"][1], I["norm_ffn"][0], I["norm_ffn"][1], I["norm_final"],
                    I["g_mlstm_out"][0], I["pool_scale"][0]]
            for i, a in enumerate(vecs):
                sp.dma_start(ptok[i * KT:(i + 1) * KT, :], a.rearrange("(k p) -> k p", p=P)).then_inc(in_par, 16)
            for i in range(2):
                for j in range(3):
                    sp.dma_start(ctok[(j % 2) * FT:(j % 2) * FT + FT, 2 * i + j // 2, :],
                                 I["conv_w"][i, j].rearrange("(k p) -> k p", p=P)).then_inc(in_par, 16)
                sp.dma_start(ctok[FT:2 * FT, 2 * i + 1, :],
                             I["conv_b"][i].rearrange("(k p) -> k p", p=P)).then_inc(in_par, 16)
            sp.dma_start(ntok, I["state_mlstm_n"][0].rearrange("b h k -> (b h) k")).then_inc(in_par, 16)
            sp.dma_start(wgr, w_in[:, :, 2 * QK_W + 2 * V_W:]).then_inc(in_gate, 16)
            with nc.allow_non_contiguous_dma(reason="40 gate biases and stabilisers"):
                sp.dma_start(bg[0:H, :], I["b_mlstm_gate"][0, 0:H].rearrange("(h a) -> h a", a=1)).then_inc(in_gate, 16)
                sp.dma_start(bg[32:32 + H, :], I["b_mlstm_gate"][0, H:2 * H].rearrange("(h a) -> h a", a=1)).then_inc(in_gate, 16)
                sp.dma_start(row[11][0:H, 0:NB], I["state_mlstm_m"][0].rearrange("b h -> h b")).then_inc(in_gate, 16)
            sp.dma_start(mb[:, :, :].rearrange("p b h -> p (b h)"),
                         I["state_mlstm_m"].rearrange("a b h -> a (b h)").to_broadcast([P, NB * H])).then_inc(in_gate, 16)

            def c_load(h, b):
                if not (isinstance(h, int) and h == 0 and b < 4):
                    sp.wait_ge(c_stored[b % 4], 32 * h + 16 * (b // 4))
                src = I["state_mlstm_C"][0, b].rearrange("h (k p) v -> p (h k) v", p=P)
                sp.dma_start(Cr[:, b % 4], src[:, bass.ds(2 * h, 2), :]).then_inc(c_landed[b % 4], 16)

            def head(h, c):
                for k in range(KT // 2):
                    chunk(c, k, [(lambda r, j=j: r[:, :, j * DK:(j + 1) * DK],
                                  w_in[:, 2 * k:2 * k + 2, bass.ds(j * QK_W + h * DK, DK)]) for j in range(2)])
                for blk in range(2):
                    if blk == 1:
                        if isinstance(h, int) and h == 0:
                            sp.wait_ge(gcol_mm, 1)
                        for b in range(4):
                            c_load(h, b)
                    for k in range(KT // 2):
                        chunk(c, 8 + 8 * blk + k, by_row(w_in, 2 * k, 2 * QK_W + blk * V_W + h * DV))
                for n in range(4):
                    for k in range(2):
                        chunk(c, 24 + 2 * n + k, by_row(w_out, h * 4 + 2 * k, n * CW))
                dst = O["C_sample"][0]
                for b in range(NB):
                    sp.wait_ge(c_updated, NB * h + b + 1)
                    sp.dma_start(dst[b].rearrange("h (k p) v -> p (h k) v", p=P)[:, bass.ds(2 * h, 2), :],
                                 Cr[:, b % 4]).then_inc(c_stored[b % 4], 16)
                    if 1 <= b <= 4:
                        c_load(h, b - 1 + 4)

            def ffn(i, c, j, nq, nt):
                def histories():
                    for q in range(nq):
                        if not isinstance(j, int) or j:
                            sp.wait_ge(hist_mm, i * HB + 2 * j + q - 1)
                        elif i == 0:
                            sp.wait_ge(hl_ready, 4 * H)
                        else:
                            sp.wait_ge(pt_mm, 1)
                        sp.dma_start(hb[:, q, 0:nt * P],
                                     I["state_ffn_conv"][i].rearrange("b r f -> (b r) f")[:, bass.ds((j * 8 + 4 * q) * P, nt * P)]
                                     ).then_inc(hb_landed[q], 16)

                k0 = 0
                for q in range(nq):
                    for a in range(2):
                        for k in range(KT // 2):
                            if (q, a, k) == (0, 0, SLOTS):
                                histories()
                            chunk(c, k0 + k, by_row(w_up[i], 2 * k, a * F + (j * 8 + 4 * q) * P, nt * P))
                        k0 += KT // 2
                kd = nq * nt
                for n in range(4):
                    for k in range(0, kd, 2):
                        f = by_row if k + 1 < kd else one_row
                        chunk(c, k0, f(w_down[i], j * 8 + k, n * CW))
                        k0 += 1

            head(0, 0)
            with sp.Fori(1, H) as h:
                head(h, h * C_HEAD)
            for i, c in ((0, C_FFN0), (1, C_FFN1)):
                ffn(i, c, 0, 2, 4)
                with sp.Fori(1, N_PASS) as j:
                    ffn(i, c + j * C_PASS, j, 2, 4)
                ffn(i, c + N_PASS * C_PASS, N_PASS, 1, TAIL_T)
                if i == 0:
                    for s in range(4):
                        sp.wait_ge(c_stored[s], 2 * H * 16)
                    sp.wait_ge(cst_stored, 16 * H)
                    sp.wait_ge(tail_mm, HB)
                    sp.dma_start(pbuf, I["state_pool"][0].rearrange("b r d -> (b r) d")).then_inc(in_pool, 16)
                    for g in range(4):
                        for k in range(2):
                            chunk(C_POOL, 2 * g + k, by_row(w_pool[g], 2 * k, 0))
            with nc.allow_non_contiguous_dma(reason="36 stabilisers"):
                last = mtrow[:, NP - 1:T:NS]
                sp.dma_start(O["m_prompt"][0].rearrange("b h -> h b"), last[:, 0:1]).then_inc(stored, 16)
                sp.dma_start(O["m_sample"][0].rearrange("b h -> h b"), last[:, 1:]).then_inc(stored, 16)
            sp.wait_ge(no_read, 2)
            sp.dma_start(O["n_sample"][0].rearrange("b h k -> (b h) k"), nsto).then_inc(stored, 16)
            sp.dma_start(O["n_prompt"][0, 0], npst).then_inc(stored, 16)
            for q in range(4):
                for s in range(3):
                    n = NB * NS if s == 2 else P
                    sp.wait_ge(y_read, 3 * q + s + 1)
                    to = O["y_sample"].rearrange("b s d -> (b s) d") if s == 2 else O["y_prompt"][0, s * P:(s + 1) * P]
                    sp.dma_start(to[:, q * 512:(q + 1) * 512], ytok[0:n, s, q * 512:(q + 1) * 512]).then_inc(stored, 16)
            sp.wait_ge(stored, 16 * (2 + 2 + 12))
            for s in range(4):
                sp.wait_ge(c_stored[s], 2 * H * 16)
            sp.wait_ge(cst_stored, 16 * H)
            sp.wait_ge(tail_stored[0], 2 * 32 * (N_PASS + 1))
            sp.wait_ge(tail_stored[1], 2 * 32 * N_PASS)

        @block.tensor
        def _(pe):
            def split_products(out, kt, s, j, m, xhk, xlk, first, last):
                wh, wl = w_hi[:, s, j, m:m + P], w_lo[:, s, j, m:m + P]
                pe.matmul(out, wh, xhk, start=first, stop=False)
                pe.matmul(out, wh, xlk, start=False, stop=False)
                return pe.matmul(out, wl, xhk, start=False, stop=last)

            def gemm(banks, c, k0, nkt, nt, xhi, xlo, c0, free=None, guard=None, fresh=None, amid=None):
                for i in range((nkt + 1) // 2):
                    if amid and i in amid:
                        amid[i]()
                    s = (k0 + i) % SLOTS
                    pe.wait_ge(lo_done, c + (k0 + i + 1))
                    if fresh:
                        fresh(2 * i)
                    for t in range(nt):
                        if i == 0 and free:
                            free(t)
                        if i == 0 and guard and t in guard:
                            pe.wait_ge(*guard[t])
                        for j in range(min(2, nkt - 2 * i)):
                            kt = 2 * i + j
                            mm_ = split_products(banks[t][:, c0:T], kt, s, j, t * P, xhi[:, kt, c0:T], xlo[:, kt, c0:T],
                                                 kt == 0, kt == nkt - 1)
                    mm_.then_inc(chunk_used, 1)

            def after(e):
                return lambda t: pe.wait_ge(evac, e + (t + 1))

            pe.wait_ge(consts, 1)
            pe.wait_ge(in_par, 16 * 16)
            pe.transpose(bank[0][:, 0:7 * KT], ptok, ident[0:7 * KT, 0:7 * KT]).then_inc(st_tr, 1)
            for i in range(2):
                for s in range(2):
                    m_ = pe.transpose(bank[1 + i][:, s * 2 * FT:(s + 1) * 2 * FT], ctok[:, 2 * i + s, :],
                                      ident[0:2 * FT, 0:2 * FT])
                m_.then_inc(st_tr, 1)
            for k in range(2):
                m_ = pe.transpose(bank[3][:, k * 32:(k + 1) * 32], ntok[:, k * P:(k + 1) * P], ident[0:32, 0:32])
            m_.then_inc(st_tr, 1)
            pe.wait_ge(in_x, 16 * 5)
            for kt in range(KT):
                i = 4 + kt
                if i >= 8:
                    pe.wait_ge(st_ev, i - 7)
                for s, (t0, n) in enumerate(TOK):
                    m_ = pe.transpose(bank[i % 8][:, t0:t0 + n], xtok[0:n, s, kt * P:(kt + 1) * P], ident[0:n, 0:n])
                m_.then_inc(st_tr, 1)
            pe.wait_ge(st_ev, 4 + KT)
            pe.wait_ge(wgg_ready, 1)
            for kt in range(KT):
                m_ = pe.matmul(SB[0][0:36, 0:T], wgg[:, kt, :], x[:, kt, :], start=(kt == 0), stop=(kt == KT - 1))
            m_.then_inc(gates_mm, 1)
            for kt in range(KT):
                pe.wait_ge(st_sq, kt + 1)
                m_ = pe.matmul(SB[1][:, 0:T], ones[:, :], sqr[:, kt % 4, :], start=(kt == 0), stop=(kt == KT - 1))
                m_.then_inc(st_squ, 1)

            def sum_squares(out, k):
                pe.wait_ge(ssq_ready, k)
                pe.matmul(out, ones[:, :], acc[:, :], start=True, stop=True).then_inc(rms_mm, 1)

            def head(h, c, e):
                first = isinstance(h, int)
                pe.wait_ge(xl_done, KT)
                gemm(SA, c, 0, KT, 4, xh, xl, 0, free=None if first else after(e - 8))
                if first:
                    pe.wait_ge(rows_ready, 1)
                    for s, (t0, n) in enumerate(TOK):
                        pe.transpose(SB[2][0:n, s * 8:s * 8 + 4], row[8][0:H, t0:t0 + n], ident[0:H, 0:H])
                        m_ = pe.transpose(SB[2][0:n, s * 8 + 4:s * 8 + 8], mtrow[:, t0:t0 + n], ident[0:H, 0:H])
                    m_.then_inc(gcol_mm, 1)
                pe.wait_ge(mrow_ready, h + 1)
                if not first:
                    pe.wait_ge(evac, e)
                pe.matmul(SB[3][:, 0:T], ones[0:H, :], mm[:, :], start=True, stop=True).then_inc(mb_ready, 1)
                guard = {3: (mb_read, h + 1)}
                if first:
                    guard[0] = (rows_ready, 1)
                    guard[1] = (r_ready, 1)
                    guard[2] = (gcol_em, 1)

                def scores():
                    pe.wait_ge(evac, e + 4)
                    for s, (x0, t0, t1, n) in enumerate(((X0, 0, NP, P), (X1, P, NP, P), (X2, 2 * P, T, TL))):
                        for k in range(2):
                            m_ = pe.matmul(SA[0][0:n, x0:x0 + t1 - t0], qk[:, 2 + k, s * P:s * P + n], qk[:, k, t0:t1],
                                           start=(k == 0), stop=(k == 1))
                    m_.then_inc(s_ready, 1)
                    for k in range(2):
                        for s, (t0, n) in enumerate(TOK):
                            m_ = pe.transpose(SA[1 + k][0:n, s * P:(s + 1) * P], qk[:, 2 + k, t0:t0 + n], ident[:, :])
                    m_.then_inc(kt_ready, 1)

                def values():
                    pe.wait_ge(evac, e + 8)
                    pe.wait_ge(ps_ready, h + 1)
                    pe.wait_ge(ktok_ready, h + 1)
                    for f in range(4):
                        for s, (t0, n) in enumerate(TOK):
                            m_ = pe.transpose(SA[f][0:n, s * P:(s + 1) * P], v[:, f, t0:t0 + n], ident[:, :])
                        m_.then_inc(vt_ready, 1)

                gemm(SB, c, 8, KT, 4, xh, xl, 0, free=None if first else after(e - 4), guard=guard, amid={2: scores})
                gemm(SB, c, 16, KT, 4, xh, xl, 0, free=after(e + 4), amid={3: values})
                pe.wait_ge(vtok_v, h + 1)
                pe.wait_ge(vtok_a, h + 1)
                pe.wait_ge(qm_ready, h + 1)
                one = ones[:, 0:1]
                pe.matmul(SA[3][:, 0:1], PS0[:, 0:P], one, start=True, stop=True)
                pe.matmul(SA[3][:, 1:2], PS0[:, P:2 * P], one, start=True, stop=False)
                pe.matmul(SA[3][:, 1:2], PS1[:, 0:P], one, start=False, stop=True)
                pe.matmul(SA[3][0:TL, 2:3], PS0[:, 2 * P:T], one, start=True, stop=False)
                pe.matmul(SA[3][0:TL, 2:3], PS1[:, P:T - P], one, start=False, stop=False)
                pe.matmul(SA[3][0:TL, 2:3], qn[:, 0, :], one, start=False, stop=False)
                pe.matmul(SA[3][0:TL, 2:3], qn[:, 1, :], one, start=False, stop=False)
                pe.matmul(SA[3][0:TL, 2:3], PS2[0:TL, :], ones[0:TL, 0:1], start=False, stop=True).then_inc(den_ready, 1)
                pe.matmul(SA[0][:, :], PS0[:, 0:P], vtok[:, 0, :], start=True, stop=True).then_inc(num_ready, 1)
                pe.matmul(SA[1][:, :], PS0[:, P:2 * P], vtok[:, 0, :], start=True, stop=False)
                pe.matmul(SA[1][:, :], PS1[:, 0:P], vtok[:, 1, :], start=False, stop=True).then_inc(num_ready, 1)
                num2 = SA[2][0:TL, :]
                pe.matmul(num2, PS0[:, 2 * P:T], vtok[:, 0, :], start=True, stop=False)
                pe.matmul(num2, PS1[:, P:T - P], vtok[:, 1, :], start=False, stop=False)
                pe.matmul(num2, PS2[0:TL, :], vtok[0:TL, 2, :], start=False, stop=False)
                for b in range(NB):
                    pe.wait_ge(c_landed[b % 4], 32 * h + 16 * (b // 4 + 1))
                    for k in range(2):
                        m_ = pe.matmul(num2, qm[:, k, b * TL:(b + 1) * TL], Cr[:, b % 4, k, :], start=False,
                                       stop=(b == NB - 1 and k == 1))
                    if b == NB - 1:
                        m_.then_inc(num_ready, 1)
                    pe.wait_ge(wkb_ready, NB * h + b + 1)
                    if b < 2:
                        pe.wait_ge(evac, e + 12)
                    else:
                        pe.wait_ge(c_updated, NB * h + b - 1)
                    for k in range(2):
                        m_ = pe.matmul(SB[2 * (b % 2) + k][:, :], wkb[0:TL, b % 2, k * P:(k + 1) * P], vtok[0:TL, 2, :],
                                       start=True, stop=True)
                    m_.then_inc(cnew_ready, 1)
                pe.wait_ge(wkp_ready, h + 1)
                pe.wait_ge(c_updated, NB * h + NB - 1)
                for k in range(2):
                    for s, (t0, n) in enumerate(TOK):
                        m_ = pe.matmul(SB[k][:, :], wkp[0:n, s, k * P:(k + 1) * P], vtok[0:n, s, :],
                                       start=(s == 0), stop=(s == 2))
                m_.then_inc(cp_ready, 1)
                pe.wait_ge(den_read, h + 1)
                for k in range(2):
                    out = SA[3][:, 16 * k:16 * k + 1 + NB]
                    pe.matmul(out, ktok[0:TL, 2, k * P:(k + 1) * P], X[0:TL, X2 + META - 1:XW:NS], start=True, stop=False)
                    pe.matmul(out[:, 0:1], ktok[:, 0, k * P:(k + 1) * P], X[:, X1 - 1:X1], start=False, stop=False)
                    m_ = pe.matmul(out[:, 0:1], ktok[:, 1, k * P:(k + 1) * P], X[:, X2 - 1:X2], start=False, stop=True)
                m_.then_inc(n_ready, 1)
                pe.wait_ge(c_updated, NB * h + NB)
                pe.wait_ge(cst_ready, h + 1)
                for s, (t0, n) in enumerate(TOK):
                    pe.wait_ge(hn_ready, 3 * h + s + 1)
                    for f in range(4):
                        m_ = pe.transpose(SB[f][:, t0:t0 + n], hn[0:n, s, f * P:(f + 1) * P], ident[0:n, 0:n])
                m_.then_inc(ht_ready, 1)
                pe.wait_ge(n_read, h + 1)
                for n in range(4):
                    gemm((SA, SB)[n % 2], c, 24 + 2 * n, 4, 4, hh, hl, 0,
                         free=after(e + 4 + 4 * n) if n >= 2 else None,
                         fresh=(lambda kt: pe.wait_ge(hl_ready, 4 * h + (kt + 2))) if n == 0 else None)

            def ffn(i, c, e, j, nq, nt):
                first = isinstance(j, int) and j == 0
                fresh = (lambda kt: pe.wait_ge(xl_done, (1 + 2 * i) * KT + kt + 2)) if first else None
                n_q = nq * nt
                eb = 0
                k0 = 0
                for q in range(nq):
                    hj = i * HB + 2 * j + q

                    def history():
                        pe.wait_ge(evac, e + eb)
                        wait_apart(pe, pe_passed, hb_landed[q], 16 * (j + 1 + (i * (N_PASS + 1 - q))))
                        for t in range(nt):
                            m_ = pe.transpose(SB[2][:, t * 2 * NB:(t + 1) * 2 * NB], hb[:, q, t * P:(t + 1) * P],
                                              ident[0:2 * NB, 0:2 * NB])
                        m_.then_inc(hist_mm, 1)

                    gemm(SA, c, k0, KT, nt, xh, xl, G0[i], free=after(e + (eb - 8)), fresh=fresh if q == 0 else None,
                         guard={2: (tail_read, hj)} if q == 1 else None, amid={4: history})
                    k0 += KT // 2
                    if first and q == 0:
                        pe.wait_ge(evac, e)
                        sum_squares(SB[3][:, 0:T], (1, 3)[i])
                    guard = {2: (hist_read, hj + 1)}
                    if first and q == 0:
                        guard[3] = (rt_ready, (2, 4)[i])
                    gemm(SB, c, k0, KT, nt, xh, xl, A0[i], free=after(e + (eb - 4)), guard=guard,
                         amid={4: lambda: tails(q, nt, hj + 1)})
                    k0 += KT // 2
                    eb += 2 * nt
                hj = i * HB + 2 * j + nq
                for n in range(4):
                    if n == 0:
                        free = lambda t: pe.wait_ge(evac, e + (eb - nt))
                    elif n == 1:
                        free = lambda t: pe.wait_ge(evac, e + eb)
                    else:
                        free = after(e + (eb + 4 * n - 8))
                    gemm((SA, SB)[n % 2], c, k0, n_q, 4, hh, hl, A0[i], free=free, guard={2: (tail_read, hj)} if n == 0 else None,
                         fresh=(lambda kt: pe.wait_ge(hl_ready, 4 * H + i * FT + 8 * j + min(kt + 2, n_q))) if n == 0 else None)
                    k0 += (n_q + 1) // 2

            def tails(q, nt, n):
                pe.wait_ge(last_ready, n)
                for t in range(nt):
                    m_ = pe.transpose(SA[2][0:2 * NB + 2, t * P:(t + 1) * P], last[:, q, t], ident[:, :])
                m_.then_inc(tail_mm, 1)

            def pooling():
                pe.wait_ge(evac, E_POOL)
                pe.wait_ge(in_pool, 16)
                for kt in range(KT):
                    m_ = pe.transpose(SB[kt // 4][:, (kt % 4) * 120:(kt % 4) * 120 + 120], pbuf[:, kt * P:(kt + 1) * P],
                                      ident[0:120, 0:120])
                m_.then_inc(ph_mm, 1)
                sum_squares(SA[3][:, 0:T], 2)
                for g in range(4):
                    guard = [{3: (rt_ready, 3)}, {t: (ph_read, 4) for t in range(4)}, None, None][g]
                    gemm((SA, SB)[g % 2], C_POOL, 2 * g, 4, 4, xh[:, 4 * g:4 * g + 4], xl[:, 4 * g:4 * g + 4], 0,
                         free=after(E_POOL + 4 * g - 8) if g >= 2 else None, guard=guard,
                         fresh=lambda kt: pe.wait_ge(xl_done, 2 * KT + 4 * g + kt + 2))
                pe.wait_ge(evac, E_POOL + 12)
                pe.wait_ge(hrow_ready, KT)
                for kt in range(KT):
                    m_ = pe.transpose(SA[kt // 4][0:120, (kt % 4) * P:(kt % 4 + 1) * P], hrow[:, kt], ident[:, :])
                m_.then_inc(pt_mm, 1)
                pe.wait_ge(evac, E_POOL + 16)
                for kt in range(KT):
                    m_ = pe.transpose(SB[kt // 4][0:PADW, (kt % 4) * P:(kt % 4 + 1) * P], U[:, kt, NP:NP + PADW], ident[:, :])
                m_.then_inc(pt_mm, 1)
                pe.wait_ge(pt_read, 8)

            head(0, 0, 0)
            with pe.Fori(1, H) as h:
                head(h, h * C_HEAD, h * E_HEAD)
            for i, c, e in ((0, C_FFN0, E_FFN0), (1, C_FFN1, E_FFN1)):
                ffn(i, c, e, 0, 2, 4)
                with pe.Fori(1, N_PASS) as j:
                    ffn(i, c + j * C_PASS, e + j * E_PASS, j, 2, 4)
                ffn(i, c + N_PASS * C_PASS, e + N_PASS * E_PASS, N_PASS, 1, TAIL_T)
                if i == 0:
                    pooling()
            pe.wait_ge(evac, E_END)
            for k in range(2):
                m_ = pe.transpose(SA[0][0:NB * H, k * P:(k + 1) * P], nT[:, k].rearrange("p b h -> p (b h)"), ident[:, :])
            m_.then_inc(no_mm, 1)
            for k in range(2):
                m_ = pe.transpose(SA[1][0:H, k * P:(k + 1) * P], nP[:, k], ident[:, :])
            m_.then_inc(no_mm, 1)
            sum_squares(SA[3][:, 0:T], 4)
            for kt in range(KT):
                pe.wait_ge(y_ready, kt + 1)
                for s in range(3):
                    i = 3 * (kt // 4) + s
                    if kt % 4 == 0:
                        if i >= 8:
                            pe.wait_ge(y_read, i - 7)
                        elif i >= 6:
                            pe.wait_ge(no_read, i - 5)
                    n = NB * NS if s == 2 else P
                    m_ = pe.transpose(YB[i % 8][0:n, (kt % 4) * P:(kt % 4 + 1) * P], yT[:, kt % 4, META + s * P:META + s * P + n],
                                      ident[:, :])
                m_.then_inc(y_mm, 1)

        @block.scalar
        def _(act):
            def hi(c, k):
                s = k % SLOTS
                if isinstance(c, int) and c + k >= C_END:
                    return
                act.wait_ge(raw_landed[s], c * 8 + 32 * (k // SLOTS + 1))
                if not (isinstance(c, int) and c + k < SLOTS):
                    act.wait_ge(chunk_used, c + (k - SLOTS + 1))
                nc.scalar.activation(w_hi[:, s], w_raw[:, s], ACT.Copy).then_inc(hi_done, 1)

            def his(c, k0, k1):
                for k in range(k0, k1):
                    hi(c, k)

            def x_high(stage, e, gain, c0):
                for kt in range(KT):
                    act.wait_ge(evac, e + kt + 1)
                    nc.scalar.activation(xh[:, kt, c0:], x[:, kt, c0:], ACT.Copy,
                                         scale=par[:, gain * KT + kt:gain * KT + kt + 1]).then_inc(xh_done, 1)

            def rms(ps, k):
                act.wait_ge(rms_mm, k)
                nc.scalar.activation(rt[:, :], ps[:, 0:T], ACT.Sqrt, bias=eps[:, :], scale=1.0 / D).then_inc(rt_ready, 1)

            his(0, 0, SLOTS)
            for kt in range(KT):
                act.wait_ge(st_ev, 5 + kt)
                nc.scalar.activation(xh[:, kt], x[:, kt], ACT.Copy, scale=par[:, kt:kt + 1]).then_inc(xh_done, 1)
                if kt >= 4:
                    act.wait_ge(st_squ, kt - 3)
                nc.scalar.activation(sqr[:, kt % 4], x[:, kt], ACT.Square).then_inc(st_sq, 1)
            act.wait_ge(st_squ, KT)
            nc.scalar.activation(rt[:, :], SB[1][:, 0:T], ACT.Sqrt, bias=eps[:, :], scale=1.0 / D).then_inc(rt_ready, 1)
            act.wait_ge(row_abs, 1)
            nc.scalar.activation(row[5][0:H], row[4][0:H], ACT.Exp).then_inc(row_exp, 1)
            act.wait_ge(row_exp, 1)
            nc.scalar.activation(row[6][0:H], row[5][0:H], ACT.Ln, bias=ones[0:H, 0:1]).then_inc(row_ln, 1)

            def head(h, c, e):
                first = isinstance(h, int)
                his(c, 4, 12)
                if first:
                    act.wait_ge(gcol_a, 1)
                    nc.scalar.activation(gcol[:, :, 1], gcol[:, :, 1], ACT.Exp, scale=-1.0).then_inc(gcol_em, 1)
                act.wait_ge(mb_read, h + 1)
                nc.scalar.activation(X, X, ACT.Exp)
                nc.scalar.activation(WI, WI, ACT.Exp).then_inc(x_exp, 1)
                his(c, 12, 14)
                act.wait_ge(kt_ready, h + 1)
                for k in range(2):
                    nc.scalar.activation(ktok[:, 0:2, k * P:(k + 1) * P],
                                         SA[1 + k][:, 0:2 * P].rearrange("p (s n) -> p s n", n=P), ACT.Copy)
                    m_ = nc.scalar.activation(ktok[0:TL, 2, k * P:(k + 1) * P], SA[1 + k][0:TL, 2 * P:3 * P], ACT.Copy)
                m_.then_inc(ktok_ready, 1)
                his(c, 14, 22)
                for f in range(2):
                    act.wait_ge(vt_ready, 4 * h + f + 1)
                    nc.scalar.activation(vtok[:, 0:2, f * P:(f + 1) * P],
                                         SA[f][:, 0:2 * P].rearrange("p (s n) -> p s n", n=P), ACT.Copy)
                    m_ = nc.scalar.activation(vtok[0:TL, 2, f * P:(f + 1) * P], SA[f][0:TL, 2 * P:3 * P], ACT.Copy)
                m_.then_inc(vtok_a, 1)
                his(c, 22, 28)
                act.wait_ge(evac, e + 12)
                nc.scalar.activation(o, o, ACT.Sigmoid).then_inc(sig_done, 1)
                for s, (t0, n) in enumerate(TOK):
                    act.wait_ge(num_ready, 3 * h + s + 1)
                    nc.scalar.activation(junk[0:n], SA[s][0:n, :], ACT.Square,
                                         accum_out=stat[0:n, 3, s:s + 1]).then_inc(ss_done, 1)
                    act.wait_ge(ss_done, 3 * h + s + 1)
                act.wait_ge(z_ready, h + 1)
                nc.scalar.activation(stat[:, 5], stat[:, 4], ACT.Sqrt, bias=eps[:, :], scale=1.0 / DV).then_inc(z_sqrt, 1)
                act.wait_ge(cp_ready, h + 1)
                if not first:
                    act.wait_ge(cst_stored, 16 * h)
                nc.scalar.activation(Cst[:, 0], SB[0][:, :], ACT.Copy)
                nc.scalar.activation(Cst[:, 1], SB[1][:, :], ACT.Copy).then_inc(cst_ready, 1)
                act.wait_ge(cst_ready, h + 1)
                act.dma_start(O["C_prompt"][0, 0].rearrange("h (k p) v -> p (h k) v", p=P)[:, bass.ds(2 * h, 2), :],
                              Cst).then_inc(cst_stored, 16)
                for f in range(4):
                    act.wait_ge(hf_ready, 4 * h + f + 1)
                    nc.scalar.activation(hh[:, f], hf[:, f], ACT.Copy).then_inc(hh_ready, 1)
                his(c, 28, 36)

            def ffn(i, c, e, j, nq, nt):
                first = isinstance(j, int) and j == 0
                a0 = A0[i]
                eb = k0 = 0
                for q in range(nq):
                    hj = i * HB + 2 * j + q
                    his(c, k0 + 4, k0 + 8)
                    act.wait_ge(hist_mm, hj + 1)
                    if not (i == 0 and first and q == 0):
                        act.wait_ge(last_ready, hj)
                        act.wait_ge(taps_ready, i * FT + 8 * j + 4 * q)
                    else:
                        act.wait_ge(e_zero, 1)
                    nc.scalar.activation(E[:, 0:nt, 2 + NP:].rearrange("p f (b s) -> p f b s", s=NS + 2)[:, :, :, 0:2],
                                         SB[2][:, 0:nt * 2 * NB].rearrange("p (f b s) -> p f b s", b=NB, s=2),
                                         ACT.Copy).then_inc(hist_read, 1)
                    his(c, k0 + 8, k0 + 12)
                    if first and q == 0:
                        rms(SB[3], (1, 3)[i])
                    for t in range(nt):
                        act.wait_ge(evac, e + (eb + t + 1))
                        nc.scalar.activation(Tt[:, t, a0:GW - 2], E[:, t, a0 + 2:GW], ACT.Identity,
                                             bias=cp[:, 3, 4 * q + t:4 * q + t + 1],
                                             scale=cp[:, 2, 4 * q + t:4 * q + t + 1]).then_inc(tap0_ready, 1)
                    for t in range(nt):
                        act.wait_ge(taps_ready, i * FT + 8 * j + (4 * q + t + 1))
                        nc.scalar.activation(Tt[:, t, a0:GW - 2], Tt[:, t, a0:GW - 2], ACT.Silu).then_inc(silu_ready, 1)
                    his(c, k0 + 12, k0 + 16)
                    tails(i, j, q, nt, hj + 1)
                    his(c, k0 + 16, k0 + 20)
                    for t in range(nt):
                        act.wait_ge(evac, e + (eb + nt + t + 1))
                        nc.scalar.activation(hh[:, 4 * q + t, a0:], fh[:, t, a0:], ACT.Copy).then_inc(hh_ready, 1)
                    k0 += KT
                    eb += 2 * nt
                his(c, k0 + 4, k0 + 4 + 4 * ((nq * nt + 1) // 2))

            def tails(i, j, q, nt, n):
                act.wait_ge(tail_mm, n)
                if not (i == 0 and isinstance(j, int) and j == 0):
                    act.wait_ge(tail_stored[q], 32 * (j + i * (N_PASS + 1 - q)))
                nc.scalar.activation(tst[:, q, 0:nt * P], SA[2][0:2 * NB + 2, 0:nt * P], ACT.Copy).then_inc(tail_read, 1)
                act.wait_ge(tail_read, n)
                cols = bass.ds((j * 8 + 4 * q) * P, nt * P)
                act.dma_start(O["conv_prompt"][i, 0][:, cols], tst[0:2, q, 0:nt * P]).then_inc(tail_stored[q], 16)
                act.dma_start(O["conv_sample"][i].rearrange("b r f -> (b r) f")[:, cols],
                              tst[2:2 * NB + 2, q, 0:nt * P]).then_inc(tail_stored[q], 16)

            def pooling():
                act.wait_ge(ph_mm, 1)
                for g in range(4):
                    nc.scalar.activation(
                        U[:, 4 * g:4 * g + 4, PADW + NP:].rearrange("p f (b s) -> p f b s", s=SEQW)[:, :, :, 0:PADW],
                        SB[g][:, 0:480].rearrange("p (f b s) -> p f b s", f=4, b=NB), ACT.Copy).then_inc(ph_read, 1)
                rms(SA[3], 2)
                for kt in range(KT):
                    act.wait_ge(pd_ready, kt + 1)
                    nc.scalar.activation(xh[:, kt], PD[:, kt % 4], ACT.Copy).then_inc(xh_done, 1)
                    if kt in (7, 11):
                        his(C_POOL, 4 + (kt - 7) // 2, 6 + (kt - 7) // 2)
                his(C_POOL, 8, 12)
                act.wait_ge(pt_mm, 2)
                for kt in range(4):
                    nc.scalar.activation(psto[:, kt * 512:(kt + 1) * 512], SA[kt][0:120, :], ACT.Copy).then_inc(pt_read, 1)
                for kt in range(4):
                    nc.scalar.activation(pstp[:, kt * 512:(kt + 1) * 512], SB[kt][0:PADW, :], ACT.Copy).then_inc(pt_read, 1)
                act.wait_ge(pt_read, 8)
                act.dma_start(O["pool_sample"][0].rearrange("b r d -> (b r) d"), psto).then_inc(pool_stored, 16)
                act.dma_start(O["pool_prompt"][0, 0], pstp).then_inc(pool_stored, 16)

            head(0, 0, 0)
            with act.Fori(1, H) as h:
                head(h, h * C_HEAD, h * E_HEAD)
            for i, c, e in ((0, C_FFN0, E_FFN0), (1, C_FFN1, E_FFN1)):
                x_high(1 + 2 * i, e - 16, 2 + i, G0[i])
                ffn(i, c, e, 0, 2, 4)
                with act.Fori(1, N_PASS) as j:
                    ffn(i, c + j * C_PASS, e + j * E_PASS, j, 2, 4)
                ffn(i, c + N_PASS * C_PASS, e + N_PASS * E_PASS, N_PASS, 1, TAIL_T)
                if i == 0:
                    pooling()
            act.wait_ge(no_mm, 2)
            nc.scalar.activation(nsto, SA[0][0:NB * H, 0:DK], ACT.Copy).then_inc(no_read, 1)
            nc.scalar.activation(npst, SA[1][0:H, 0:DK], ACT.Copy).then_inc(no_read, 1)
            rms(SA[3], 4)
            act.wait_ge(pool_stored, 32)
            for i in range(12):
                act.wait_ge(y_mm, 4 * (i // 3) + 4)
                s, q = i % 3, i // 3
                n = NB * NS if s == 2 else P
                nc.scalar.activation(ytok[0:n, s, q * 512:(q + 1) * 512], YB[i % 8][0:n, :], ACT.Copy).then_inc(y_read, 1)

        @block.vector
        def _(dve):
            step = Chain(dve, dve_step)
            V = nc.vector

            def lo(c, k):
                s = k % SLOTS
                if isinstance(c, int) and c + k >= C_END:
                    return
                dve.wait_ge(hi_done, c + (k + 1))
                V.tensor_tensor(w_lo[:, s], w_raw[:, s], w_hi[:, s].bitcast(F32), ALU.subtract).then_inc(lo_done, 1)

            def los(c, k0, k1):
                for k in range(k0, k1):
                    lo(c, k)

            def x_low(stage, gain, c0):
                for kt in range(KT):
                    dve.wait_ge(xh_done, stage * KT + kt + 1)
                    V.scalar_tensor_tensor(xl[:, kt, c0:], x[:, kt, c0:], par[:, gain * KT + kt:gain * KT + kt + 1],
                                           xh[:, kt, c0:].bitcast(F32), ALU.mult, ALU.subtract).then_inc(xl_done, 1)

            def inv_rms(k):
                dve.wait_ge(rt_ready, k)
                V.reciprocal(rbc[:, :], rt[:, :]).then_inc(r_ready, 1)
                dve.wait_ge(r_ready, k)

            def add_to_x(banks, n, c0):
                for t in range(4):
                    V.tensor_tensor(x[:, 4 * n + t, c0:], banks[t][:, c0:T], x[:, 4 * n + t, c0:], ALU.add).then_inc(evac, 1)

            dve.wait_ge(st_tr, 1)
            V.tensor_copy(par[:, :], bank[0][:, 0:7 * KT]).then_inc(st_ev, 1)
            for i in range(2):
                dve.wait_ge(st_tr, 2 + i)
                V.tensor_copy(cpar[:, i].rearrange("p a f -> p (a f)"), bank[1 + i][:, 0:4 * FT]).then_inc(st_ev, 1)
            dve.wait_ge(st_tr, 4)
            V.tensor_copy(nT[:, :, :, :].rearrange("p k b h -> p (k b h)"), bank[3][:, 0:64]).then_inc(st_ev, 1)
            for kt in range(KT):
                dve.wait_ge(st_tr, 5 + kt)
                V.tensor_copy(x[:, kt], bank[(4 + kt) % 8][:, 0:T]).then_inc(st_ev, 1)
            dve.wait_ge(in_gate, 16 * 5)
            dve.wait_ge(consts, 2)
            dve.wait_ge(st_ev, 4)
            gain = par[:, 0:KT].unsqueeze(2).to_broadcast([P, KT, 4])
            V.tensor_tensor(wgg[:, :, 0:4], wgr[:, :, 0:4], gain, ALU.mult)
            V.tensor_tensor(wgg[:, :, 32:36], wgr[:, :, 4:8], gain, ALU.mult).then_inc(wgg_ready, 1)
            los(0, 0, SLOTS)
            dve.wait_ge(st_ev, 4 + KT)
            x_low(0, 0, 0)
            inv_rms(1)
            dve.wait_ge(gates_mm, 1)
            h4 = slice(0, H)
            step(V.tensor_tensor(row[0], SB[0][0:36, 0:T], rbc[0:36, :], ALU.mult))
            V.tensor_scalar(row[1][h4], row[0][h4], bg[0:H, :], None, ALU.add)
            step(V.tensor_scalar(row[2][h4], row[0][32:36], bg[32:36, :], None, ALU.add))
            V.scalar_tensor_tensor(row[4][h4], row[2][h4], -1.0, row[2][h4], ALU.mult, ALU.min).then_inc(row_abs, 1)
            dve.wait_ge(row_ln, 1)
            step(V.scalar_tensor_tensor(row[3][h4], row[2][h4], 0.0, row[6][h4], ALU.min, ALU.subtract))
            step(V.tensor_tensor_scan(row[7][h4], row[9][h4], row[3][h4], 0.0, ALU.mult, ALU.add))
            step(V.tensor_tensor(row[8][h4], row[1][h4], row[7][h4], ALU.subtract))
            step(V.tensor_copy(row[4][h4], row[8][h4]))
            V.tensor_scalar(row[4][h4, 0:1], row[8][h4, 0:1], 0.0, None, ALU.max)
            step(V.tensor_tensor(row[4][h4, NP:T:NS], row[8][h4, NP:T:NS], row[11][h4, 0:NB], ALU.max))
            step(V.tensor_tensor_scan(mrow[:, :], row[10][h4], row[4][h4], 0.0, ALU.add, ALU.max))
            V.tensor_tensor(mtrow[:, :], row[7][h4], mrow[:, :], ALU.add).then_inc(rows_ready, 1)

            def head(h, c, e):
                first = isinstance(h, int)
                if not first:
                    dve.wait_ge(mb_ready, h)
                V.tensor_scalar(mm[:, :], mrow[:, :], negeye[:, bass.ds(h, 1)], None, ALU.mult).then_inc(mrow_ready, 1)
                los(c, 4, 12)
                if first:
                    dve.wait_ge(gcol_mm, 1)
                    V.tensor_copy(gcol[:, 0:2].rearrange("p s a h -> p (s a h)"), SB[2][:, 0:16])
                    V.tensor_copy(gcol[0:TL, 2].rearrange("p a h -> p (a h)"), SB[2][0:TL, 16:24]).then_inc(gcol_a, 1)
                    dve.wait_ge(gcol_em, 1)
                V.tensor_copy(hcol[:, :, :].unsqueeze(3), gcol[:, :, :, bass.ds(h, 1)])
                V.tensor_copy(mbh[:, :].unsqueeze(2), mb[:, :, bass.ds(h, 1)])
                V.tensor_copy(nh[:, :, :].unsqueeze(3), nT[:, :, :, bass.ds(h, 1)])
                step(V.tensor_copy(gh[:, :], par[:, bass.ds(5 * KT + 4 * h, 4)]))
                dve.wait_ge(mb_ready, h + 1)
                nM = SB[3]
                V.tensor_scalar(X[:, X0:X1], nM[:, 0:NP], hcol[:, 0, 0:1], 0.0, ALU.add, ALU.min)
                V.tensor_scalar(X[:, X1:X2], nM[:, P:NP], hcol[:, 1, 0:1], 0.0, ALU.add, ALU.min)
                V.tensor_scalar(X[0:TL, X2:XW], nM[0:TL, 2 * P:T], hcol[0:TL, 2, 0:1], 0.0, ALU.add, ALU.min)
                V.tensor_tensor(seqs(WI), seqs(nM[:, NP:T]), mbh[:, :].unsqueeze(2).to_broadcast([P, NB, NS]),
                                ALU.add).then_inc(mb_read, 1)
                dve.wait_ge(chunk_used, c + 8)
                for t in range(2):
                    V.scalar_tensor_tensor(qk[:, t], SA[t][:, 0:T], DK ** -0.5, rbc[:, :], ALU.mult, ALU.mult).then_inc(evac, 1)
                for t in range(2, 4):
                    V.tensor_tensor(qk[:, t], SA[t][:, 0:T], rbc[:, :], ALU.mult).then_inc(evac, 1)
                dve.wait_ge(x_exp, h + 1)
                V.tensor_tensor(X, X, mask[:, :], ALU.mult).then_inc(pm_ready, 1)
                dve.wait_ge(evac, e + 2)
                for k in range(2):
                    step.mark(V.tensor_tensor(qmb(k), seqs(qk[:, k, NP:T]), seqs(WI), ALU.mult))
                step.sync()
                for k in range(2):
                    m_ = V.tensor_tensor(seqs(qn[:, k, META:TL]), qmb(k), nh[:, k, :].unsqueeze(2).to_broadcast([P, NB, NS]),
                                         ALU.mult)
                m_.then_inc(qm_ready, 1)
                los(c, 12, 14)
                dve.wait_ge(s_ready, h + 1)
                dve.wait_ge(pm_ready, h + 1)
                V.tensor_tensor(PS0[:, 0:NP], SA[0][:, X0:X1], X[:, X0:X1], ALU.mult)
                V.tensor_tensor(PS1[:, 0:NP - P], SA[0][:, X1:X2], X[:, X1:X2], ALU.mult)
                V.tensor_tensor(PS2[0:TL, :], SA[0][0:TL, X2:XW], X[0:TL, X2:XW], ALU.mult).then_inc(ps_ready, 1)
                los(c, 14, 19)
                dve.wait_ge(chunk_used, c + 16)
                for t in range(4):
                    V.tensor_tensor(v[:, t], SB[t][:, 0:T], rbc[:, :], ALU.mult).then_inc(evac, 1)
                los(c, 19, 22)
                for f in range(2, 4):
                    dve.wait_ge(vt_ready, 4 * h + f + 1)
                    V.tensor_copy(vtok[:, 0:2, f * P:(f + 1) * P], SA[f][:, 0:2 * P].rearrange("p (s n) -> p s n", n=P))
                    m_ = V.tensor_copy(vtok[0:TL, 2, f * P:(f + 1) * P], SA[f][0:TL, 2 * P:3 * P])
                m_.then_inc(vtok_v, 1)
                los(c, 22, 27)
                dve.wait_ge(chunk_used, c + 24)
                for t in range(4):
                    V.tensor_tensor(o[:, t], SB[t][:, 0:T], rbc[:, :], ALU.mult).then_inc(evac, 1)
                lo(c, 27)
                dve.wait_ge(den_ready, h + 1)
                V.tensor_copy(stat[:, 0, 0:2], SA[3][:, 0:2])
                V.tensor_copy(stat[0:TL, 0, 2:3], SA[3][0:TL, 2:3]).then_inc(den_read, 1)
                dve.wait_ge(den_read, h + 1)
                step(V.scalar_tensor_tensor(stat[:, 1], stat[:, 0], -1.0, stat[:, 0], ALU.mult, ALU.max))
                step(V.tensor_tensor(stat[:, 1], stat[:, 1], hcol[:, :, 1], ALU.max))
                step(V.reciprocal(stat[:, 2], stat[:, 1]))
                step(V.tensor_tensor(stat[:, 1], stat[:, 2], stat[:, 2], ALU.mult))
                for b in range(NB):
                    dve.wait_ge(cnew_ready, NB * h + b + 1)
                    for k in range(2):
                        m_ = V.scalar_tensor_tensor(Cr[:, b % 4, k], Cr[:, b % 4, k], WI[:, NS * b + NS - 1:NS * b + NS],
                                                    SB[2 * (b % 2) + k][:, :], ALU.mult, ALU.add)
                    m_.then_inc(c_updated, 1)
                dve.wait_ge(ss_done, 3 * h + 3)
                V.tensor_tensor(stat[:, 4], stat[:, 1], stat[:, 3], ALU.mult).then_inc(z_ready, 1)
                dve.wait_ge(z_sqrt, h + 1)
                step(V.reciprocal(stat[:, 6], stat[:, 5]))
                step(V.tensor_tensor(stat[:, 7], stat[:, 6], stat[:, 2], ALU.mult))
                for s, (t0, n) in enumerate(TOK):
                    V.tensor_scalar(hn[0:n, s], SA[s][0:n, :], stat[0:n, 7, s:s + 1], None, ALU.mult).then_inc(hn_ready, 1)
                dve.wait_ge(n_ready, h + 1)
                for k in range(2):
                    step.mark(V.tensor_tensor(nt2[:, k], nh[:, k], WI[:, NS - 1::NS], ALU.mult))
                step.sync()
                for k in range(2):
                    V.tensor_tensor(nT[:, k, :, bass.ds(h, 1)], nt2[:, k].unsqueeze(2), SA[3][:, 16 * k + 1:16 * k + 9].unsqueeze(2),
                                    ALU.add)
                    m_ = V.tensor_copy(nP[:, k, bass.ds(h, 1)], SA[3][:, 16 * k:16 * k + 1])
                m_.then_inc(n_read, 1)
                dve.wait_ge(ht_ready, h + 1)
                dve.wait_ge(sig_done, h + 1)
                for f in range(4):
                    V.scalar_tensor_tensor(hf[:, f], SB[f][:, 0:T], gh[:, f:f + 1], o[:, f], ALU.mult, ALU.mult).then_inc(hf_ready, 1)
                for f in range(4):
                    dve.wait_ge(hh_ready, 4 * h + f + 1)
                    V.tensor_tensor(hl[:, f], hf[:, f], hh[:, f].bitcast(F32), ALU.subtract).then_inc(hl_ready, 1)
                for n in range(4):
                    los(c, 28 + 2 * n, 30 + 2 * n)
                    dve.wait_ge(chunk_used, c + (26 + 2 * n))
                    add_to_x((SA, SB)[n % 2], n, 0)

            def qmb(k):
                return qm[:, k].rearrange("p (b s) -> p b s", s=TL + NS)[:, :, META:META + NS]

            def ffn(i, c, e, j, nq, nt):
                first = isinstance(j, int) and j == 0
                a0, g0 = A0[i], G0[i]
                eb = k0 = 0
                V.tensor_copy(cp[:, :, 0:nq * nt], cpar[:, i, :, bass.ds(8 * j, nq * nt)])
                for q in range(nq):
                    los(c, k0 + 4, k0 + 11)
                    if first and q == 0:
                        inv_rms((2, 4)[i])
                    dve.wait_ge(chunk_used, c + (k0 + 8))
                    if not (i == 0 and first and q == 0):
                        dve.wait_ge(last_ready, i * HB + 2 * j + q)
                    for t in range(nt):
                        V.tensor_tensor(E[:, t, 2 + g0:2 + NP], SA[t][:, g0:NP], rbc[:, g0:NP], ALU.mult)
                        V.tensor_tensor(seqs(E[:, t, 2 + NP:], 2), seqs(SA[t][:, NP:T]), seqs(rbc[:, NP:T]), ALU.mult).then_inc(evac, 1)
                    lo(c, k0 + 11)
                    dve.wait_ge(hist_read, i * HB + 2 * j + q + 1)
                    for t in range(nt):
                        f = 4 * q + t
                        dve.wait_ge(tap0_ready, i * FT + 8 * j + (f + 1))
                        step(V.scalar_tensor_tensor(Tt[:, t, a0:GW - 2], E[:, t, a0 + 1:GW - 1], cp[:, 1, f:f + 1],
                                                    Tt[:, t, a0:GW - 2], ALU.mult, ALU.add))
                        V.scalar_tensor_tensor(Tt[:, t, a0:GW - 2], E[:, t, a0:GW - 2], cp[:, 0, f:f + 1],
                                               Tt[:, t, a0:GW - 2], ALU.mult, ALU.add).then_inc(taps_ready, 1)
                    for t in range(nt):
                        dve.wait_ge(silu_ready, i * FT + 8 * j + (4 * q + t + 1))
                        V.tensor_tensor(Sp[:, t, a0:NP], Tt[:, t, a0:NP], rbc[:, a0:NP], ALU.mult)
                        m_ = V.tensor_tensor(seqs(Sp[:, t, NP:T]),
                                             Tt[:, t, 2 + NP:].rearrange("p (b s) -> p b s", s=NS + 2)[:, :, 0:NS],
                                             seqs(rbc[:, NP:T]), ALU.mult)
                        step.mark(m_)
                    los(c, k0 + 12, k0 + 19)
                    dve.wait_ge(chunk_used, c + (k0 + 16))
                    step.sync()
                    for t in range(nt):
                        V.tensor_tensor(fh[:, t, a0:], SB[t][:, a0:T], Sp[:, t, a0:], ALU.mult).then_inc(evac, 1)
                    lo(c, k0 + 19)
                    for t in range(nt):
                        dve.wait_ge(hh_ready, 4 * H + i * FT + 8 * j + (4 * q + t + 1))
                        V.tensor_tensor(hl[:, 4 * q + t, a0:], fh[:, t, a0:], hh[:, 4 * q + t, a0:].bitcast(F32),
                                        ALU.subtract).then_inc(hl_ready, 1)
                    k0 += KT
                    eb += 2 * nt
                nd = (nq * nt + 1) // 2
                for n in range(4):
                    los(c, k0 + 4, k0 + 3 + nd)
                    k0 += nd
                    dve.wait_ge(chunk_used, c + k0)
                    add_to_x((SA, SB)[n % 2], n, a0)
                    lo(c, k0 + 3)

            def pooling():
                inv_rms(3)
                dve.wait_ge(in_pool, 16)
                V.memset(U[:, :, 0:PADW], 0.0)

                def low(kt):
                    dve.wait_ge(xh_done, 2 * KT + kt + 1)
                    V.tensor_tensor(xl[:, kt], PD[:, kt % 4], xh[:, kt].bitcast(F32), ALU.subtract).then_inc(xl_done, 1)

                def out(g):
                    dve.wait_ge(chunk_used, C_POOL + 2 * g + 2)
                    for t in range(4):
                        f = 4 * g + t
                        V.scalar_tensor_tensor(x[:, f], (SA, SB)[g % 2][t][:, 0:T], par[:, 6 * KT + f:6 * KT + f + 1], x[:, f],
                                               ALU.mult, ALU.add).then_inc(evac, 1)

                for kt in range(KT):
                    w = 2 << (kt // 4)
                    u, pd = U[:, kt], PD[:, kt % 4]
                    gk = par[:, KT + kt:KT + kt + 1]
                    V.scalar_tensor_tensor(u[:, PADW:PADW + NP], x[:, kt, 0:NP], gk, rbc[:, 0:NP], ALU.mult, ALU.mult)
                    step(V.scalar_tensor_tensor(seqs(u[:, PADW + NP:], PADW), seqs(x[:, kt, NP:]), gk, seqs(rbc[:, NP:]),
                                                ALU.mult, ALU.mult))
                    if kt == 0:
                        dve.wait_ge(ph_read, 4)
                    src, n, at = u, 1, 0
                    while n < w:
                        at += n
                        to = (Wa, Wb)[n in (2, 8)]
                        step(V.tensor_tensor(to[:, at:], src[:, at:], src[:, at - n:UW - n], ALU.add))
                        src, n = to, 2 * n
                    V.scalar_tensor_tensor(pd[:, 0:NP], src[:, PADW:PADW + NP], 1.0 / w, u[:, PADW:PADW + NP], ALU.mult, ALU.subtract)
                    step(V.scalar_tensor_tensor(seqs(pd[:, NP:]), seqs(src[:, PADW + NP:], PADW), 1.0 / w,
                                                seqs(u[:, PADW + NP:], PADW), ALU.mult, ALU.subtract))
                    step(V.tensor_tensor(pd[:, 0:w - 1], src[:, PADW:PADW + w - 1], rc[:, 0:w - 1], ALU.mult))
                    V.tensor_tensor(pd[:, 0:w - 1], pd[:, 0:w - 1], u[:, PADW:PADW + w - 1], ALU.subtract).then_inc(pd_ready, 1)
                    if kt:
                        low(kt - 1)
                    if kt in (7, 11):
                        los(C_POOL, 4 + (kt - 7) // 2, 6 + (kt - 7) // 2)
                        out((kt - 7) // 4)
                low(KT - 1)
                los(C_POOL, 8, 10)
                out(2)
                los(C_POOL, 10, 12)
                out(3)

            step.base, step.n, before = 0, step.n, step.n
            head(0, 0, 0)
            per, step.n = step.n - before, before
            with dve.Fori(1, H) as h:
                step.base = h * per
                head(h, h * C_HEAD, h * E_HEAD)
            step.base = (H - 1) * per
            dve.wait_ge(hl_ready, 4 * H)
            V.memset(E[:, :, 0:2], 0.0).then_inc(e_zero, 1)
            for i, c, e in ((0, C_FFN0, E_FFN0), (1, C_FFN1, E_FFN1)):
                x_low(1 + 2 * i, 2 + i, G0[i])
                before, base = step.n, step.base
                ffn(i, c, e, 0, 2, 4)
                per, step.n = step.n - before, before
                with dve.Fori(1, N_PASS) as j:
                    step.base = j * per + base
                    ffn(i, c + j * C_PASS, e + j * E_PASS, j, 2, 4)
                step.base = (N_PASS - 1) * per + base
                ffn(i, c + N_PASS * C_PASS, e + N_PASS * E_PASS, N_PASS, 1, TAIL_T)
                if i == 0:
                    pooling()
            inv_rms(5)
            for kt in range(KT):
                if kt >= 4:
                    dve.wait_ge(y_mm, kt - 3)
                V.scalar_tensor_tensor(yT[:, kt % 4, META:], x[:, kt, META:], par[:, 4 * KT + kt:4 * KT + kt + 1],
                                       rbc[:, META:], ALU.mult, ALU.mult).then_inc(y_ready, 1)

        @block.gpsimd
        def _(pool):
            step = Chain(pool, pool_step)
            G = nc.gpsimd
            G.memset(ones[:, :], 1.0)
            step(G.memset(ident[:, :], 0.0))
            G.affine_select(out=ident[:, :], in_=ident[:, :], compare_op=ALU.not_equal, fill=1.0, base=0,
                            pattern=[[-1, P]], channel_multiplier=1).then_inc(consts, 1)
            G.memset(eps[:, :], EPS)
            G.memset(stat[:, :, :], 1.0)
            G.memset(gcol[:, :, :, :], 0.0)
            G.memset(row[9][0:H], 1.0)
            G.memset(row[10][0:H], 0.0)
            G.memset(negeye[:, :], 0.0)
            for t in range(16):
                G.memset(rc[:, t:t + 1], 1.0 / (t + 1))
            step(G.memset(wgg, 0.0))
            for s, value in ((9, 0.0), (10, BIG)):
                G.memset(row[s][0:H, 0:1], value)
                G.memset(row[s][0:H, NP:T:NS], value)
            step(G.affine_select(out=negeye[:, :], in_=negeye[:, :], compare_op=ALU.not_equal, fill=-1.0, base=0,
                                 pattern=[[-1, H]], channel_multiplier=1))
            step(G.memset(mask[:, :], 1.0))
            for x0, x1 in ((X0, X1), (X1, X2)):
                G.affine_select(out=mask[:, x0:x1], in_=mask[:, x0:x1], compare_op=ALU.is_ge, fill=0.0, base=0,
                                pattern=[[1, x1 - x0]], channel_multiplier=-1)
            step(G.affine_select(out=mask[:, X2:XW], in_=mask[:, X2:XW], compare_op=ALU.is_ge, fill=0.0, base=0,
                                 pattern=[[1, TL]], channel_multiplier=-1))
            own = mask[:, X2 + META:XW].rearrange("p (b s) -> p b s", s=NS)
            G.affine_select(out=own, in_=own, compare_op=ALU.is_ge, fill=0.0, base=-META,
                            pattern=[[-NS, NB], [0, NS]], channel_multiplier=1)
            pool.wait_ge(st_tr, 4)
            G.memset(area[:, 6528:9216], 0.0).then_inc(consts, 1)

            def sum_of_squares(k, e, c0):
                for kt in range(KT):
                    pool.wait_ge(evac, e + kt + 1)
                    if kt == 0:
                        if k > 1:
                            pool.wait_ge(rms_mm, k - 1)
                        step(G.tensor_tensor(acc[:, c0:], x[:, kt, c0:], x[:, kt, c0:], ALU.mult))
                        continue
                    step(G.tensor_tensor(sq[:, c0:], x[:, kt, c0:], x[:, kt, c0:], ALU.mult))
                    m_ = G.tensor_tensor(acc[:, c0:], acc[:, c0:], sq[:, c0:], ALU.add)
                    if kt < KT - 1:
                        step(m_)
                m_.then_inc(ssq_ready, 1)

            def head(h):
                first = isinstance(h, int)
                pool.wait_ge(pm_ready, h + 1)
                pool.wait_ge(ktok_ready, h + 1)
                for b in range(NB):
                    if not (first and b < 2):
                        wait_apart(pool, pool_passed, cnew_ready, NB * h + b - 1)
                    col = X2 + META + NS * b + NS - 1
                    G.tensor_scalar(wkb[0:TL, b % 2], ktok[0:TL, 2], X[0:TL, col:col + 1], None, ALU.mult).then_inc(wkb_ready, 1)
                    if b == 1:
                        G.tensor_scalar(wkp[:, 0], ktok[:, 0], X[:, X1 - 1:X1], None, ALU.mult)
                        G.tensor_scalar(wkp[:, 1], ktok[:, 1], X[:, X2 - 1:X2], None, ALU.mult)
                        G.tensor_scalar(wkp[0:TL, 2], ktok[0:TL, 2], X[0:TL, X2 + META - 1:X2 + META], None,
                                        ALU.mult).then_inc(wkp_ready, 1)

            head(0)
            with pool.Fori(1, H) as h:
                head(h)

            def last_rows(i, e, j, nq, nt):
                for q in range(nq):
                    n = i * HB + 2 * j + q
                    if not (isinstance(j, int) and j == 0):
                        pool.wait_ge(tail_mm, n - 1)
                    elif i:
                        pool.wait_ge(tail_mm, HB)
                    for t in range(nt):
                        wait_apart(pool, pool_passed, evac, e + (2 * nt * q + t + 1))
                        m_ = G.tensor_copy(last[:, q, t].rearrange("p (b s) -> p b s", s=2),
                                           E[:, t, NP - NS:].rearrange("p (b s) -> p b s", s=NS + 2)[:, :, NS:])
                    m_.then_inc(last_ready, 1)

            pool.wait_ge(c_stored[2], 2 * H * 16)
            pool.wait_ge(c_stored[3], 2 * H * 16)
            for i, e in ((0, E_FFN0), (1, E_FFN1)):
                sum_of_squares(1 + 2 * i, e - 16, 0)
                last_rows(i, e, 0, 2, 4)
                with pool.Fori(1, N_PASS) as j:
                    last_rows(i, e + j * E_PASS, j, 2, 4)
                last_rows(i, e + N_PASS * E_PASS, N_PASS, 1, TAIL_T)
                if i == 0:
                    sum_of_squares(2, E_POOL - 16, 0)
                    pool.wait_ge(tail_stored[0], 32 * (N_PASS + 1))
                    pool.wait_ge(tail_stored[1], 32 * N_PASS)
                    for kt in range(KT):
                        pool.wait_ge(pd_ready, kt + 1)
                        G.tensor_copy(hrow[:, kt].rearrange("p (b s) -> p b s", s=PADW),
                                      U[:, kt, PADW + NP:].rearrange("p (b s) -> p b s", s=SEQW)[:, :, NS:]).then_inc(hrow_ready, 1)
            sum_of_squares(4, E_END - 16, 0)


INPUTS = ["x_prompt", "x_sample", "state_mlstm_C", "state_mlstm_n", "state_mlstm_m", "state_pool", "state_ffn_conv",
          "meta_tokens", "norm_mix", "norm_ffn", "norm_final", "w_mlstm_in", "b_mlstm_gate", "g_mlstm_out",
          "w_mlstm_out", "w_pool", "pool_scale", "w_up", "conv_w", "conv_b", "w_down"]
OUTPUTS = [("y_prompt", (1, SEQ, D)), ("y_sample", (NB, NS, D)), ("C_prompt", (1, 1, H, DK, DV)), ("n_prompt", (1, 1, H, DK)),
           ("m_prompt", (1, 1, H)), ("pool_prompt", (1, 1, PADW, D)), ("conv_prompt", (2, 1, 2, F)),
           ("C_sample", (1, NB, H, DK, DV)), ("n_sample", (1, NB, H, DK)), ("m_sample", (1, NB, H)),
           ("pool_sample", (1, NB, PADW, D)), ("conv_sample", (2, NB, 2, F))]


def kernel(**inputs):
    import numpy as np
    from concourse import bacc
    from concourse.bass_utils import run_bass_kernel_spmd

    nc = bacc.Bacc("TRN2", target_bir_lowering=False, num_devices=1)
    arrays, I, O = {}, {}, {}
    for name in INPUTS:
        a = np.ascontiguousarray(inputs[name])
        arrays[f"in_{name}"] = a
        I[name] = nc.dram_tensor(f"in_{name}", a.shape, mybir.dt.from_np(a.dtype), kind="ExternalInput").ap()
    for name, shape in OUTPUTS:
        O[name] = nc.dram_tensor(f"out_{name}", shape, F32, kind="ExternalOutput").ap()
    program(nc, I, O)
    r = run_bass_kernel_spmd(nc, [arrays], core_ids=[0])
    return tuple(r.results[0][f"out_{name}"] for name, _ in OUTPUTS)
```

```python
from contextlib import ExitStack

import concourse.bass as bass
from concourse import mybir

F32 = mybir.dt.float32
F32R = mybir.dt.float32r
ALU = mybir.AluOpType
ACT = mybir.ActivationFunctionType

P = 128
D = 2048
KT = D // P
META, SEQ = 16, 256
NP = META + SEQ
NB, NS = 8, 8
T = NP + NB * NS
H, DK, DV = 4, 256, 512
QK_W = H * DK
V_W = H * DV
EPS = 1e-6
F = 5504
FT = F // P
TOK = [(0, 128), (128, 128), (256, T - 256)]
TL = TOK[2][1]
PADW = 15
CW = 512
SLOTS = 4
X0, X1, X2, XW = 0, NP, NP + NP - 128, NP + NP - 128 + TL
SEQW = PADW + NS
UW = PADW + NP + NB * SEQW
GW = 2 + NP + NB * (2 + NS)
BIG = -1.0e38

C_HEAD = 3 * (KT // 2) + 4 * 2
C_FFN0 = H * C_HEAD
PASS_T = 8
N_PASS = FT // PASS_T
C_PASS = 4 * (KT // 2) + 4 * (PASS_T // 2)
TAIL_T = FT - N_PASS * PASS_T
C_TAIL = 2 * (KT // 2) + 4 * 2
C_POOL = C_FFN0 + N_PASS * C_PASS + C_TAIL
C_FFN1 = C_POOL + 4 * 2
HB = 2 * N_PASS + 1
C_END = C_FFN1 + N_PASS * C_PASS + C_TAIL
E_HEAD = 12 + 16
E_FFN0 = H * E_HEAD
E_PASS = 16 + 16
E_TAIL = 2 * TAIL_T + 16
E_POOL = E_FFN0 + N_PASS * E_PASS + E_TAIL
E_FFN1 = E_POOL + 16
E_END = E_FFN1 + N_PASS * E_PASS + E_TAIL
G0 = [0, META - 2]
A0 = [0, META]


class Chain:

    def __init__(self, eng, sem):
        self.eng, self.sem, self.base, self.n = eng, sem, 0, 0

    def __call__(self, ins):
        ins.then_inc(self.sem, 1)
        self.n += 1
        self.eng.wait_ge(self.sem, self.base + self.n)

    def mark(self, ins):
        ins.then_inc(self.sem, 1)
        self.n += 1

    def sync(self):
        self.eng.wait_ge(self.sem, self.base + self.n)


def wait_apart(eng, passed, semaphore, value):
    eng.wait_ge(semaphore, value)
    eng.sem_inc(passed, 1)


def program(nc, I, O):
    with ExitStack() as ctx:
        def sb(name, shape, dt=F32):
            return ctx.enter_context(nc.sbuf_tensor(name, shape, dt))

        def sem(name):
            return ctx.enter_context(nc.semaphore(name))

        bank = [ctx.enter_context(nc.psum_tensor(f"bank{i}", [P, 512], F32)) for i in range(8)]
        SA, SB = bank[0:4], bank[4:8]
        YB = SB + [SA[2], SA[3], SA[0], SA[1]]

        x = sb("x", [P, KT, T])
        xh = sb("xh", [P, KT, T], F32R)
        xl = sb("xl", [P, KT, T], F32R)
        w_raw = sb("w_raw", [P, SLOTS, 2, CW])
        w_hi = sb("w_hi", [P, SLOTS, 2, CW], F32R)
        w_lo = sb("w_lo", [P, SLOTS, 2, CW], F32R)
        hh = sb("hh", [P, PASS_T, T], F32R)
        hl = sb("hl", [P, PASS_T, T], F32R)
        ident = sb("ident", [P, P])
        ones = sb("ones", [P, P])
        mask = sb("mask", [P, XW])
        par = sb("par", [P, 7 * KT])
        cpar = sb("cpar", [P, 2, 4, FT])
        cp = sb("cp", [P, 4, PASS_T])
        rbc = sb("rbc", [P, T])
        acc = sb("acc", [P, T])

        rt = sb("rt", [P, T])
        eps = sb("eps", [P, 1])
        nT = sb("nT", [P, 2, NB, H])
        nP = sb("nP", [P, 2, H])
        mrow = sb("mrow", [H, T])
        mtrow = sb("mtrow", [H, T])
        mm = sb("mm", [H, T])
        negeye = sb("negeye", [H, H])
        gcol = sb("gcol", [P, 3, 2, H])
        hcol = sb("hcol", [P, 3, 2])
        mb = sb("mb", [P, NB, H])
        mbh = sb("mbh", [P, NB])
        nh = sb("nh", [P, 2, NB])
        gh = sb("gh", [P, 4])
        bg = sb("bg", [36, 1])
        rc = sb("rc", [P, 16])
        stat = sb("stat", [P, 8, 3])
        nt2 = sb("nt2", [P, 2, NB])
        AREA = 15700
        area = sb("area", [P, AREA])

        def view(at, n, parts=P):
            assert at + n <= AREA
            return area[0:parts, at:at + n]

        at = 0
        qk = view(0, 4 * T).rearrange("p (f t) -> p f t", t=T)
        v = view(1344, 4 * T).rearrange("p (f t) -> p f t", t=T)
        hn = view(1344, 3 * DV).rearrange("p (s n) -> p s n", n=DV)
        o = view(2880, 4 * T).rearrange("p (f t) -> p f t", t=T)
        ktok = view(4224, 3 * DK).rearrange("p (s n) -> p s n", n=DK)
        vtok = view(4992, 3 * DV).rearrange("p (s n) -> p s n", n=DV)
        X = view(6528, XW)
        PS0 = view(7024, T)
        PS1 = view(7360, T - 128)
        PS2 = view(7568, TL)
        qm = view(7648, 2 * 704).rearrange("p (k n) -> p k n", k=2)
        qn = view(9056, 2 * TL).rearrange("p (k n) -> p k n", k=2)
        WI = view(9216, NB * NS)
        wkp = view(9280, 3 * DK).rearrange("p (s n) -> p s n", n=DK)
        wkb = view(10048, 2 * DK).rearrange("p (s n) -> p s n", n=DK)
        Cst = view(10560, 2 * DV).rearrange("p (k n) -> p k n", n=DV)
        Cr = view(11584, 4 * 2 * DV).rearrange("p (s k n) -> p s k n", s=4, k=2)
        hf = view(0, 4 * T).rearrange("p (f t) -> p f t", t=T)
        junk = view(0, DV)
        xtok = view(0, 3 * D).rearrange("p (s n) -> p s n", n=D)
        ptok = view(6144, P, 7 * KT)
        ctok = view(6272, 4 * P, 86).rearrange("p (s n) -> p s n", n=P)
        ntok = view(6784, DK, NB * H)
        wgr = view(9280, KT * 8).rearrange("p (k n) -> p k n", n=8)
        wgg = view(9408, KT * 36).rearrange("p (k n) -> p k n", n=36)
        sqr = view(9984, 4 * T).rearrange("p (s n) -> p s n", n=T)
        row = [view(11584 + i * T, T, 36) for i in range(12)]
        E = view(0, 4 * GW).rearrange("p (f t) -> p f t", t=GW)
        Tt = view(1416, 4 * GW).rearrange("p (f t) -> p f t", t=GW)
        Sp = view(2832, 4 * T).rearrange("p (f t) -> p f t", t=T)
        fh = view(4176, 4 * T).rearrange("p (f t) -> p f t", t=T)
        hb = view(5620, 2 * CW, 2 * NB).rearrange("p (s n) -> p s n", n=CW)
        tst = view(6644, 2 * CW, 2 * NB + 2).rearrange("p (s n) -> p s n", n=CW)
        last = view(15204, 2 * 4 * 2 * (NB + 1)).rearrange("p (q f n) -> p q f n", q=2, f=4)
        sqf = view(2880, 4 * T).rearrange("p (f t) -> p f t", t=T)
        pbuf = view(768, D, NB * PADW)
        hrow = view(0, KT * NB * PADW).rearrange("p (f n) -> p f n", f=KT)
        U = view(7668, KT * UW).rearrange("p (f t) -> p f t", t=UW)
        Wa, Wb = (view(at, 2 * UW).rearrange("p (f t) -> p f t", t=UW) for at in (1920, 6644))
        PD = view(4224, 4 * T).rearrange("p (f t) -> p f t", t=T)
        psto = view(7668, D, NB * PADW)
        pstp = view(9716, D, PADW)
        yT = view(4224, 4 * T).rearrange("p (f t) -> p f t", t=T)
        ytok = view(7668, 3 * D).rearrange("p (s n) -> p s n", n=D)
        nsto = view(5620, DK, NB * H)
        npst = view(5876, DK, H)

        def seqs(ap, pad=0):
            return ap.rearrange("p (b s) -> p b s", s=NS + pad)[:, :, pad:]

        raw_landed = [sem(f"raw_landed{s}") for s in range(SLOTS)]
        hi_done, lo_done, chunk_used = sem("hi_done"), sem("lo_done"), sem("chunk_used")
        evac = sem("accumulator_read")
        act_step, dve_step, pool_step = sem("act_step"), sem("dve_step"), sem("pool_step")
        in_par, in_x, in_gate, in_ntok = sem("in_par"), sem("in_x"), sem("in_gate"), sem("in_ntok")
        consts = sem("consts")
        pe_passed, pool_passed = sem("pe_passed"), sem("pool_passed")
        st_tr, st_ev = sem("start_transposed"), sem("start_read")
        st_sq, st_squ = sem("square_ready"), sem("square_used")
        xh_done, xl_done = sem("xh_done"), sem("xl_done")
        ssq_ready, rms_mm, rt_ready, r_ready = sem("ssq_ready"), sem("rms_mm"), sem("rt_ready"), sem("r_ready")
        wgg_ready, gates_mm = sem("wgg_ready"), sem("gates_mm")
        row_abs, row_exp, row_ln, rows_ready = sem("row_abs"), sem("row_exp"), sem("row_ln"), sem("rows_ready")
        gcol_mm, gcol_a, gcol_em = sem("gcol_mm"), sem("gcol_a"), sem("gcol_em")
        mrow_ready, mb_ready, mb_read = sem("mrow_ready"), sem("mb_ready"), sem("mb_read")
        x_exp, pm_ready, qm_ready = sem("x_exp"), sem("pm_ready"), sem("qm_ready")
        s_ready, kt_ready, ps_ready, ktok_ready = sem("s_ready"), sem("kt_ready"), sem("ps_ready"), sem("ktok_ready")
        sig_done, vt_ready, vtok_a, vtok_v = sem("sig_done"), sem("vt_ready"), sem("vtok_a"), sem("vtok_v")
        num_ready, den_ready, den_read = sem("num_ready"), sem("den_ready"), sem("den_read")
        c_landed = [sem(f"c_landed{s}") for s in range(4)]
        c_stored = [sem(f"c_stored{s}") for s in range(4)]
        wkp_ready, wkb_ready = sem("wkp_ready"), sem("wkb_ready")
        e_zero, cnew_ready, c_updated = sem("e_zero"), sem("cnew_ready"), sem("c_updated")
        cp_ready, cst_ready, cst_stored = sem("cp_ready"), sem("cst_ready"), sem("cst_stored")
        n_ready, n_read, nst_step = sem("n_ready"), sem("n_read"), sem("n_new")
        ss_done, z_ready, z_sqrt, hn_ready = sem("ss_done"), sem("z_ready"), sem("z_sqrt"), sem("hn_ready")
        ht_ready, hf_ready, hh_ready, hl_ready = sem("ht_ready"), sem("hf_ready"), sem("hh_ready"), sem("hl_ready")
        hb_landed = [sem(f"hb_landed{s}") for s in range(2)]
        hist_mm, hist_read, tail_mm, tail_read = sem("hist_mm"), sem("hist_read"), sem("tail_mm"), sem("tail_read")
        tail_stored = [sem(f"tail_stored{s}") for s in range(2)]
        tap0_ready, taps_ready, silu_ready = sem("tap0_ready"), sem("taps_ready"), sem("silu_ready")
        gx_ready, u_pads = sem("gx_ready"), sem("u_pads")
        in_pool, ph_mm, ph_read, pd_ready = sem("in_pool"), sem("ph_mm"), sem("ph_read"), sem("pd_ready")
        last_ready, hrow_ready = sem("last_ready"), sem("hrow_ready")
        pt_mm, pt_read = sem("pt_mm"), sem("pt_read")
        y_ready, y_mm, y_read, no_mm, no_read = sem("y_ready"), sem("y_mm"), sem("y_read"), sem("no_mm"), sem("no_read")
        stored, pool_stored = sem("stored"), sem("pool_stored")

        block = ctx.enter_context(nc.Block())

        w_in = I["w_mlstm_in"][0].rearrange("(k p) n -> p k n", p=P)
        w_out = I["w_mlstm_out"][0].rearrange("(k p) n -> p k n", p=P)
        w_pool = [I["w_pool"][0, g].rearrange("(k p) n -> p k n", p=P) for g in range(4)]
        w_up = [I["w_up"][i].rearrange("(k p) n -> p k n", p=P) for i in range(2)]
        w_down = [I["w_down"][i].rearrange("(k p) n -> p k n", p=P) for i in range(2)]

        @block.sync
        def _(sp):
            def chunk(c, k, parts):
                s = k % SLOTS
                if not (isinstance(c, int) and c + k < SLOTS):
                    sp.wait_ge(lo_done, c + (k - SLOTS + 1))
                for to, src in parts:
                    sp.dma_start(to(w_raw[:, s]), src).then_inc(raw_landed[s], 16)

            def by_row(w, k0, c0, n=CW):
                return [(lambda r, j=j: r[:, j, 0:n], w[:, bass.ds(k0 + j, 1), bass.ds(c0, n)].rearrange("p a n -> p (a n)"))
                        for j in range(2)]

            def one_row(w, k0, c0):
                return [(lambda r, j=j: r[:, 0, j * 256:j * 256 + 256],
                         w[:, bass.ds(k0, 1), bass.ds(c0 + j * 256, 256)].rearrange("p a n -> p (a n)"))
                        for j in range(2)]

            sp.dma_start(xtok[0:META, 0, :], I["meta_tokens"]).then_inc(in_x, 16)
            sp.dma_start(xtok[META:P, 0, :], I["x_prompt"][0, 0:P - META]).then_inc(in_x, 16)
            sp.dma_start(xtok[:, 1, :], I["x_prompt"][0, P - META:2 * P - META]).then_inc(in_x, 16)
            sp.dma_start(xtok[0:META, 2, :], I["x_prompt"][0, 2 * P - META:SEQ]).then_inc(in_x, 16)
            sp.dma_start(xtok[META:TL, 2, :], I["x_sample"].rearrange("b s d -> (b s) d")).then_inc(in_x, 16)
            vecs = [I["norm_mix"][0], I["norm_mix"][1], I["norm_ffn"][0], I["norm_ffn"][1], I["norm_final"],
                    I["g_mlstm_out"][0], I["pool_scale"][0]]
            for i, a in enumerate(vecs):
                sp.dma_start(ptok[i * KT:(i + 1) * KT, :], a.rearrange("(k p) -> k p", p=P)).then_inc(in_par, 16)
            for i in range(2):
                for j in range(3):
                    sp.dma_start(ctok[(j % 2) * FT:(j % 2) * FT + FT, 2 * i + j // 2, :],
                                 I["conv_w"][i, j].rearrange("(k p) -> k p", p=P)).then_inc(in_par, 16)
                sp.dma_start(ctok[FT:2 * FT, 2 * i + 1, :],
                             I["conv_b"][i].rearrange("(k p) -> k p", p=P)).then_inc(in_par, 16)
            sp.dma_start(ntok, I["state_mlstm_n"][0].rearrange("b h k -> (b h) k")).then_inc(in_par, 16)
            sp.dma_start(wgr, w_in[:, :, 2 * QK_W + 2 * V_W:]).then_inc(in_gate, 16)
            with nc.allow_non_contiguous_dma(reason="40 gate biases and stabilisers"):
                sp.dma_start(bg[0:H, :], I["b_mlstm_gate"][0, 0:H].rearrange("(h a) -> h a", a=1)).then_inc(in_gate, 16)
                sp.dma_start(bg[32:32 + H, :], I["b_mlstm_gate"][0, H:2 * H].rearrange("(h a) -> h a", a=1)).then_inc(in_gate, 16)
                sp.dma_start(row[11][0:H, 0:NB], I["state_mlstm_m"][0].rearrange("b h -> h b")).then_inc(in_gate, 16)
            sp.dma_start(mb[:, :, :].rearrange("p b h -> p (b h)"),
                         I["state_mlstm_m"].rearrange("a b h -> a (b h)").to_broadcast([P, NB * H])).then_inc(in_gate, 16)

            def c_load(h, b):
                if not (isinstance(h, int) and h == 0 and b < 4):
                    sp.wait_ge(c_stored[b % 4], 32 * h + 16 * (b // 4))
                src = I["state_mlstm_C"][0, b].rearrange("h (k p) v -> p (h k) v", p=P)
                sp.dma_start(Cr[:, b % 4], src[:, bass.ds(2 * h, 2), :]).then_inc(c_landed[b % 4], 16)

            def head(h, c):
                for k in range(KT // 2):
                    chunk(c, k, [(lambda r, j=j: r[:, :, j * DK:(j + 1) * DK],
                                  w_in[:, 2 * k:2 * k + 2, bass.ds(j * QK_W + h * DK, DK)]) for j in range(2)])
                for blk in range(2):
                    if blk == 1:
                        if isinstance(h, int) and h == 0:
                            sp.wait_ge(gcol_mm, 1)
                        for b in range(4):
                            c_load(h, b)
                    for k in range(KT // 2):
                        chunk(c, 8 + 8 * blk + k, by_row(w_in, 2 * k, 2 * QK_W + blk * V_W + h * DV))
                for n in range(4):
                    for k in range(2):
                        chunk(c, 24 + 2 * n + k, by_row(w_out, h * 4 + 2 * k, n * CW))
                dst = O["C_sample"][0]
                for b in range(NB):
                    sp.wait_ge(c_updated, NB * h + b + 1)
                    sp.dma_start(dst[b].rearrange("h (k p) v -> p (h k) v", p=P)[:, bass.ds(2 * h, 2), :],
                                 Cr[:, b % 4]).then_inc(c_stored[b % 4], 16)
                    if 1 <= b <= 4:
                        c_load(h, b - 1 + 4)

            def ffn(i, c, j, nq, nt):
                def histories():
                    for q in range(nq):
                        if not isinstance(j, int) or j:
                            sp.wait_ge(hist_mm, i * HB + 2 * j + q - 1)
                        elif i == 0:
                            sp.wait_ge(hl_ready, 4 * H)
                        else:
                            sp.wait_ge(hist_mm, HB)
                        sp.dma_start(hb[:, q, 0:nt * P],
                                     I["state_ffn_conv"][i].rearrange("b r f -> (b r) f")[:, bass.ds((j * 8 + 4 * q) * P, nt * P)]
                                     ).then_inc(hb_landed[q], 16)

                k0 = 0
                for q in range(nq):
                    for a in range(2):
                        for k in range(KT // 2):
                            if (q, a, k) == (0, 0, SLOTS):
                                histories()
                            chunk(c, k0 + k, by_row(w_up[i], 2 * k, a * F + (j * 8 + 4 * q) * P, nt * P))
                        k0 += KT // 2
                kd = nq * nt
                for n in range(4):
                    if n == 2 and i == 0 and nt < 4:
                        sp.wait_ge(hl_ready, 4 * H + FT)
                        sp.dma_start(pbuf, I["state_pool"][0].rearrange("b r d -> (b r) d")).then_inc(in_pool, 16)
                    for k in range(0, kd, 2):
                        f = by_row if k + 1 < kd else one_row
                        chunk(c, k0, f(w_down[i], j * 8 + k, n * CW))
                        k0 += 1

            head(0, 0)
            with sp.Fori(1, H) as h:
                head(h, h * C_HEAD)
            for i, c in ((0, C_FFN0), (1, C_FFN1)):
                ffn(i, c, 0, 2, 4)
                with sp.Fori(1, N_PASS) as j:
                    ffn(i, c + j * C_PASS, j, 2, 4)
                ffn(i, c + N_PASS * C_PASS, N_PASS, 1, TAIL_T)
                if i == 0:
                    for g in range(4):
                        for k in range(2):
                            chunk(C_POOL, 2 * g + k, by_row(w_pool[g], 2 * k, 0))
            with nc.allow_non_contiguous_dma(reason="36 stabilisers"):
                last = mtrow[:, NP - 1:T:NS]
                sp.dma_start(O["m_prompt"][0].rearrange("b h -> h b"), last[:, 0:1]).then_inc(stored, 16)
                sp.dma_start(O["m_sample"][0].rearrange("b h -> h b"), last[:, 1:]).then_inc(stored, 16)
            sp.wait_ge(no_read, 2)
            sp.dma_start(O["n_sample"][0].rearrange("b h k -> (b h) k"), nsto).then_inc(stored, 16)
            sp.dma_start(O["n_prompt"][0, 0], npst).then_inc(stored, 16)
            for q in range(4):
                for s in range(3):
                    n = NB * NS if s == 2 else P
                    sp.wait_ge(y_read, 3 * q + s + 1)
                    to = O["y_sample"].rearrange("b s d -> (b s) d") if s == 2 else O["y_prompt"][0, s * P:(s + 1) * P]
                    sp.dma_start(to[:, q * 512:(q + 1) * 512], ytok[0:n, s, q * 512:(q + 1) * 512]).then_inc(stored, 16)
            sp.wait_ge(stored, 16 * (2 + 2 + 12))
            for s in range(4):
                sp.wait_ge(c_stored[s], 2 * H * 16)
            sp.wait_ge(cst_stored, 16 * H)
            sp.wait_ge(tail_stored[0], 2 * 32 * (N_PASS + 1))
            sp.wait_ge(tail_stored[1], 2 * 32 * N_PASS)

        @block.tensor
        def _(pe):
            def split_products(out, kt, s, j, m, xhk, xlk, first, last):
                wh, wl = w_hi[:, s, j, m:m + P], w_lo[:, s, j, m:m + P]
                pe.matmul(out, wh, xhk, start=first, stop=False)
                pe.matmul(out, wh, xlk, start=False, stop=False)
                return pe.matmul(out, wl, xhk, start=False, stop=last)

            def gemm(banks, c, k0, nkt, nt, xhi, xlo, c0, free=None, guard=None, fresh=None, amid=None):
                for i in range((nkt + 1) // 2):
                    if amid and i in amid:
                        amid[i]()
                    s = (k0 + i) % SLOTS
                    pe.wait_ge(lo_done, c + (k0 + i + 1))
                    if fresh:
                        fresh(2 * i)
                    for t in range(nt):
                        if i == 0 and free:
                            free(t)
                        if i == 0 and guard and t in guard:
                            pe.wait_ge(*guard[t])
                        for j in range(min(2, nkt - 2 * i)):
                            kt = 2 * i + j
                            mm_ = split_products(banks[t][:, c0:T], kt, s, j, t * P, xhi[:, kt, c0:T], xlo[:, kt, c0:T],
                                                 kt == 0, kt == nkt - 1)
                    mm_.then_inc(chunk_used, 1)

            def after(e):
                return lambda t: pe.wait_ge(evac, e + (t + 1))

            pe.wait_ge(consts, 1)
            pe.wait_ge(in_par, 16 * 16)
            pe.transpose(bank[0][:, 0:7 * KT], ptok, ident[0:7 * KT, 0:7 * KT]).then_inc(st_tr, 1)
            for i in range(2):
                for s in range(2):
                    m_ = pe.transpose(bank[1 + i][:, s * 2 * FT:(s + 1) * 2 * FT], ctok[:, 2 * i + s, :],
                                      ident[0:2 * FT, 0:2 * FT])
                m_.then_inc(st_tr, 1)
            for k in range(2):
                m_ = pe.transpose(bank[3][:, k * 32:(k + 1) * 32], ntok[:, k * P:(k + 1) * P], ident[0:32, 0:32])
            m_.then_inc(st_tr, 1)
            pe.wait_ge(in_x, 16 * 5)
            for kt in range(KT):
                i = 4 + kt
                if i >= 8:
                    pe.wait_ge(st_ev, i - 7)
                for s, (t0, n) in enumerate(TOK):
                    m_ = pe.transpose(bank[i % 8][:, t0:t0 + n], xtok[0:n, s, kt * P:(kt + 1) * P], ident[0:n, 0:n])
                m_.then_inc(st_tr, 1)
            pe.wait_ge(st_ev, 4 + KT)
            pe.wait_ge(wgg_ready, 1)
            for kt in range(KT):
                m_ = pe.matmul(SB[0][0:36, 0:T], wgg[:, kt, :], x[:, kt, :], start=(kt == 0), stop=(kt == KT - 1))
            m_.then_inc(gates_mm, 1)
            for kt in range(KT):
                pe.wait_ge(st_sq, kt + 1)
                m_ = pe.matmul(SB[1][:, 0:T], ones[:, :], sqr[:, kt % 4, :], start=(kt == 0), stop=(kt == KT - 1))
                m_.then_inc(st_squ, 1)

            def sum_squares(out, k):
                pe.wait_ge(ssq_ready, k)
                pe.matmul(out, ones[:, :], acc[:, :], start=True, stop=True).then_inc(rms_mm, 1)

            def head(h, c, e):
                first = isinstance(h, int)
                pe.wait_ge(xl_done, KT)
                gemm(SA, c, 0, KT, 4, xh, xl, 0, free=None if first else after(e - 8))
                if first:
                    pe.wait_ge(rows_ready, 1)
                    for s, (t0, n) in enumerate(TOK):
                        pe.transpose(SB[2][0:n, s * 8:s * 8 + 4], row[8][0:H, t0:t0 + n], ident[0:H, 0:H])
                        m_ = pe.transpose(SB[2][0:n, s * 8 + 4:s * 8 + 8], mtrow[:, t0:t0 + n], ident[0:H, 0:H])
                    m_.then_inc(gcol_mm, 1)
                pe.wait_ge(mrow_ready, h + 1)
                if not first:
                    pe.wait_ge(evac, e)
                pe.matmul(SB[3][:, 0:T], ones[0:H, :], mm[:, :], start=True, stop=True).then_inc(mb_ready, 1)
                guard = {3: (mb_read, h + 1)}
                if first:
                    guard[0] = (rows_ready, 1)
                    guard[1] = (r_ready, 1)
                    guard[2] = (gcol_em, 1)

                def scores():
                    pe.wait_ge(evac, e + 4)
                    for s, (x0, t0, t1, n) in enumerate(((X0, 0, NP, P), (X1, P, NP, P), (X2, 2 * P, T, TL))):
                        for k in range(2):
                            m_ = pe.matmul(SA[0][0:n, x0:x0 + t1 - t0], qk[:, 2 + k, s * P:s * P + n], qk[:, k, t0:t1],
                                           start=(k == 0), stop=(k == 1))
                    m_.then_inc(s_ready, 1)
                    for k in range(2):
                        for s, (t0, n) in enumerate(TOK):
                            m_ = pe.transpose(SA[1 + k][0:n, s * P:(s + 1) * P], qk[:, 2 + k, t0:t0 + n], ident[:, :])
                    m_.then_inc(kt_ready, 1)

                def values():
                    pe.wait_ge(evac, e + 8)
                    pe.wait_ge(ps_ready, h + 1)
                    pe.wait_ge(ktok_ready, h + 1)
                    for f in range(4):
                        for s, (t0, n) in enumerate(TOK):
                            m_ = pe.transpose(SA[f][0:n, s * P:(s + 1) * P], v[:, f, t0:t0 + n], ident[:, :])
                        m_.then_inc(vt_ready, 1)

                gemm(SB, c, 8, KT, 4, xh, xl, 0, free=None if first else after(e - 4), guard=guard, amid={2: scores})
                gemm(SB, c, 16, KT, 4, xh, xl, 0, free=after(e + 4), amid={3: values})
                pe.wait_ge(vtok_v, h + 1)
                pe.wait_ge(vtok_a, h + 1)
                pe.wait_ge(qm_ready, h + 1)
                one = ones[:, 0:1]
                pe.matmul(SA[3][:, 0:1], PS0[:, 0:P], one, start=True, stop=True)
                pe.matmul(SA[3][:, 1:2], PS0[:, P:2 * P], one, start=True, stop=False)
                pe.matmul(SA[3][:, 1:2], PS1[:, 0:P], one, start=False, stop=True)
                pe.matmul(SA[3][0:TL, 2:3], PS0[:, 2 * P:T], one, start=True, stop=False)
                pe.matmul(SA[3][0:TL, 2:3], PS1[:, P:T - P], one, start=False, stop=False)
                pe.matmul(SA[3][0:TL, 2:3], qn[:, 0, :], one, start=False, stop=False)
                pe.matmul(SA[3][0:TL, 2:3], qn[:, 1, :], one, start=False, stop=False)
                pe.matmul(SA[3][0:TL, 2:3], PS2[0:TL, :], ones[0:TL, 0:1], start=False, stop=True).then_inc(den_ready, 1)
                pe.matmul(SA[0][:, :], PS0[:, 0:P], vtok[:, 0, :], start=True, stop=True).then_inc(num_ready, 1)
                pe.matmul(SA[1][:, :], PS0[:, P:2 * P], vtok[:, 0, :], start=True, stop=False)
                pe.matmul(SA[1][:, :], PS1[:, 0:P], vtok[:, 1, :], start=False, stop=True).then_inc(num_ready, 1)
                num2 = SA[2][0:TL, :]
                pe.matmul(num2, PS0[:, 2 * P:T], vtok[:, 0, :], start=True, stop=False)
                pe.matmul(num2, PS1[:, P:T - P], vtok[:, 1, :], start=False, stop=False)
                pe.matmul(num2, PS2[0:TL, :], vtok[0:TL, 2, :], start=False, stop=False)
                for b in range(NB):
                    pe.wait_ge(c_landed[b % 4], 32 * h + 16 * (b // 4 + 1))
                    for k in range(2):
                        m_ = pe.matmul(num2, qm[:, k, b * TL:(b + 1) * TL], Cr[:, b % 4, k, :], start=False,
                                       stop=(b == NB - 1 and k == 1))
                    if b == NB - 1:
                        m_.then_inc(num_ready, 1)
                    pe.wait_ge(wkb_ready, NB * h + b + 1)
                    if b < 2:
                        pe.wait_ge(evac, e + 12)
                    else:
                        pe.wait_ge(c_updated, NB * h + b - 1)
                    for k in range(2):
                        m_ = pe.matmul(SB[2 * (b % 2) + k][:, :], wkb[0:TL, b % 2, k * P:(k + 1) * P], vtok[0:TL, 2, :],
                                       start=True, stop=True)
                    m_.then_inc(cnew_ready, 1)
                pe.wait_ge(wkp_ready, h + 1)
                pe.wait_ge(c_updated, NB * h + NB - 1)
                for k in range(2):
                    for s, (t0, n) in enumerate(TOK):
                        m_ = pe.matmul(SB[k][:, :], wkp[0:n, s, k * P:(k + 1) * P], vtok[0:n, s, :],
                                       start=(s == 0), stop=(s == 2))
                m_.then_inc(cp_ready, 1)
                pe.wait_ge(den_read, h + 1)
                for k in range(2):
                    out = SA[3][:, 16 * k:16 * k + 1 + NB]
                    pe.matmul(out, ktok[0:TL, 2, k * P:(k + 1) * P], X[0:TL, X2 + META - 1:XW:NS], start=True, stop=False)
                    pe.matmul(out[:, 0:1], ktok[:, 0, k * P:(k + 1) * P], X[:, X1 - 1:X1], start=False, stop=False)
                    m_ = pe.matmul(out[:, 0:1], ktok[:, 1, k * P:(k + 1) * P], X[:, X2 - 1:X2], start=False, stop=True)
                m_.then_inc(n_ready, 1)
                pe.wait_ge(c_updated, NB * h + NB)
                pe.wait_ge(cst_ready, h + 1)
                for s, (t0, n) in enumerate(TOK):
                    pe.wait_ge(hn_ready, 3 * h + s + 1)
                    for f in range(4):
                        m_ = pe.transpose(SB[f][:, t0:t0 + n], hn[0:n, s, f * P:(f + 1) * P], ident[0:n, 0:n])
                m_.then_inc(ht_ready, 1)
                pe.wait_ge(n_read, h + 1)
                for n in range(4):
                    gemm((SA, SB)[n % 2], c, 24 + 2 * n, 4, 4, hh, hl, 0,
                         free=after(e + 4 + 4 * n) if n >= 2 else None,
                         fresh=(lambda kt: pe.wait_ge(hl_ready, 4 * h + (kt + 2))) if n == 0 else None)

            def ffn(i, c, e, j, nq, nt, amid_last=None):
                first = isinstance(j, int) and j == 0
                fresh = (lambda kt: pe.wait_ge(xl_done, (1 + 2 * i) * KT + kt + 2)) if first else None
                n_q = nq * nt
                eb = 0
                k0 = 0
                for q in range(nq):
                    hj = i * HB + 2 * j + q

                    def history():
                        pe.wait_ge(evac, e + eb)
                        if first and q == 0 and i == 1:
                            pe.wait_ge(pt_read, 8)
                        wait_apart(pe, pe_passed, hb_landed[q], 16 * (j + 1 + (i * (N_PASS + 1 - q))))
                        for t in range(nt):
                            m_ = pe.transpose(SB[2][:, t * 2 * NB:(t + 1) * 2 * NB], hb[:, q, t * P:(t + 1) * P],
                                              ident[0:2 * NB, 0:2 * NB])
                        m_.then_inc(hist_mm, 1)

                    amid = {4: history}
                    if first and q == 0 and i == 1:
                        amid = {1: lambda: pool_tails(0), 4: lambda: pool_tails(1), 6: history}
                    gemm(SA, c, k0, KT, nt, xh, xl, G0[i], free=after(e + (eb - 8)), fresh=fresh if q == 0 else None,
                         guard={2: (tail_read, hj)} if q == 1 else None, amid=amid)
                    k0 += KT // 2
                    if first and q == 0:
                        pe.wait_ge(evac, e)
                        sum_squares(SB[3][:, 0:T], (1, 3)[i])
                    guard = {2: (hist_read, hj + 1)}
                    if first and q == 0:
                        guard[3] = (rt_ready, (2, 4)[i])
                    gemm(SB, c, k0, KT, nt, xh, xl, A0[i], free=after(e + (eb - 4)), guard=guard,
                         amid={4: lambda: tails(q, nt, hj + 1)})
                    k0 += KT // 2
                    eb += 2 * nt
                hj = i * HB + 2 * j + nq
                for n in range(4):
                    if n == 0:
                        free = lambda t: pe.wait_ge(evac, e + (eb - nt))
                    elif n == 1:
                        free = lambda t: pe.wait_ge(evac, e + eb)
                    else:
                        free = after(e + (eb + 4 * n - 8))
                    gemm((SA, SB)[n % 2], c, k0, n_q, 4, hh, hl, A0[i], free=free, guard={2: (tail_read, hj)} if n == 0 else None,
                         fresh=(lambda kt: pe.wait_ge(hl_ready, 4 * H + i * FT + 8 * j + min(kt + 2, n_q))) if n == 0 else None,
                         amid={1: amid_last} if n == 3 and amid_last else None)
                    k0 += (n_q + 1) // 2

            def tails(q, nt, n):
                pe.wait_ge(last_ready, n)
                for t in range(nt):
                    m_ = pe.transpose(SA[2][0:2 * NB + 2, t * P:(t + 1) * P], last[:, q, t], ident[:, :])
                m_.then_inc(tail_mm, 1)

            def pool_history():
                pe.wait_ge(evac, E_POOL - 4)
                pe.wait_ge(in_pool, 16)
                for kt in range(KT):
                    m_ = pe.transpose(SA[kt // 4][:, (kt % 4) * 120:(kt % 4) * 120 + 120], pbuf[:, kt * P:(kt + 1) * P],
                                      ident[0:120, 0:120])
                m_.then_inc(ph_mm, 1)

            def pooling():
                pe.wait_ge(evac, E_POOL)
                sum_squares(SB[3][:, 0:T], 2)
                for g in range(4):
                    guard = [{t: (ph_read, 4) for t in range(4)}, {3: (rt_ready, 3)}, None, None][g]
                    gemm((SA, SB)[g % 2], C_POOL, 2 * g, 4, 4, xh[:, 4 * g:4 * g + 4], xl[:, 4 * g:4 * g + 4], 0,
                         free=after(E_POOL + 4 * g - 8) if g >= 2 else None, guard=guard,
                         fresh=lambda kt: pe.wait_ge(xl_done, 2 * KT + 4 * g + kt + 2))

            def pool_tails(samples):
                if samples:
                    pe.wait_ge(pt_read, 4)
                    pe.wait_ge(hrow_ready, KT)
                else:
                    pe.wait_ge(evac, E_POOL + 16)
                for kt in range(KT):
                    n, rows = (NB * PADW, hrow[:, kt]) if samples else (PADW, U[:, kt, NP:NP + PADW])
                    m_ = pe.transpose(SB[kt // 4][0:n, (kt % 4) * P:(kt % 4 + 1) * P], rows, ident[:, :])
                m_.then_inc(pt_mm, 1)

            def normalisers():
                pe.wait_ge(evac, E_END - 4)
                for k in range(2):
                    m_ = pe.transpose(SA[0][0:NB * H, k * P:(k + 1) * P], nT[:, k].rearrange("p b h -> p (b h)"), ident[:, :])
                m_.then_inc(no_mm, 1)
                for k in range(2):
                    m_ = pe.transpose(SA[1][0:H, k * P:(k + 1) * P], nP[:, k], ident[:, :])
                m_.then_inc(no_mm, 1)

            head(0, 0, 0)
            with pe.Fori(1, H) as h:
                head(h, h * C_HEAD, h * E_HEAD)
            for i, c, e in ((0, C_FFN0, E_FFN0), (1, C_FFN1, E_FFN1)):
                ffn(i, c, e, 0, 2, 4)
                with pe.Fori(1, N_PASS) as j:
                    ffn(i, c + j * C_PASS, e + j * E_PASS, j, 2, 4)
                ffn(i, c + N_PASS * C_PASS, e + N_PASS * E_PASS, N_PASS, 1, TAIL_T, (pool_history, normalisers)[i])
                if i == 0:
                    pooling()
            pe.wait_ge(evac, E_END)
            sum_squares(SA[3][:, 0:T], 4)
            for kt in range(KT):
                pe.wait_ge(y_ready, kt + 1)
                for s in range(3):
                    i = 3 * (kt // 4) + s
                    if kt % 4 == 0:
                        if i >= 8:
                            pe.wait_ge(y_read, i - 7)
                        elif i >= 6:
                            pe.wait_ge(no_read, i - 5)
                    n = NB * NS if s == 2 else P
                    m_ = pe.transpose(YB[i % 8][0:n, (kt % 4) * P:(kt % 4 + 1) * P], yT[:, kt % 4, META + s * P:META + s * P + n],
                                      ident[:, :])
                m_.then_inc(y_mm, 1)

        @block.scalar
        def _(act):
            def hi(c, k):
                s = k % SLOTS
                if isinstance(c, int) and c + k >= C_END:
                    return
                act.wait_ge(raw_landed[s], c * 8 + 32 * (k // SLOTS + 1))
                if not (isinstance(c, int) and c + k < SLOTS):
                    act.wait_ge(chunk_used, c + (k - SLOTS + 1))
                nc.scalar.activation(w_hi[:, s], w_raw[:, s], ACT.Copy).then_inc(hi_done, 1)

            def his(c, k0, k1):
                for k in range(k0, k1):
                    hi(c, k)

            def hand_over(stage, n):
                e = (0, E_FFN0, E_POOL, E_FFN1, E_END)[stage] - 16
                for kt in range(4 * n, 4 * n + 4):
                    act.wait_ge(evac, e + kt + 1)
                    if stage in (1, 3):
                        gain, c0 = (2, G0[0]) if stage == 1 else (3, G0[1])
                        nc.scalar.activation(xh[:, kt, c0:], x[:, kt, c0:], ACT.Copy,
                                             scale=par[:, gain * KT + kt:gain * KT + kt + 1]).then_inc(xh_done, 1)
                    act.wait_ge(st_squ, stage * KT + kt - 3)
                    nc.scalar.activation(sqf[:, kt % 4], x[:, kt], ACT.Square).then_inc(st_sq, 1)
                    if stage == 2:
                        gain = par[:, KT + kt:KT + kt + 1]
                        nc.scalar.activation(U[:, kt, PADW:PADW + NP], x[:, kt, 0:NP], ACT.Copy, scale=gain)
                        nc.scalar.activation(seqs(U[:, kt, PADW + NP:], PADW), seqs(x[:, kt, NP:]), ACT.Copy,
                                             scale=gain).then_inc(gx_ready, 1)

            def rms(ps, k):
                act.wait_ge(rms_mm, k)
                nc.scalar.activation(rt[:, :], ps[:, 0:T], ACT.Sqrt, bias=eps[:, :], scale=1.0 / D).then_inc(rt_ready, 1)

            his(0, 0, SLOTS)
            for kt in range(KT):
                act.wait_ge(st_ev, 5 + kt)
                nc.scalar.activation(xh[:, kt], x[:, kt], ACT.Copy, scale=par[:, kt:kt + 1]).then_inc(xh_done, 1)
                if kt >= 4:
                    act.wait_ge(st_squ, kt - 3)
                nc.scalar.activation(sqr[:, kt % 4], x[:, kt], ACT.Square).then_inc(st_sq, 1)
            act.wait_ge(st_squ, KT)
            nc.scalar.activation(rt[:, :], SB[1][:, 0:T], ACT.Sqrt, bias=eps[:, :], scale=1.0 / D).then_inc(rt_ready, 1)
            act.wait_ge(row_abs, 1)
            nc.scalar.activation(row[5][0:H], row[4][0:H], ACT.Exp).then_inc(row_exp, 1)
            act.wait_ge(row_exp, 1)
            nc.scalar.activation(row[6][0:H], row[5][0:H], ACT.Ln, bias=ones[0:H, 0:1]).then_inc(row_ln, 1)

            def head(h, c, e):
                first = isinstance(h, int) and h == 0
                his(c, 4, 12)
                if first:
                    act.wait_ge(gcol_a, 1)
                    nc.scalar.activation(gcol[:, :, 1], gcol[:, :, 1], ACT.Exp, scale=-1.0).then_inc(gcol_em, 1)
                act.wait_ge(mb_read, h + 1)
                nc.scalar.activation(X, X, ACT.Exp)
                nc.scalar.activation(WI, WI, ACT.Exp).then_inc(x_exp, 1)
                his(c, 12, 14)
                act.wait_ge(kt_ready, h + 1)
                for k in range(2):
                    nc.scalar.activation(ktok[:, 0:2, k * P:(k + 1) * P],
                                         SA[1 + k][:, 0:2 * P].rearrange("p (s n) -> p s n", n=P), ACT.Copy)
                    m_ = nc.scalar.activation(ktok[0:TL, 2, k * P:(k + 1) * P], SA[1 + k][0:TL, 2 * P:3 * P], ACT.Copy)
                m_.then_inc(ktok_ready, 1)
                his(c, 14, 22)
                for f in range(2):
                    act.wait_ge(vt_ready, 4 * h + f + 1)
                    nc.scalar.activation(vtok[:, 0:2, f * P:(f + 1) * P],
                                         SA[f][:, 0:2 * P].rearrange("p (s n) -> p s n", n=P), ACT.Copy)
                    m_ = nc.scalar.activation(vtok[0:TL, 2, f * P:(f + 1) * P], SA[f][0:TL, 2 * P:3 * P], ACT.Copy)
                m_.then_inc(vtok_a, 1)
                his(c, 22, 28)
                act.wait_ge(evac, e + 12)
                nc.scalar.activation(o, o, ACT.Sigmoid).then_inc(sig_done, 1)
                for s, (t0, n) in enumerate(TOK):
                    act.wait_ge(num_ready, 3 * h + s + 1)
                    nc.scalar.activation(junk[0:n], SA[s][0:n, :], ACT.Square,
                                         accum_out=stat[0:n, 3, s:s + 1]).then_inc(ss_done, 1)
                    act.wait_ge(ss_done, 3 * h + s + 1)
                act.wait_ge(z_ready, h + 1)
                nc.scalar.activation(stat[:, 5], stat[:, 4], ACT.Sqrt, bias=eps[:, :], scale=1.0 / DV).then_inc(z_sqrt, 1)
                act.wait_ge(cp_ready, h + 1)
                if not first:
                    act.wait_ge(cst_stored, 16 * h)
                nc.scalar.activation(Cst[:, 0], SB[0][:, :], ACT.Copy)
                nc.scalar.activation(Cst[:, 1], SB[1][:, :], ACT.Copy).then_inc(cst_ready, 1)
                act.wait_ge(cst_ready, h + 1)
                act.dma_start(O["C_prompt"][0, 0].rearrange("h (k p) v -> p (h k) v", p=P)[:, bass.ds(2 * h, 2), :],
                              Cst).then_inc(cst_stored, 16)
                for f in range(4):
                    act.wait_ge(hf_ready, 4 * h + f + 1)
                    nc.scalar.activation(hh[:, f], hf[:, f], ACT.Copy).then_inc(hh_ready, 1)
                for n in range(4):
                    his(c, 28 + 2 * n, 30 + 2 * n)
                    if isinstance(h, int) and h == H - 1:
                        hand_over(1, n)

            def ffn(i, c, e, j, nq, nt):
                first = isinstance(j, int) and j == 0
                a0 = A0[i]
                eb = k0 = 0
                for q in range(nq):
                    hj = i * HB + 2 * j + q
                    pooled = i == 1 and first and q == 0
                    if pooled:
                        his(c, 4, 5)
                        act.wait_ge(pt_mm, 1)
                        act.wait_ge(hrow_ready, KT)
                        for n in range(4):
                            nc.scalar.activation(pstp[:, n * 512:(n + 1) * 512], SB[n][0:PADW, :], ACT.Copy).then_inc(pt_read, 1)
                        his(c, 5, 8)
                        act.wait_ge(pt_mm, 2)
                        for n in range(4):
                            nc.scalar.activation(psto[:, n * 512:(n + 1) * 512], SB[n][0:NB * PADW, :],
                                                 ACT.Copy).then_inc(pt_read, 1)
                        act.wait_ge(pt_read, 8)
                        act.dma_start(O["pool_prompt"][0, 0], pstp).then_inc(pool_stored, 16)
                        act.dma_start(O["pool_sample"][0].rearrange("b r d -> (b r) d"), psto).then_inc(pool_stored, 16)
                        his(c, 8, 10)
                    else:
                        his(c, k0 + 4, k0 + 8)
                    act.wait_ge(hist_mm, hj + 1)
                    if not (i == 0 and first and q == 0):
                        act.wait_ge(last_ready, hj)
                        act.wait_ge(taps_ready, i * FT + 8 * j + 4 * q)
                    else:
                        act.wait_ge(e_zero, 1)
                    nc.scalar.activation(E[:, 0:nt, 2 + NP:].rearrange("p f (b s) -> p f b s", s=NS + 2)[:, :, :, 0:2],
                                         SB[2][:, 0:nt * 2 * NB].rearrange("p (f b s) -> p f b s", b=NB, s=2),
                                         ACT.Copy).then_inc(hist_read, 1)
                    his(c, k0 + (10 if pooled else 8), k0 + 12)
                    if first and q == 0:
                        rms(SB[3], (1, 3)[i])
                    for t in range(nt):
                        act.wait_ge(evac, e + (eb + t + 1))
                        nc.scalar.activation(Tt[:, t, a0:GW - 2], E[:, t, a0 + 2:GW], ACT.Identity,
                                             bias=cp[:, 3, 4 * q + t:4 * q + t + 1],
                                             scale=cp[:, 2, 4 * q + t:4 * q + t + 1]).then_inc(tap0_ready, 1)
                    for t in range(nt):
                        act.wait_ge(taps_ready, i * FT + 8 * j + (4 * q + t + 1))
                        nc.scalar.activation(Tt[:, t, a0:GW - 2], Tt[:, t, a0:GW - 2], ACT.Silu).then_inc(silu_ready, 1)
                    his(c, k0 + 12, k0 + 16)
                    tails(i, j, q, nt, hj + 1)
                    his(c, k0 + 16, k0 + 20)
                    for t in range(nt):
                        act.wait_ge(evac, e + (eb + nt + t + 1))
                        nc.scalar.activation(hh[:, 4 * q + t, a0:], fh[:, t, a0:], ACT.Copy).then_inc(hh_ready, 1)
                    k0 += KT
                    eb += 2 * nt
                nd = (nq * nt + 1) // 2
                if nt < 4:
                    if i == 0:
                        act.wait_ge(u_pads, 1)
                    for n in range(4):
                        his(c, k0 + 4 + n * nd, k0 + 4 + (n + 1) * nd)
                        hand_over((2, 4)[i], n)
                else:
                    his(c, k0 + 4, k0 + 4 + 4 * nd)

            def tails(i, j, q, nt, n):
                act.wait_ge(tail_mm, n)
                if not (i == 0 and isinstance(j, int) and j == 0):
                    act.wait_ge(tail_stored[q], 32 * (j + i * (N_PASS + 1 - q)))
                nc.scalar.activation(tst[:, q, 0:nt * P], SA[2][0:2 * NB + 2, 0:nt * P], ACT.Copy).then_inc(tail_read, 1)
                act.wait_ge(tail_read, n)
                cols = bass.ds((j * 8 + 4 * q) * P, nt * P)
                act.dma_start(O["conv_prompt"][i, 0][:, cols], tst[0:2, q, 0:nt * P]).then_inc(tail_stored[q], 16)
                act.dma_start(O["conv_sample"][i].rearrange("b r f -> (b r) f")[:, cols],
                              tst[2:2 * NB + 2, q, 0:nt * P]).then_inc(tail_stored[q], 16)

            def pooling():
                act.wait_ge(ph_mm, 1)
                for g in range(4):
                    nc.scalar.activation(
                        U[:, 4 * g:4 * g + 4, PADW + NP:].rearrange("p f (b s) -> p f b s", s=SEQW)[:, :, :, 0:PADW],
                        SA[g][:, 0:480].rearrange("p (f b s) -> p f b s", f=4, b=NB), ACT.Copy).then_inc(ph_read, 1)
                rms(SB[3], 2)
                for g in range(4):
                    for t in range(4):
                        act.wait_ge(pd_ready, 2 * g + t // 2 + 1)
                        nc.scalar.activation(xh[:, 4 * g + t], PD[:, t], ACT.Copy).then_inc(xh_done, 1)
                    if g:
                        his(C_POOL, 2 + 2 * g, 4 + 2 * g)
                for n in range(4):
                    if n == 2:
                        his(C_POOL, 10, 12)
                    hand_over(3, n)

            head(0, 0, 0)
            with act.Fori(1, H - 1) as h:
                head(h, h * C_HEAD, h * E_HEAD)
            head(H - 1, (H - 1) * C_HEAD, (H - 1) * E_HEAD)
            for i, c, e in ((0, C_FFN0, E_FFN0), (1, C_FFN1, E_FFN1)):
                ffn(i, c, e, 0, 2, 4)
                with act.Fori(1, N_PASS) as j:
                    ffn(i, c + j * C_PASS, e + j * E_PASS, j, 2, 4)
                ffn(i, c + N_PASS * C_PASS, e + N_PASS * E_PASS, N_PASS, 1, TAIL_T)
                if i == 0:
                    pooling()
            act.wait_ge(no_mm, 2)
            nc.scalar.activation(nsto, SA[0][0:NB * H, 0:DK], ACT.Copy).then_inc(no_read, 1)
            nc.scalar.activation(npst, SA[1][0:H, 0:DK], ACT.Copy).then_inc(no_read, 1)
            rms(SA[3], 4)
            act.wait_ge(pool_stored, 32)
            for i in range(12):
                act.wait_ge(y_mm, 4 * (i // 3) + 4)
                s, q = i % 3, i // 3
                n = NB * NS if s == 2 else P
                nc.scalar.activation(ytok[0:n, s, q * 512:(q + 1) * 512], YB[i % 8][0:n, :], ACT.Copy).then_inc(y_read, 1)

        @block.vector
        def _(dve):
            step = Chain(dve, dve_step)
            V = nc.vector

            def lo(c, k):
                s = k % SLOTS
                if isinstance(c, int) and c + k >= C_END:
                    return
                dve.wait_ge(hi_done, c + (k + 1))
                V.tensor_tensor(w_lo[:, s], w_raw[:, s], w_hi[:, s].bitcast(F32), ALU.subtract).then_inc(lo_done, 1)

            def los(c, k0, k1):
                for k in range(k0, k1):
                    lo(c, k)

            def x_low(stage, gain, c0, k0, k1):
                for kt in range(k0, k1):
                    dve.wait_ge(xh_done, stage * KT + kt + 1)
                    V.scalar_tensor_tensor(xl[:, kt, c0:], x[:, kt, c0:], par[:, gain * KT + kt:gain * KT + kt + 1],
                                           xh[:, kt, c0:].bitcast(F32), ALU.mult, ALU.subtract).then_inc(xl_done, 1)

            def inv_rms(k):
                dve.wait_ge(rt_ready, k)
                V.reciprocal(rbc[:, :], rt[:, :]).then_inc(r_ready, 1)
                dve.wait_ge(r_ready, k)

            def add_to_x(banks, n, c0):
                for t in range(4):
                    V.tensor_tensor(x[:, 4 * n + t, c0:], banks[t][:, c0:T], x[:, 4 * n + t, c0:], ALU.add).then_inc(evac, 1)

            dve.wait_ge(st_tr, 1)
            V.tensor_copy(par[:, :], bank[0][:, 0:7 * KT]).then_inc(st_ev, 1)
            for i in range(2):
                dve.wait_ge(st_tr, 2 + i)
                V.tensor_copy(cpar[:, i].rearrange("p a f -> p (a f)"), bank[1 + i][:, 0:4 * FT]).then_inc(st_ev, 1)
            dve.wait_ge(st_tr, 4)
            V.tensor_copy(nT[:, :, :, :].rearrange("p k b h -> p (k b h)"), bank[3][:, 0:64]).then_inc(st_ev, 1)
            for kt in range(KT):
                dve.wait_ge(st_tr, 5 + kt)
                V.tensor_copy(x[:, kt], bank[(4 + kt) % 8][:, 0:T]).then_inc(st_ev, 1)
            dve.wait_ge(in_gate, 16 * 5)
            dve.wait_ge(consts, 2)
            dve.wait_ge(st_ev, 4)
            gain = par[:, 0:KT].unsqueeze(2).to_broadcast([P, KT, 4])
            V.tensor_tensor(wgg[:, :, 0:4], wgr[:, :, 0:4], gain, ALU.mult)
            V.tensor_tensor(wgg[:, :, 32:36], wgr[:, :, 4:8], gain, ALU.mult).then_inc(wgg_ready, 1)
            los(0, 0, SLOTS)
            dve.wait_ge(st_ev, 4 + KT)
            x_low(0, 0, 0, 0, KT)
            inv_rms(1)
            dve.wait_ge(gates_mm, 1)
            h4 = slice(0, H)
            step(V.tensor_tensor(row[0], SB[0][0:36, 0:T], rbc[0:36, :], ALU.mult))
            V.tensor_scalar(row[1][h4], row[0][h4], bg[0:H, :], None, ALU.add)
            step(V.tensor_scalar(row[2][h4], row[0][32:36], bg[32:36, :], None, ALU.add))
            V.scalar_tensor_tensor(row[4][h4], row[2][h4], -1.0, row[2][h4], ALU.mult, ALU.min).then_inc(row_abs, 1)
            dve.wait_ge(row_ln, 1)
            step(V.scalar_tensor_tensor(row[3][h4], row[2][h4], 0.0, row[6][h4], ALU.min, ALU.subtract))
            step(V.tensor_tensor_scan(row[7][h4], row[9][h4], row[3][h4], 0.0, ALU.mult, ALU.add))
            step(V.tensor_tensor(row[8][h4], row[1][h4], row[7][h4], ALU.subtract))
            step(V.tensor_copy(row[4][h4], row[8][h4]))
            V.tensor_scalar(row[4][h4, 0:1], row[8][h4, 0:1], 0.0, None, ALU.max)
            step(V.tensor_tensor(row[4][h4, NP:T:NS], row[8][h4, NP:T:NS], row[11][h4, 0:NB], ALU.max))
            step(V.tensor_tensor_scan(mrow[:, :], row[10][h4], row[4][h4], 0.0, ALU.add, ALU.max))
            V.tensor_tensor(mtrow[:, :], row[7][h4], mrow[:, :], ALU.add).then_inc(rows_ready, 1)

            def head(h, c, e):
                first = isinstance(h, int) and h == 0
                if not first:
                    dve.wait_ge(mb_ready, h)
                V.tensor_scalar(mm[:, :], mrow[:, :], negeye[:, bass.ds(h, 1)], None, ALU.mult).then_inc(mrow_ready, 1)
                los(c, 4, 12)
                if first:
                    dve.wait_ge(gcol_mm, 1)
                    V.tensor_copy(gcol[:, 0:2].rearrange("p s a h -> p (s a h)"), SB[2][:, 0:16])
                    V.tensor_copy(gcol[0:TL, 2].rearrange("p a h -> p (a h)"), SB[2][0:TL, 16:24]).then_inc(gcol_a, 1)
                    dve.wait_ge(gcol_em, 1)
                V.tensor_copy(hcol[:, :, :].unsqueeze(3), gcol[:, :, :, bass.ds(h, 1)])
                V.tensor_copy(mbh[:, :].unsqueeze(2), mb[:, :, bass.ds(h, 1)])
                V.tensor_copy(nh[:, :, :].unsqueeze(3), nT[:, :, :, bass.ds(h, 1)])
                step(V.tensor_copy(gh[:, :], par[:, bass.ds(5 * KT + 4 * h, 4)]))
                dve.wait_ge(mb_ready, h + 1)
                nM = SB[3]
                V.tensor_scalar(X[:, X0:X1], nM[:, 0:NP], hcol[:, 0, 0:1], 0.0, ALU.add, ALU.min)
                V.tensor_scalar(X[:, X1:X2], nM[:, P:NP], hcol[:, 1, 0:1], 0.0, ALU.add, ALU.min)
                V.tensor_scalar(X[0:TL, X2:XW], nM[0:TL, 2 * P:T], hcol[0:TL, 2, 0:1], 0.0, ALU.add, ALU.min)
                V.tensor_tensor(seqs(WI), seqs(nM[:, NP:T]), mbh[:, :].unsqueeze(2).to_broadcast([P, NB, NS]),
                                ALU.add).then_inc(mb_read, 1)
                dve.wait_ge(chunk_used, c + 8)
                for t in range(2):
                    V.scalar_tensor_tensor(qk[:, t], SA[t][:, 0:T], DK ** -0.5, rbc[:, :], ALU.mult, ALU.mult).then_inc(evac, 1)
                for t in range(2, 4):
                    V.tensor_tensor(qk[:, t], SA[t][:, 0:T], rbc[:, :], ALU.mult).then_inc(evac, 1)
                dve.wait_ge(x_exp, h + 1)
                V.tensor_tensor(X, X, mask[:, :], ALU.mult).then_inc(pm_ready, 1)
                dve.wait_ge(evac, e + 2)
                for k in range(2):
                    step.mark(V.tensor_tensor(qmb(k), seqs(qk[:, k, NP:T]), seqs(WI), ALU.mult))
                step.sync()
                for k in range(2):
                    m_ = V.tensor_tensor(seqs(qn[:, k, META:TL]), qmb(k), nh[:, k, :].unsqueeze(2).to_broadcast([P, NB, NS]),
                                         ALU.mult)
                m_.then_inc(qm_ready, 1)
                los(c, 12, 14)
                dve.wait_ge(s_ready, h + 1)
                dve.wait_ge(pm_ready, h + 1)
                V.tensor_tensor(PS0[:, 0:NP], SA[0][:, X0:X1], X[:, X0:X1], ALU.mult)
                V.tensor_tensor(PS1[:, 0:NP - P], SA[0][:, X1:X2], X[:, X1:X2], ALU.mult)
                V.tensor_tensor(PS2[0:TL, :], SA[0][0:TL, X2:XW], X[0:TL, X2:XW], ALU.mult).then_inc(ps_ready, 1)
                los(c, 14, 19)
                dve.wait_ge(chunk_used, c + 16)
                for t in range(4):
                    V.tensor_tensor(v[:, t], SB[t][:, 0:T], rbc[:, :], ALU.mult).then_inc(evac, 1)
                los(c, 19, 22)
                for f in range(2, 4):
                    dve.wait_ge(vt_ready, 4 * h + f + 1)
                    V.tensor_copy(vtok[:, 0:2, f * P:(f + 1) * P], SA[f][:, 0:2 * P].rearrange("p (s n) -> p s n", n=P))
                    m_ = V.tensor_copy(vtok[0:TL, 2, f * P:(f + 1) * P], SA[f][0:TL, 2 * P:3 * P])
                m_.then_inc(vtok_v, 1)
                los(c, 22, 27)
                dve.wait_ge(chunk_used, c + 24)
                for t in range(4):
                    V.tensor_tensor(o[:, t], SB[t][:, 0:T], rbc[:, :], ALU.mult).then_inc(evac, 1)
                lo(c, 27)
                dve.wait_ge(den_ready, h + 1)
                V.tensor_copy(stat[:, 0, 0:2], SA[3][:, 0:2])
                V.tensor_copy(stat[0:TL, 0, 2:3], SA[3][0:TL, 2:3]).then_inc(den_read, 1)
                dve.wait_ge(den_read, h + 1)
                step(V.scalar_tensor_tensor(stat[:, 1], stat[:, 0], -1.0, stat[:, 0], ALU.mult, ALU.max))
                step(V.tensor_tensor(stat[:, 1], stat[:, 1], hcol[:, :, 1], ALU.max))
                step(V.reciprocal(stat[:, 2], stat[:, 1]))
                step(V.tensor_tensor(stat[:, 1], stat[:, 2], stat[:, 2], ALU.mult))
                for b in range(NB):
                    dve.wait_ge(cnew_ready, NB * h + b + 1)
                    for k in range(2):
                        m_ = V.scalar_tensor_tensor(Cr[:, b % 4, k], Cr[:, b % 4, k], WI[:, NS * b + NS - 1:NS * b + NS],
                                                    SB[2 * (b % 2) + k][:, :], ALU.mult, ALU.add)
                    m_.then_inc(c_updated, 1)
                dve.wait_ge(ss_done, 3 * h + 3)
                V.tensor_tensor(stat[:, 4], stat[:, 1], stat[:, 3], ALU.mult).then_inc(z_ready, 1)
                dve.wait_ge(z_sqrt, h + 1)
                step(V.reciprocal(stat[:, 6], stat[:, 5]))
                step(V.tensor_tensor(stat[:, 7], stat[:, 6], stat[:, 2], ALU.mult))
                for s, (t0, n) in enumerate(TOK):
                    V.tensor_scalar(hn[0:n, s], SA[s][0:n, :], stat[0:n, 7, s:s + 1], None, ALU.mult).then_inc(hn_ready, 1)
                dve.wait_ge(n_ready, h + 1)
                for k in range(2):
                    step.mark(V.tensor_tensor(nt2[:, k], nh[:, k], WI[:, NS - 1::NS], ALU.mult))
                step.sync()
                for k in range(2):
                    V.tensor_tensor(nT[:, k, :, bass.ds(h, 1)], nt2[:, k].unsqueeze(2), SA[3][:, 16 * k + 1:16 * k + 9].unsqueeze(2),
                                    ALU.add)
                    m_ = V.tensor_copy(nP[:, k, bass.ds(h, 1)], SA[3][:, 16 * k:16 * k + 1])
                m_.then_inc(n_read, 1)
                dve.wait_ge(ht_ready, h + 1)
                dve.wait_ge(sig_done, h + 1)
                for f in range(4):
                    V.scalar_tensor_tensor(hf[:, f], SB[f][:, 0:T], gh[:, f:f + 1], o[:, f], ALU.mult, ALU.mult).then_inc(hf_ready, 1)
                for f in range(4):
                    dve.wait_ge(hh_ready, 4 * h + f + 1)
                    V.tensor_tensor(hl[:, f], hf[:, f], hh[:, f].bitcast(F32), ALU.subtract).then_inc(hl_ready, 1)
                for n in range(4):
                    los(c, 28 + 2 * n, 30 + 2 * n)
                    dve.wait_ge(chunk_used, c + (26 + 2 * n))
                    add_to_x((SA, SB)[n % 2], n, 0)
                    if isinstance(h, int) and h == H - 1:
                        x_low(1, 2, G0[0], 4 * n, 4 * n + 4)

            def qmb(k):
                return qm[:, k].rearrange("p (b s) -> p b s", s=TL + NS)[:, :, META:META + NS]

            def ffn(i, c, e, j, nq, nt):
                first = isinstance(j, int) and j == 0
                a0, g0 = A0[i], G0[i]
                eb = k0 = 0
                V.tensor_copy(cp[:, :, 0:nq * nt], cpar[:, i, :, bass.ds(8 * j, nq * nt)])
                for q in range(nq):
                    los(c, k0 + 4, k0 + 11)
                    if first and q == 0:
                        inv_rms((2, 4)[i])
                    dve.wait_ge(chunk_used, c + (k0 + 8))
                    if not (i == 0 and first and q == 0):
                        dve.wait_ge(last_ready, i * HB + 2 * j + q)
                    if i == 1 and first and q == 0:
                        dve.wait_ge(pt_mm, 2)
                    for t in range(nt):
                        V.tensor_tensor(E[:, t, 2 + g0:2 + NP], SA[t][:, g0:NP], rbc[:, g0:NP], ALU.mult)
                        V.tensor_tensor(seqs(E[:, t, 2 + NP:], 2), seqs(SA[t][:, NP:T]), seqs(rbc[:, NP:T]), ALU.mult).then_inc(evac, 1)
                    lo(c, k0 + 11)
                    dve.wait_ge(hist_read, i * HB + 2 * j + q + 1)
                    for t in range(nt):
                        f = 4 * q + t
                        dve.wait_ge(tap0_ready, i * FT + 8 * j + (f + 1))
                        step(V.scalar_tensor_tensor(Tt[:, t, a0:GW - 2], E[:, t, a0 + 1:GW - 1], cp[:, 1, f:f + 1],
                                                    Tt[:, t, a0:GW - 2], ALU.mult, ALU.add))
                        V.scalar_tensor_tensor(Tt[:, t, a0:GW - 2], E[:, t, a0:GW - 2], cp[:, 0, f:f + 1],
                                               Tt[:, t, a0:GW - 2], ALU.mult, ALU.add).then_inc(taps_ready, 1)
                    for t in range(nt):
                        dve.wait_ge(silu_ready, i * FT + 8 * j + (4 * q + t + 1))
                        V.tensor_tensor(Sp[:, t, a0:NP], Tt[:, t, a0:NP], rbc[:, a0:NP], ALU.mult)
                        m_ = V.tensor_tensor(seqs(Sp[:, t, NP:T]),
                                             Tt[:, t, 2 + NP:].rearrange("p (b s) -> p b s", s=NS + 2)[:, :, 0:NS],
                                             seqs(rbc[:, NP:T]), ALU.mult)
                        step.mark(m_)
                    los(c, k0 + 12, k0 + 19)
                    dve.wait_ge(chunk_used, c + (k0 + 16))
                    step.sync()
                    for t in range(nt):
                        V.tensor_tensor(fh[:, t, a0:], SB[t][:, a0:T], Sp[:, t, a0:], ALU.mult).then_inc(evac, 1)
                    lo(c, k0 + 19)
                    for t in range(nt):
                        dve.wait_ge(hh_ready, 4 * H + i * FT + 8 * j + (4 * q + t + 1))
                        V.tensor_tensor(hl[:, 4 * q + t, a0:], fh[:, t, a0:], hh[:, 4 * q + t, a0:].bitcast(F32),
                                        ALU.subtract).then_inc(hl_ready, 1)
                    k0 += KT
                    eb += 2 * nt
                nd = (nq * nt + 1) // 2
                for n in range(4):
                    los(c, k0 + 4, k0 + 3 + nd)
                    k0 += nd
                    dve.wait_ge(chunk_used, c + k0)
                    add_to_x((SA, SB)[n % 2], n, a0)
                    lo(c, k0 + 3)

            def pooling():
                inv_rms(3)

                def out(g):
                    los(C_POOL, 4 + 2 * g, 6 + 2 * g)
                    dve.wait_ge(chunk_used, C_POOL + 2 * g + 2)
                    for t in range(4):
                        f = 4 * g + t
                        V.scalar_tensor_tensor(x[:, f], (SA, SB)[g % 2][t][:, 0:T], par[:, 6 * KT + f:6 * KT + f + 1], x[:, f],
                                               ALU.mult, ALU.add).then_inc(evac, 1)

                def prompt(ap):
                    return ap[:, :, PADW:PADW + NP]

                def samples(ap):
                    return ap[:, :, PADW + NP:].rearrange("p f (b s) -> p f b s", s=SEQW)[:, :, :, PADW:]

                dve.wait_ge(tail_stored[0], 32 * (N_PASS + 1))
                dve.wait_ge(tail_stored[1], 32 * N_PASS)
                for p in range(KT // 2):
                    g = p // 2
                    w = 2 << g
                    u = U[:, 2 * p:2 * p + 2]
                    pd = PD[:, p % 2 * 2:p % 2 * 2 + 2]
                    dve.wait_ge(gx_ready, 2 * p + 2)
                    dve.wait_ge(ph_read, g + 1)
                    step.mark(V.tensor_tensor(prompt(u), prompt(u), rbc[:, 0:NP].unsqueeze(1).to_broadcast([P, 2, NP]), ALU.mult))
                    step(V.tensor_tensor(samples(u), samples(u),
                                         seqs(rbc[:, NP:]).unsqueeze(1).to_broadcast([P, 2, NB, NS]), ALU.mult))
                    src, n, at = u, 1, 0
                    while n < w:
                        at += n
                        to = (Wa, Wb)[n in (2, 8)]
                        step(V.tensor_tensor(to[:, :, at:], src[:, :, at:], src[:, :, at - n:UW - n], ALU.add))
                        src, n = to, 2 * n
                    if p >= 2:
                        dve.wait_ge(xl_done, 2 * KT + 2 * p - 2)
                    step.mark(V.scalar_tensor_tensor(pd[:, :, 0:NP], prompt(src), 1.0 / w, prompt(u), ALU.mult, ALU.subtract))
                    for t in range(2):
                        V.scalar_tensor_tensor(seqs(pd[:, t, NP:]), seqs(src[:, t, PADW + NP:], PADW), 1.0 / w,
                                               seqs(u[:, t, PADW + NP:], PADW), ALU.mult, ALU.subtract)
                    step.sync()
                    few = pd[:, :, 0:w - 1]
                    step(V.tensor_tensor(few, prompt(src)[:, :, 0:w - 1], rc[:, 0:w - 1].unsqueeze(1).to_broadcast([P, 2, w - 1]),
                                         ALU.mult))
                    V.tensor_tensor(few, few, prompt(u)[:, :, 0:w - 1], ALU.subtract).then_inc(pd_ready, 1)
                    if g and p % 2:
                        out(g - 1)
                out(3)

            step.base, step.n, before = 0, step.n, step.n
            head(0, 0, 0)
            per, step.n = step.n - before, before
            with dve.Fori(1, H - 1) as h:
                step.base = h * per
                head(h, h * C_HEAD, h * E_HEAD)
            step.base, step.n = (H - 1) * per, before
            head(H - 1, (H - 1) * C_HEAD, (H - 1) * E_HEAD)
            dve.wait_ge(hl_ready, 4 * H)
            V.memset(E[:, :, 0:2], 0.0).then_inc(e_zero, 1)
            for i, c, e in ((0, C_FFN0, E_FFN0), (1, C_FFN1, E_FFN1)):
                if i == 1:
                    x_low(3, 3, G0[1], 0, KT)
                before, base = step.n, step.base
                ffn(i, c, e, 0, 2, 4)
                per, step.n = step.n - before, before
                with dve.Fori(1, N_PASS) as j:
                    step.base = j * per + base
                    ffn(i, c + j * C_PASS, e + j * E_PASS, j, 2, 4)
                step.base = (N_PASS - 1) * per + base
                ffn(i, c + N_PASS * C_PASS, e + N_PASS * E_PASS, N_PASS, 1, TAIL_T)
                if i == 0:
                    pooling()
            inv_rms(5)
            for kt in range(KT):
                if kt >= 4:
                    dve.wait_ge(y_mm, kt - 3)
                V.scalar_tensor_tensor(yT[:, kt % 4, META:], x[:, kt, META:], par[:, 4 * KT + kt:4 * KT + kt + 1],
                                       rbc[:, META:], ALU.mult, ALU.mult).then_inc(y_ready, 1)

        @block.gpsimd
        def _(pool):
            step = Chain(pool, pool_step)
            G = nc.gpsimd
            G.memset(ones[:, :], 1.0)
            step(G.memset(ident[:, :], 0.0))
            G.affine_select(out=ident[:, :], in_=ident[:, :], compare_op=ALU.not_equal, fill=1.0, base=0,
                            pattern=[[-1, P]], channel_multiplier=1).then_inc(consts, 1)
            G.memset(eps[:, :], EPS)
            G.memset(stat[:, :, :], 1.0)
            G.memset(gcol[:, :, :, :], 0.0)
            G.memset(row[9][0:H], 1.0)
            G.memset(row[10][0:H], 0.0)
            G.memset(negeye[:, :], 0.0)
            for t in range(16):
                G.memset(rc[:, t:t + 1], 1.0 / (t + 1))
            step(G.memset(wgg, 0.0))
            for s, value in ((9, 0.0), (10, BIG)):
                G.memset(row[s][0:H, 0:1], value)
                G.memset(row[s][0:H, NP:T:NS], value)
            step(G.affine_select(out=negeye[:, :], in_=negeye[:, :], compare_op=ALU.not_equal, fill=-1.0, base=0,
                                 pattern=[[-1, H]], channel_multiplier=1))
            step(G.memset(mask[:, :], 1.0))
            for x0, x1 in ((X0, X1), (X1, X2)):
                G.affine_select(out=mask[:, x0:x1], in_=mask[:, x0:x1], compare_op=ALU.is_ge, fill=0.0, base=0,
                                pattern=[[1, x1 - x0]], channel_multiplier=-1)
            step(G.affine_select(out=mask[:, X2:XW], in_=mask[:, X2:XW], compare_op=ALU.is_ge, fill=0.0, base=0,
                                 pattern=[[1, TL]], channel_multiplier=-1))
            own = mask[:, X2 + META:XW].rearrange("p (b s) -> p b s", s=NS)
            G.affine_select(out=own, in_=own, compare_op=ALU.is_ge, fill=0.0, base=-META,
                            pattern=[[-NS, NB], [0, NS]], channel_multiplier=1)
            pool.wait_ge(st_tr, 4)
            G.memset(area[:, 6528:9216], 0.0).then_inc(consts, 1)

            def sum_of_squares(k):
                pool.wait_ge(rms_mm, k - 1) if k > 1 else None
                for kt in range(KT):
                    pool.wait_ge(st_sq, k * KT + kt + 1)
                    if kt:
                        pool.wait_ge(st_squ, k * KT + kt)
                        m_ = G.tensor_tensor(acc[:, :], acc[:, :], sqf[:, kt % 4], ALU.add)
                    else:
                        m_ = G.tensor_copy(acc[:, :], sqf[:, 0])
                    m_.then_inc(st_squ, 1)
                pool.wait_ge(st_squ, k * KT + KT)
                pool.sem_inc(ssq_ready, 1)

            def head(h):
                first = isinstance(h, int)
                pool.wait_ge(pm_ready, h + 1)
                pool.wait_ge(ktok_ready, h + 1)
                for b in range(NB):
                    if not (first and b < 2):
                        wait_apart(pool, pool_passed, cnew_ready, NB * h + b - 1)
                    col = X2 + META + NS * b + NS - 1
                    G.tensor_scalar(wkb[0:TL, b % 2], ktok[0:TL, 2], X[0:TL, col:col + 1], None, ALU.mult).then_inc(wkb_ready, 1)
                    if b == 1:
                        G.tensor_scalar(wkp[:, 0], ktok[:, 0], X[:, X1 - 1:X1], None, ALU.mult)
                        G.tensor_scalar(wkp[:, 1], ktok[:, 1], X[:, X2 - 1:X2], None, ALU.mult)
                        G.tensor_scalar(wkp[0:TL, 2], ktok[0:TL, 2], X[0:TL, X2 + META - 1:X2 + META], None,
                                        ALU.mult).then_inc(wkp_ready, 1)

            head(0)
            with pool.Fori(1, H) as h:
                head(h)

            def last_rows(i, e, j, nq, nt):
                for q in range(nq):
                    n = i * HB + 2 * j + q
                    if not (isinstance(j, int) and j == 0):
                        pool.wait_ge(tail_mm, n - 1)
                    elif i:
                        pool.wait_ge(tail_mm, HB)
                    for t in range(nt):
                        wait_apart(pool, pool_passed, evac, e + (2 * nt * q + t + 1))
                        m_ = G.tensor_copy(last[:, q, t].rearrange("p (b s) -> p b s", s=2),
                                           E[:, t, NP - NS:].rearrange("p (b s) -> p b s", s=NS + 2)[:, :, NS:])
                    m_.then_inc(last_ready, 1)

            sum_of_squares(1)
            for b in range(4):
                pool.wait_ge(c_stored[b], 2 * H * 16)
            pool.wait_ge(cst_stored, 16 * H)
            G.memset(U[:, :, 0:PADW], 0.0).then_inc(u_pads, 1)
            for i, e in ((0, E_FFN0), (1, E_FFN1)):
                last_rows(i, e, 0, 2, 4)
                with pool.Fori(1, N_PASS) as j:
                    last_rows(i, e + j * E_PASS, j, 2, 4)
                last_rows(i, e + N_PASS * E_PASS, N_PASS, 1, TAIL_T)
                if i == 0:
                    sum_of_squares(2)
                    for g in range(4):
                        for t in range(4):
                            kt = 4 * g + t
                            pool.wait_ge(xh_done, 2 * KT + kt + 1)
                            G.tensor_tensor(xl[:, kt], PD[:, t], xh[:, kt].bitcast(F32), ALU.subtract).then_inc(xl_done, 1)
                        G.tensor_copy(hrow[:, 4 * g:4 * g + 4].rearrange("p f (b s) -> p f b s", s=PADW),
                                      U[:, 4 * g:4 * g + 4, PADW + NP:].rearrange("p f (b s) -> p f b s", s=SEQW)[:, :, :, NS:]
                                      ).then_inc(hrow_ready, 4)
                    sum_of_squares(3)
            sum_of_squares(4)


INPUTS = ["x_prompt", "x_sample", "state_mlstm_C", "state_mlstm_n", "state_mlstm_m", "state_pool", "state_ffn_conv",
          "meta_tokens", "norm_mix", "norm_ffn", "norm_final", "w_mlstm_in", "b_mlstm_gate", "g_mlstm_out",
          "w_mlstm_out", "w_pool", "pool_scale", "w_up", "conv_w", "conv_b", "w_down"]
OUTPUTS = [("y_prompt", (1, SEQ, D)), ("y_sample", (NB, NS, D)), ("C_prompt", (1, 1, H, DK, DV)), ("n_prompt", (1, 1, H, DK)),
           ("m_prompt", (1, 1, H)), ("pool_prompt", (1, 1, PADW, D)), ("conv_prompt", (2, 1, 2, F)),
           ("C_sample", (1, NB, H, DK, DV)), ("n_sample", (1, NB, H, DK)), ("m_sample", (1, NB, H)),
           ("pool_sample", (1, NB, PADW, D)), ("conv_sample", (2, NB, 2, F))]


def kernel(**inputs):
    import numpy as np
    from concourse import bacc
    from concourse.bass_utils import run_bass_kernel_spmd

    nc = bacc.Bacc("TRN2", target_bir_lowering=False, num_devices=1)
    arrays, I, O = {}, {}, {}
    for name in INPUTS:
        a = np.ascontiguousarray(inputs[name])
        arrays[f"in_{name}"] = a
        I[name] = nc.dram_tensor(f"in_{name}", a.shape, mybir.dt.from_np(a.dtype), kind="ExternalInput").ap()
    for name, shape in OUTPUTS:
        O[name] = nc.dram_tensor(f"out_{name}", shape, F32, kind="ExternalOutput").ap()
    program(nc, I, O)
    r = run_bass_kernel_spmd(nc, [arrays], core_ids=[0])
    return tuple(r.results[0][f"out_{name}"] for name, _ in OUTPUTS)
```

```python
from contextlib import ExitStack

import concourse.bass as bass
from concourse import mybir

F32 = mybir.dt.float32
F32R = mybir.dt.float32r
ALU = mybir.AluOpType
ACT = mybir.ActivationFunctionType

P = 128
D = 2048
KT = D // P
META, SEQ = 16, 256
NP = META + SEQ
NB, NS = 8, 8
T = NP + NB * NS
H, DK, DV = 4, 256, 512
QK_W = H * DK
V_W = H * DV
EPS = 1e-6
F = 5504
FT = F // P
TOK = [(0, 128), (128, 128), (256, T - 256)]
TL = TOK[2][1]
PADW = 15
CW = 512
SLOTS = 4
X0, X1, X2, XW = 0, NP, NP + NP - 128, NP + NP - 128 + TL
SEQW = PADW + NS
UW = PADW + NP + NB * SEQW
GW = 2 + NP + NB * (2 + NS)
BIG = -1.0e38

C_HEAD = 3 * (KT // 2) + 4 * 2
C_FFN0 = H * C_HEAD
PASS_T = 8
N_PASS = FT // PASS_T
C_PASS = 4 * (KT // 2) + 4 * (PASS_T // 2)
TAIL_T = FT - N_PASS * PASS_T
C_TAIL = 2 * (KT // 2) + 4 * 2
C_POOL = C_FFN0 + N_PASS * C_PASS + C_TAIL
C_FFN1 = C_POOL + 4 * 2
HB = 2 * N_PASS + 1
C_END = C_FFN1 + N_PASS * C_PASS + C_TAIL
E_HEAD = 12 + 16
E_FFN0 = H * E_HEAD
E_PASS = 16 + 16
E_TAIL = 2 * TAIL_T + 16
E_POOL = E_FFN0 + N_PASS * E_PASS + E_TAIL
E_FFN1 = E_POOL + 16
E_END = E_FFN1 + N_PASS * E_PASS + E_TAIL
G0 = [0, META - 2]
A0 = [0, META]


class Chain:

    def __init__(self, eng, sem):
        self.eng, self.sem, self.base, self.n = eng, sem, 0, 0

    def __call__(self, ins):
        ins.then_inc(self.sem, 1)
        self.n += 1
        self.eng.wait_ge(self.sem, self.base + self.n)

    def mark(self, ins):
        ins.then_inc(self.sem, 1)
        self.n += 1

    def sync(self):
        self.eng.wait_ge(self.sem, self.base + self.n)


def wait_apart(eng, passed, semaphore, value):
    eng.wait_ge(semaphore, value)
    eng.sem_inc(passed, 1)


def program(nc, I, O):
    with ExitStack() as ctx:
        def sb(name, shape, dt=F32):
            return ctx.enter_context(nc.sbuf_tensor(name, shape, dt))

        def sem(name):
            return ctx.enter_context(nc.semaphore(name))

        bank = [ctx.enter_context(nc.psum_tensor(f"bank{i}", [P, 512], F32)) for i in range(8)]
        SA, SB = bank[0:4], bank[4:8]
        YB = [SA[2], SA[3], SA[0], SA[1]] + SB

        x = sb("x", [P, KT, T])
        xh = sb("xh", [P, KT, T], F32R)
        xl = sb("xl", [P, KT, T], F32R)
        w_raw = sb("w_raw", [P, SLOTS, 2, CW])
        w_hi = sb("w_hi", [P, SLOTS, 2, CW], F32R)
        w_lo = sb("w_lo", [P, SLOTS, 2, CW], F32R)
        hh = sb("hh", [P, PASS_T, T], F32R)
        hl = sb("hl", [P, PASS_T, T], F32R)
        ident = sb("ident", [P, P])
        ones = sb("ones", [P, P])
        mask = sb("mask", [P, XW])
        par = sb("par", [P, 7 * KT])
        cpar = sb("cpar", [P, 2, 4, FT])
        cp = sb("cp", [P, 4, PASS_T])
        rbc = sb("rbc", [P, T])
        acc = sb("acc", [P, T])

        rt = sb("rt", [P, T])
        eps = sb("eps", [P, 1])
        warm = sb("warm", [P, 1])
        nT = sb("nT", [P, 2, NB, H])
        nP = sb("nP", [P, 2, H])
        mrow = sb("mrow", [H, T])
        mtrow = sb("mtrow", [H, T])
        mm = sb("mm", [H, T])
        negeye = sb("negeye", [H, H])
        gcol = sb("gcol", [P, 3, 2, H])
        hcol = sb("hcol", [P, 3, 2])
        mb = sb("mb", [P, NB, H])
        mbh = sb("mbh", [P, NB])
        nh = sb("nh", [P, 2, NB])
        gh = sb("gh", [P, 4])
        bg = sb("bg", [36, 1])
        rc = sb("rc", [P, 16])
        stat = sb("stat", [P, 8, 3])
        nt2 = sb("nt2", [P, 2, NB])
        AREA = 15700
        area = sb("area", [P, AREA])

        def view(at, n, parts=P):
            assert at + n <= AREA
            return area[0:parts, at:at + n]

        at = 0
        qk = view(0, 4 * T).rearrange("p (f t) -> p f t", t=T)
        v = view(1344, 4 * T).rearrange("p (f t) -> p f t", t=T)
        hn = view(1344, 3 * DV).rearrange("p (s n) -> p s n", n=DV)
        o = view(2880, 4 * T).rearrange("p (f t) -> p f t", t=T)
        ktok = view(4224, 3 * DK).rearrange("p (s n) -> p s n", n=DK)
        vtok = view(4992, 3 * DV).rearrange("p (s n) -> p s n", n=DV)
        X = view(6528, XW)
        PS0 = view(7024, T)
        PS1 = view(7360, T - 128)
        PS2 = view(7568, TL)
        qm = view(7648, 2 * 704).rearrange("p (k n) -> p k n", k=2)
        qn = view(9056, 2 * TL).rearrange("p (k n) -> p k n", k=2)
        WI = view(9216, NB * NS)
        wkp = view(9280, 3 * DK).rearrange("p (s n) -> p s n", n=DK)
        wkb = view(10048, 2 * DK).rearrange("p (s n) -> p s n", n=DK)
        Cst = view(10560, 2 * DV).rearrange("p (k n) -> p k n", n=DV)
        Cr = view(11584, 4 * 2 * DV).rearrange("p (s k n) -> p s k n", s=4, k=2)
        (vh, wkbh), (vl, wkbl) = (
            (a[:, 0:2].rearrange("p f t -> p (f t)")[:, 0:DV],
             a[:, 2:4].rearrange("p f t -> p (f t)")[:, 0:2 * DK].rearrange("p (s n) -> p s n", n=DK)) for a in (hh, hl))
        hf = view(0, 4 * T).rearrange("p (f t) -> p f t", t=T)
        junk = view(0, DV)
        xtok = view(0, 3 * D).rearrange("p (s n) -> p s n", n=D)
        ptok = view(6144, P, 7 * KT)
        ctok = view(6272, 4 * P, 86).rearrange("p (s n) -> p s n", n=P)
        ntok = view(6784, DK, NB * H)
        wgr = view(9280, KT * 8).rearrange("p (k n) -> p k n", n=8)
        wgg = view(9408, KT * 36).rearrange("p (k n) -> p k n", n=36)
        sqr = view(9984, 4 * T).rearrange("p (s n) -> p s n", n=T)
        row = [view(11584 + i * T, T, 36) for i in range(12)]
        E = view(0, 4 * GW).rearrange("p (f t) -> p f t", t=GW)
        Tt = view(1416, 4 * GW).rearrange("p (f t) -> p f t", t=GW)
        Sp = view(2832, 4 * T).rearrange("p (f t) -> p f t", t=T)
        fh = view(4176, 4 * T).rearrange("p (f t) -> p f t", t=T)
        hb = view(5620, 2 * CW, 2 * NB).rearrange("p (s n) -> p s n", n=CW)
        tst = view(6644, 2 * CW, 2 * NB + 2).rearrange("p (s n) -> p s n", n=CW)
        last = view(15204, 2 * 4 * 2 * (NB + 1)).rearrange("p (q f n) -> p q f n", q=2, f=4)
        sqf = view(2880, 4 * T).rearrange("p (f t) -> p f t", t=T)
        pbuf = view(768, D, NB * PADW)
        hrow = view(0, KT * NB * PADW).rearrange("p (f n) -> p f n", f=KT)
        U = view(7668, KT * UW).rearrange("p (f t) -> p f t", t=UW)
        Wa, Wb = (view(at, 2 * UW).rearrange("p (f t) -> p f t", t=UW) for at in (1920, 6644))
        PD = view(4224, 4 * T).rearrange("p (f t) -> p f t", t=T)
        psto = view(7668, D, NB * PADW)
        pstp = view(9716, D, PADW)
        ytok = view(7668, 3 * D).rearrange("p (s n) -> p s n", n=D)
        nsto = view(5620, DK, NB * H)
        npst = view(5876, DK, H)

        def seqs(ap, pad=0):
            return ap.rearrange("p (b s) -> p b s", s=NS + pad)[:, :, pad:]

        raw_landed = [sem(f"raw_landed{s}") for s in range(SLOTS)]
        hi_done, lo_done, chunk_used = sem("hi_done"), sem("lo_done"), sem("chunk_used")
        evac = sem("accumulator_read")
        dve_step, pool_step = sem("dve_step"), sem("pool_step")
        in_par, in_gate = sem("in_par"), sem("in_gate")
        in_x = [sem(f"in_x{s}") for s in range(3)]
        consts, warmed = sem("consts"), sem("warmed")
        pe_passed, pool_passed = sem("pe_passed"), sem("pool_passed")
        st_tr, st_ev = sem("start_transposed"), sem("start_read")
        st_sq, st_squ = sem("square_ready"), sem("square_used")
        xh_done, xl_done = sem("xh_done"), sem("xl_done")
        ssq_ready, rms_mm, rt_ready, r_ready = sem("ssq_ready"), sem("rms_mm"), sem("rt_ready"), sem("r_ready")
        wgg_ready, gates_mm = sem("wgg_ready"), sem("gates_mm")
        row_abs, row_exp, row_ln, rows_ready = sem("row_abs"), sem("row_exp"), sem("row_ln"), sem("rows_ready")
        gcol_mm, gcol_a, gcol_em = sem("gcol_mm"), sem("gcol_a"), sem("gcol_em")
        mrow_ready, mb_ready, mb_read = sem("mrow_ready"), sem("mb_ready"), sem("mb_read")
        x_exp, pm_ready, qm_ready = sem("x_exp"), sem("pm_ready"), sem("qm_ready")
        s_ready, kt_ready, ps_ready, ktok_ready = sem("s_ready"), sem("kt_ready"), sem("ps_ready"), sem("ktok_ready")
        sig_done, vt_ready, vtok_a, vtok_v = sem("sig_done"), sem("vt_ready"), sem("vtok_a"), sem("vtok_v")
        num_ready, den_ready, den_read = sem("num_ready"), sem("den_ready"), sem("den_read")
        c_landed = [sem(f"c_landed{s}") for s in range(4)]
        c_stored = [sem(f"c_stored{s}") for s in range(4)]
        wkp_ready, wkb_ready = sem("wkp_ready"), sem("wkb_ready")
        vh_ready, vl_ready, wkbh_ready, wkbl_ready = sem("vh_ready"), sem("vl_ready"), sem("wkbh_ready"), sem("wkbl_ready")
        e_zero, cnew_ready, c_updated = sem("e_zero"), sem("cnew_ready"), sem("c_updated")
        cp_ready, cst_ready, cst_stored = sem("cp_ready"), sem("cst_ready"), sem("cst_stored")
        n_ready, n_read = sem("n_ready"), sem("n_read")
        ss_done, z_ready, z_sqrt, hn_ready = sem("ss_done"), sem("z_ready"), sem("z_sqrt"), sem("hn_ready")
        ht_ready, hf_ready, hh_ready, hl_ready = sem("ht_ready"), sem("hf_ready"), sem("hh_ready"), sem("hl_ready")
        hb_landed = [sem(f"hb_landed{s}") for s in range(2)]
        hist_mm, hist_read, tail_mm, tail_read = sem("hist_mm"), sem("hist_read"), sem("tail_mm"), sem("tail_read")
        tail_stored = [sem(f"tail_stored{s}") for s in range(2)]
        tap0_ready, taps_ready, silu_ready = sem("tap0_ready"), sem("taps_ready"), sem("silu_ready")
        gx_ready, u_pads, u_ready = sem("gx_ready"), sem("u_pads"), sem("u_ready")
        pd_low = sem("pd_low")
        in_pool, ph_mm, ph_read, pd_ready = sem("in_pool"), sem("ph_mm"), sem("ph_read"), sem("pd_ready")
        last_ready, hrow_ready = sem("last_ready"), sem("hrow_ready")
        pt_mm, pt_read = sem("pt_mm"), sem("pt_read")
        y_ready, y_mm, no_mm, no_read = sem("y_ready"), sem("y_mm"), sem("no_mm"), sem("no_read")
        y_read = [sem("y_read_scalar"), sem("y_read_vector")]
        stored, pool_stored = sem("stored"), sem("pool_stored")

        block = ctx.enter_context(nc.Block())

        w_in = I["w_mlstm_in"][0].rearrange("(k p) n -> p k n", p=P)
        w_out = I["w_mlstm_out"][0].rearrange("(k p) n -> p k n", p=P)
        w_pool = [I["w_pool"][0, g].rearrange("(k p) n -> p k n", p=P) for g in range(4)]
        w_up = [I["w_up"][i].rearrange("(k p) n -> p k n", p=P) for i in range(2)]
        w_down = [I["w_down"][i].rearrange("(k p) n -> p k n", p=P) for i in range(2)]

        @block.sync
        def _(sp):
            def chunk(c, k, parts):
                s = k % SLOTS
                if not (isinstance(c, int) and c + k < SLOTS):
                    sp.wait_ge(lo_done, c + (k - SLOTS + 1))
                for to, src in parts:
                    sp.dma_start(to(w_raw[:, s]), src).then_inc(raw_landed[s], 16)

            def by_row(w, k0, c0, n=CW):
                return [(lambda r, j=j: r[:, j, 0:n], w[:, bass.ds(k0 + j, 1), bass.ds(c0, n)].rearrange("p a n -> p (a n)"))
                        for j in range(2)]

            def one_row(w, k0, c0):
                return [(lambda r, j=j: r[:, 0, j * 256:j * 256 + 256],
                         w[:, bass.ds(k0, 1), bass.ds(c0 + j * 256, 256)].rearrange("p a n -> p (a n)"))
                        for j in range(2)]

            sp.dma_start(xtok[0:META, 0, :], I["meta_tokens"]).then_inc(in_x[0], 16)
            sp.dma_start(xtok[META:P, 0, :], I["x_prompt"][0, 0:P - META]).then_inc(in_x[0], 16)
            sp.dma_start(xtok[:, 1, :], I["x_prompt"][0, P - META:2 * P - META]).then_inc(in_x[1], 16)
            sp.dma_start(xtok[0:META, 2, :], I["x_prompt"][0, 2 * P - META:SEQ]).then_inc(in_x[2], 16)
            sp.dma_start(xtok[META:TL, 2, :], I["x_sample"].rearrange("b s d -> (b s) d")).then_inc(in_x[2], 16)
            at = 0
            for a in (I["norm_mix"], I["norm_ffn"], I["norm_final"].rearrange("(a n) -> a n", a=1), I["g_mlstm_out"],
                      I["pool_scale"]):
                n = a.shape[0] * KT
                sp.dma_start(ptok[at:at + n, :], a.rearrange("a (k p) -> (a k) p", p=P)).then_inc(in_par, 16)
                at += n
            for i in range(2):
                sp.dma_start(ctok[:, 2 * i, :], I["conv_w"][i, 0:2].rearrange("j (k p) -> (j k) p", p=P)).then_inc(in_par, 16)
                sp.dma_start(ctok[0:FT, 2 * i + 1, :], I["conv_w"][i, 2].rearrange("(k p) -> k p", p=P)).then_inc(in_par, 16)
                sp.dma_start(ctok[FT:2 * FT, 2 * i + 1, :],
                             I["conv_b"][i].rearrange("(k p) -> k p", p=P)).then_inc(in_par, 16)
            sp.dma_start(ntok, I["state_mlstm_n"][0].rearrange("b h k -> (b h) k")).then_inc(in_par, 16)
            sp.dma_start(wgr, w_in[:, :, 2 * QK_W + 2 * V_W:]).then_inc(in_gate, 16)
            with nc.allow_non_contiguous_dma(reason="40 gate biases and stabilisers"):
                sp.dma_start(bg[0:H, :], I["b_mlstm_gate"][0, 0:H].rearrange("(h a) -> h a", a=1)).then_inc(in_gate, 16)
                sp.dma_start(bg[32:32 + H, :], I["b_mlstm_gate"][0, H:2 * H].rearrange("(h a) -> h a", a=1)).then_inc(in_gate, 16)
                sp.dma_start(row[11][0:H, 0:NB], I["state_mlstm_m"][0].rearrange("b h -> h b")).then_inc(in_gate, 16)
            sp.dma_start(mb[:, :, :].rearrange("p b h -> p (b h)"),
                         I["state_mlstm_m"].rearrange("a b h -> a (b h)").to_broadcast([P, NB * H])).then_inc(in_gate, 16)

            def c_load(h, b):
                if not (isinstance(h, int) and h == 0 and b < 4):
                    sp.wait_ge(c_stored[b % 4], 32 * h + 16 * (b // 4))
                src = I["state_mlstm_C"][0, b].rearrange("h (k p) v -> p (h k) v", p=P)
                sp.dma_start(Cr[:, b % 4], src[:, bass.ds(2 * h, 2), :]).then_inc(c_landed[b % 4], 16)

            def head(h, c):
                for k in range(KT // 2):
                    chunk(c, k, [(lambda r, j=j: r[:, :, j * DK:(j + 1) * DK],
                                  w_in[:, 2 * k:2 * k + 2, bass.ds(j * QK_W + h * DK, DK)]) for j in range(2)])
                for blk in range(2):
                    if blk == 1:
                        if isinstance(h, int) and h == 0:
                            sp.wait_ge(gcol_mm, 1)
                        for b in range(4):
                            c_load(h, b)
                    for k in range(KT // 2):
                        chunk(c, 8 + 8 * blk + k, by_row(w_in, 2 * k, 2 * QK_W + blk * V_W + h * DV))
                for n in range(4):
                    for k in range(2):
                        chunk(c, 24 + 2 * n + k, by_row(w_out, h * 4 + 2 * k, n * CW))
                dst = O["C_sample"][0]
                for b in range(NB):
                    sp.wait_ge(c_updated, NB * h + b + 1)
                    sp.dma_start(dst[b].rearrange("h (k p) v -> p (h k) v", p=P)[:, bass.ds(2 * h, 2), :],
                                 Cr[:, b % 4]).then_inc(c_stored[b % 4], 16)
                    if 1 <= b <= 4:
                        c_load(h, b - 1 + 4)

            def ffn(i, c, j, nq, nt):
                def histories():
                    for q in range(nq):
                        if not isinstance(j, int) or j:
                            sp.wait_ge(hist_mm, i * HB + 2 * j + q - 1)
                        elif i == 0:
                            sp.wait_ge(hl_ready, 4 * H)
                        else:
                            sp.wait_ge(hist_mm, HB)
                        sp.dma_start(hb[:, q, 0:nt * P],
                                     I["state_ffn_conv"][i].rearrange("b r f -> (b r) f")[:, bass.ds((j * 8 + 4 * q) * P, nt * P)]
                                     ).then_inc(hb_landed[q], 16)

                k0 = 0
                for q in range(nq):
                    for a in range(2):
                        for k in range(KT // 2):
                            if (q, a, k) == (0, 0, SLOTS):
                                histories()
                            chunk(c, k0 + k, by_row(w_up[i], 2 * k, a * F + (j * 8 + 4 * q) * P, nt * P))
                        k0 += KT // 2
                kd = nq * nt
                for n in range(4):
                    if n == 2 and i == 0 and nt < 4:
                        sp.wait_ge(hl_ready, 4 * H + FT)
                        sp.dma_start(pbuf, I["state_pool"][0].rearrange("b r d -> (b r) d")).then_inc(in_pool, 16)
                    for k in range(0, kd, 2):
                        f = by_row if k + 1 < kd else one_row
                        chunk(c, k0, f(w_down[i], j * 8 + k, n * CW))
                        k0 += 1

            head(0, 0)
            with sp.Fori(1, H) as h:
                head(h, h * C_HEAD)
            for i, c in ((0, C_FFN0), (1, C_FFN1)):
                ffn(i, c, 0, 2, 4)
                with sp.Fori(1, N_PASS) as j:
                    ffn(i, c + j * C_PASS, j, 2, 4)
                ffn(i, c + N_PASS * C_PASS, N_PASS, 1, TAIL_T)
                if i == 0:
                    for g in range(4):
                        for k in range(2):
                            chunk(C_POOL, 2 * g + k, by_row(w_pool[g], 2 * k, 0))
            with nc.allow_non_contiguous_dma(reason="36 stabilisers"):
                last = mtrow[:, NP - 1:T:NS]
                sp.dma_start(O["m_prompt"][0].rearrange("b h -> h b"), last[:, 0:1]).then_inc(stored, 16)
                sp.dma_start(O["m_sample"][0].rearrange("b h -> h b"), last[:, 1:]).then_inc(stored, 16)
            sp.wait_ge(no_read, 2)
            sp.dma_start(O["n_sample"][0].rearrange("b h k -> (b h) k"), nsto).then_inc(stored, 16)
            sp.dma_start(O["n_prompt"][0, 0], npst).then_inc(stored, 16)
            for q in range(4):
                for s in range(3):
                    n = NB * NS if s == 2 else P
                    i = 3 * q + s
                    sp.wait_ge(y_read[i % 2], i // 2 + 1)
                    to = O["y_sample"].rearrange("b s d -> (b s) d") if s == 2 else O["y_prompt"][0, s * P:(s + 1) * P]
                    sp.dma_start(to[:, q * 512:(q + 1) * 512], ytok[0:n, s, q * 512:(q + 1) * 512]).then_inc(stored, 16)
            sp.wait_ge(stored, 16 * (2 + 2 + 12))
            for s in range(4):
                sp.wait_ge(c_stored[s], 2 * H * 16)
            sp.wait_ge(cst_stored, 16 * H)
            sp.wait_ge(tail_stored[0], 2 * 32 * (N_PASS + 1))
            sp.wait_ge(tail_stored[1], 2 * 32 * N_PASS)

        @block.tensor
        def _(pe):
            def split_products(out, kt, s, j, m, xhk, xlk, first, last):
                wh, wl = w_hi[:, s, j, m:m + P], w_lo[:, s, j, m:m + P]
                pe.matmul(out, wh, xhk, start=first, stop=False)
                pe.matmul(out, wh, xlk, start=False, stop=False)
                return pe.matmul(out, wl, xhk, start=False, stop=last)

            def gemm(banks, c, k0, nkt, nt, xhi, xlo, c0, free=None, guard=None, fresh=None, amid=None):
                for i in range((nkt + 1) // 2):
                    if amid and i in amid:
                        amid[i]()
                    s = (k0 + i) % SLOTS
                    pe.wait_ge(lo_done, c + (k0 + i + 1))
                    if fresh:
                        fresh(2 * i)
                    for t in range(nt):
                        if i == 0 and free:
                            free(t)
                        if i == 0 and guard and t in guard:
                            pe.wait_ge(*guard[t])
                        for j in range(min(2, nkt - 2 * i)):
                            kt = 2 * i + j
                            mm_ = split_products(banks[t][:, c0:T], kt, s, j, t * P, xhi[:, kt, c0:T], xlo[:, kt, c0:T],
                                                 kt == 0, kt == nkt - 1)
                    mm_.then_inc(chunk_used, 1)

            def after(e):
                return lambda t: pe.wait_ge(evac, e + (t + 1))

            pe.wait_ge(consts, 1)
            for s, (t0, n) in enumerate(TOK):
                pe.wait_ge(in_x[s], 16 * (2, 1, 2)[s])
                for q in range(4):
                    if s == 2:
                        pe.wait_ge(st_ev, q + 1)
                    for t in range(4):
                        kt = 4 * q + t
                        m_ = pe.transpose(bank[(4 * s + q) % 8][:, t * P:t * P + n], xtok[0:n, s, kt * P:(kt + 1) * P],
                                          ident[0:n, 0:n])
                    m_.then_inc(st_tr, 1)
            pe.wait_ge(in_par, 16 * 12)
            pe.wait_ge(st_ev, 8)
            pe.transpose(SB[0][:, 0:7 * KT], ptok, ident[0:7 * KT, 0:7 * KT]).then_inc(st_tr, 1)
            for i in range(2):
                for s in range(2):
                    m_ = pe.transpose(SB[1 + i][:, s * 2 * FT:(s + 1) * 2 * FT], ctok[:, 2 * i + s, :],
                                      ident[0:2 * FT, 0:2 * FT])
                m_.then_inc(st_tr, 1)
            for k in range(2):
                m_ = pe.transpose(SB[3][:, k * 32:(k + 1) * 32], ntok[:, k * P:(k + 1) * P], ident[0:32, 0:32])
            m_.then_inc(st_tr, 1)
            pe.wait_ge(st_ev, 16)
            pe.wait_ge(wgg_ready, 1)
            for kt in range(KT):
                m_ = pe.matmul(SB[0][0:36, 0:T], wgg[:, kt, :], x[:, kt, :], start=(kt == 0), stop=(kt == KT - 1))
            m_.then_inc(gates_mm, 1)
            for kt in range(KT):
                pe.wait_ge(st_sq, kt + 1)
                m_ = pe.matmul(SB[1][:, 0:T], ones[:, :], sqr[:, kt % 4, :], start=(kt == 0), stop=(kt == KT - 1))
                m_.then_inc(st_squ, 1)

            def sum_squares(out, k):
                pe.wait_ge(ssq_ready, k)
                pe.matmul(out, ones[:, :], acc[:, :], start=True, stop=True).then_inc(rms_mm, 1)

            def head(h, c, e):
                first = isinstance(h, int)
                pe.wait_ge(xl_done, KT)

                def stabilisers():
                    if first:
                        pe.wait_ge(rows_ready, 1)
                        for s, (t0, n) in enumerate(TOK):
                            pe.transpose(SB[2][0:n, s * 8:s * 8 + 4], row[8][0:H, t0:t0 + n], ident[0:H, 0:H])
                            m_ = pe.transpose(SB[2][0:n, s * 8 + 4:s * 8 + 8], mtrow[:, t0:t0 + n], ident[0:H, 0:H])
                        m_.then_inc(gcol_mm, 1)
                    else:
                        pe.wait_ge(evac, e)
                    pe.wait_ge(mrow_ready, h + 1)
                    pe.matmul(SB[3][:, 0:T], ones[0:H, :], mm[:, :], start=True, stop=True).then_inc(mb_ready, 1)

                gemm(SA, c, 0, KT, 4, xh, xl, 0, free=None if first else after(e - 8), amid={5: stabilisers})
                guard = {3: (mb_read, h + 1)}
                if first:
                    guard[0] = (rows_ready, 1)
                    guard[1] = (r_ready, 1)
                    guard[2] = (gcol_em, 1)

                def scores():
                    pe.wait_ge(evac, e + 4)
                    for s, (x0, t0, t1, n) in enumerate(((X0, 0, NP, P), (X1, P, NP, P), (X2, 2 * P, T, TL))):
                        for k in range(2):
                            m_ = pe.matmul(SA[0][0:n, x0:x0 + t1 - t0], qk[:, 2 + k, s * P:s * P + n], qk[:, k, t0:t1],
                                           start=(k == 0), stop=(k == 1))
                    m_.then_inc(s_ready, 1)
                    for k in range(2):
                        for s, (t0, n) in enumerate(TOK):
                            m_ = pe.transpose(SA[1 + k][0:n, s * P:(s + 1) * P], qk[:, 2 + k, t0:t0 + n], ident[:, :])
                    m_.then_inc(kt_ready, 1)

                def values():
                    pe.wait_ge(evac, e + 8)
                    pe.wait_ge(ps_ready, h + 1)
                    pe.wait_ge(ktok_ready, h + 1)
                    for f in range(4):
                        for s, (t0, n) in enumerate(TOK):
                            m_ = pe.transpose(SA[f][0:n, s * P:(s + 1) * P], v[:, f, t0:t0 + n], ident[:, :])
                        m_.then_inc(vt_ready, 1)

                gemm(SB, c, 8, KT, 4, xh, xl, 0, free=None if first else after(e - 4), guard=guard, amid={2: scores})
                gemm(SB, c, 16, KT, 4, xh, xl, 0, free=after(e + 4), amid={3: values})
                pe.wait_ge(vtok_v, h + 1)
                pe.wait_ge(vtok_a, h + 1)
                pe.wait_ge(qm_ready, h + 1)
                one = ones[:, 0:1]
                pe.matmul(SA[3][:, 0:1], PS0[:, 0:P], one, start=True, stop=True)
                pe.matmul(SA[3][:, 1:2], PS0[:, P:2 * P], one, start=True, stop=False)
                pe.matmul(SA[3][:, 1:2], PS1[:, 0:P], one, start=False, stop=True)
                pe.matmul(SA[3][0:TL, 2:3], PS0[:, 2 * P:T], one, start=True, stop=False)
                pe.matmul(SA[3][0:TL, 2:3], PS1[:, P:T - P], one, start=False, stop=False)
                pe.matmul(SA[3][0:TL, 2:3], qn[:, 0, :], one, start=False, stop=False)
                pe.matmul(SA[3][0:TL, 2:3], qn[:, 1, :], one, start=False, stop=False)
                pe.matmul(SA[3][0:TL, 2:3], PS2[0:TL, :], ones[0:TL, 0:1], start=False, stop=True).then_inc(den_ready, 1)
                pe.matmul(SA[0][:, :], PS0[:, 0:P], vtok[:, 0, :], start=True, stop=True).then_inc(num_ready, 1)
                pe.matmul(SA[1][:, :], PS0[:, P:2 * P], vtok[:, 0, :], start=True, stop=False)
                pe.matmul(SA[1][:, :], PS1[:, 0:P], vtok[:, 1, :], start=False, stop=True).then_inc(num_ready, 1)
                num2 = SA[2][0:TL, :]
                pe.matmul(num2, PS0[:, 2 * P:T], vtok[:, 0, :], start=True, stop=False)
                pe.matmul(num2, PS1[:, P:T - P], vtok[:, 1, :], start=False, stop=False)
                pe.matmul(num2, PS2[0:TL, :], vtok[0:TL, 2, :], start=False, stop=False)
                for b in range(NB):
                    pe.wait_ge(c_landed[b % 4], 32 * h + 16 * (b // 4 + 1))
                    for k in range(2):
                        m_ = pe.matmul(num2, qm[:, k, b * TL:(b + 1) * TL], Cr[:, b % 4, k, :], start=False,
                                       stop=(b == NB - 1 and k == 1))
                    if b == NB - 1:
                        m_.then_inc(num_ready, 1)
                    if b == 0:
                        pe.wait_ge(vl_ready, h + 1)
                    pe.wait_ge(wkbl_ready, NB * h + b + 1)
                    if b < 2:
                        pe.wait_ge(evac, e + 12)
                    else:
                        pe.wait_ge(c_updated, NB * h + b - 1)
                    for k in range(2):
                        new, ks = SB[2 * (b % 2) + k][:, :], slice(k * P, (k + 1) * P)
                        pe.matmul(new, wkbh[0:TL, b % 2, ks], vh[0:TL, :], start=True, stop=False)
                        pe.matmul(new, wkbh[0:TL, b % 2, ks], vl[0:TL, :], start=False, stop=False)
                        m_ = pe.matmul(new, wkbl[0:TL, b % 2, ks], vh[0:TL, :], start=False, stop=True)
                    m_.then_inc(cnew_ready, 1)

                def prompt_state(k):
                    pe.wait_ge(wkp_ready, h + 1)
                    pe.wait_ge(ss_done, 3 * h + 3)
                    pe.wait_ge(hn_ready, 3 * h + k + 1)
                    for s, (t0, n) in enumerate(TOK):
                        m_ = pe.matmul(SA[k][:, :], wkp[0:n, s, k * P:(k + 1) * P], vtok[0:n, s, :],
                                       start=(s == 0), stop=(s == 2))
                    m_.then_inc(cp_ready, 1)

                prompt_state(0)
                pe.wait_ge(c_updated, NB * h + NB)
                pe.wait_ge(hn_ready, 3 * h + 3)
                for s, (t0, n) in enumerate(TOK):
                    for f in range(4):
                        m_ = pe.transpose(SB[f][:, t0:t0 + n], hn[0:n, s, f * P:(f + 1) * P], ident[0:n, 0:n])
                m_.then_inc(ht_ready, 1)
                prompt_state(1)
                pe.wait_ge(den_read, h + 1)
                for k in range(2):
                    out = SA[3][:, 16 * k:16 * k + 1 + NB]
                    pe.matmul(out, ktok[0:TL, 2, k * P:(k + 1) * P], X[0:TL, X2 + META - 1:XW:NS], start=True, stop=False)
                    pe.matmul(out[:, 0:1], ktok[:, 0, k * P:(k + 1) * P], X[:, X1 - 1:X1], start=False, stop=False)
                    m_ = pe.matmul(out[:, 0:1], ktok[:, 1, k * P:(k + 1) * P], X[:, X2 - 1:X2], start=False, stop=True)
                m_.then_inc(n_ready, 1)
                guard = {0: (cst_ready, 2 * h + 1), 1: (cst_ready, 2 * h + 2), 3: (n_read, h + 1)}
                for n in range(4):
                    gemm((SA, SB)[n % 2], c, 24 + 2 * n, 4, 4, hh, hl, 0,
                         free=after(e + 4 + 4 * n) if n >= 2 else None, guard=guard if n == 0 else None,
                         fresh=(lambda kt: pe.wait_ge(hl_ready, 4 * h + (kt + 2))) if n == 0 else None)

            def ffn(i, c, e, j, nq, nt, amid_last=None):
                first = isinstance(j, int) and j == 0
                fresh = (lambda kt: pe.wait_ge(xl_done, (1 + i) * KT + kt + 2)) if first else None
                n_q = nq * nt
                eb = 0
                k0 = 0
                for q in range(nq):
                    hj = i * HB + 2 * j + q

                    def history():
                        pe.wait_ge(evac, e + eb)
                        if first and q == 0 and i == 1:
                            pe.wait_ge(pt_read, 8)
                        wait_apart(pe, pe_passed, hb_landed[q], 16 * (j + 1 + (i * (N_PASS + 1 - q))))
                        for t in range(nt):
                            m_ = pe.transpose(SB[2][:, t * 2 * NB:(t + 1) * 2 * NB], hb[:, q, t * P:(t + 1) * P],
                                              ident[0:2 * NB, 0:2 * NB])
                        m_.then_inc(hist_mm, 1)

                    amid = {4: history}
                    if first and q == 0 and i == 1:
                        amid = {2: lambda: pool_tails(0), 5: lambda: pool_tails(1), 7: history}
                    gemm(SA, c, k0, KT, nt, xh, xl, G0[i], free=after(e + (eb - 8)), fresh=fresh if q == 0 else None,
                         guard={2: (tail_read, hj)} if q == 1 else None, amid=amid)
                    k0 += KT // 2
                    if first and q == 0:
                        pe.wait_ge(evac, e)
                        sum_squares(SB[3][:, 0:T], (1, 3)[i])
                    guard = {2: (hist_read, hj + 1)}
                    if first and q == 0:
                        guard[3] = (rt_ready, (2, 4)[i])
                    gemm(SB, c, k0, KT, nt, xh, xl, A0[i], free=after(e + (eb - 4)), guard=guard,
                         amid={4: lambda: tails(q, nt, hj + 1)})
                    k0 += KT // 2
                    eb += 2 * nt
                hj = i * HB + 2 * j + nq
                for n in range(4):
                    if n == 0:
                        free = lambda t: pe.wait_ge(evac, e + (eb - nt))
                    elif n == 1:
                        free = lambda t: pe.wait_ge(evac, e + eb)
                    else:
                        free = after(e + (eb + 4 * n - 8))
                    gemm((SA, SB)[n % 2], c, k0, n_q, 4, hh, hl, A0[i], free=free, guard={2: (tail_read, hj)} if n == 0 else None,
                         fresh=(lambda kt: pe.wait_ge(hl_ready, 4 * H + i * FT + 8 * j + min(kt + 2, n_q))) if n == 0 else None,
                         amid={1: amid_last} if n == 3 and amid_last else None)
                    k0 += (n_q + 1) // 2

            def tails(q, nt, n):
                pe.wait_ge(last_ready, n)
                for t in range(nt):
                    m_ = pe.transpose(SA[2][0:2 * NB + 2, t * P:(t + 1) * P], last[:, q, t], ident[:, :])
                m_.then_inc(tail_mm, 1)

            def pool_history():
                pe.wait_ge(evac, E_POOL - 4)
                pe.wait_ge(in_pool, 16)
                for kt in range(KT):
                    m_ = pe.transpose(SA[kt // 4][:, (kt % 4) * 120:(kt % 4) * 120 + 120], pbuf[:, kt * P:(kt + 1) * P],
                                      ident[0:120, 0:120])
                m_.then_inc(ph_mm, 1)

            def pooling():
                pe.wait_ge(evac, E_POOL)
                sum_squares(SB[3][:, 0:T], 2)
                for g in range(4):
                    guard = [{t: (ph_read, 4) for t in range(4)}, {3: (rt_ready, 3)}, None, None][g]
                    gemm((SA, SB)[g % 2], C_POOL, 2 * g, 4, 4, xh[:, 4 * g:4 * g + 4], xl[:, 4 * g:4 * g + 4], 0,
                         free=after(E_POOL + 4 * g - 8) if g >= 2 else None, guard=guard,
                         fresh=lambda kt: pe.wait_ge(pd_low, 4 * g + kt + 2))

            def pool_tails(samples):
                if samples:
                    pe.wait_ge(pt_read, 4)
                    pe.wait_ge(hrow_ready, KT)
                else:
                    pe.wait_ge(evac, E_POOL + 16)
                for kt in range(KT):
                    n, rows = (NB * PADW, hrow[:, kt]) if samples else (PADW, U[:, kt, NP:NP + PADW])
                    m_ = pe.transpose(SB[kt // 4][0:n, (kt % 4) * P:(kt % 4 + 1) * P], rows, ident[:, :])
                m_.then_inc(pt_mm, 1)

            def normalisers():
                pe.wait_ge(evac, E_END - 4)
                for k in range(2):
                    m_ = pe.transpose(SA[0][0:NB * H, k * P:(k + 1) * P], nT[:, k].rearrange("p b h -> p (b h)"), ident[:, :])
                m_.then_inc(no_mm, 1)
                for k in range(2):
                    m_ = pe.transpose(SA[1][0:H, k * P:(k + 1) * P], nP[:, k], ident[:, :])
                m_.then_inc(no_mm, 1)

            head(0, 0, 0)
            with pe.Fori(1, H) as h:
                head(h, h * C_HEAD, h * E_HEAD)
            for i, c, e in ((0, C_FFN0, E_FFN0), (1, C_FFN1, E_FFN1)):
                ffn(i, c, e, 0, 2, 4)
                with pe.Fori(1, N_PASS) as j:
                    ffn(i, c + j * C_PASS, e + j * E_PASS, j, 2, 4)
                ffn(i, c + N_PASS * C_PASS, e + N_PASS * E_PASS, N_PASS, 1, TAIL_T, (pool_history, normalisers)[i])
                if i == 0:
                    pooling()
            for q in range(4):
                if q == 2:
                    pe.wait_ge(evac, E_END)
                    pe.wait_ge(ssq_ready, 4)
                    for s in range(3):
                        n = NB * NS if s == 2 else P
                        m_ = pe.matmul(SB[3][0:n, s:s + 1], acc[:, META + s * P:META + s * P + n], ones[:, 0:1], start=True, stop=True)
                    m_.then_inc(rms_mm, 1)
                for t in range(4):
                    kt = 4 * q + t
                    pe.wait_ge(y_ready, kt + 1)
                    for s in range(3):
                        i = 3 * q + s
                        if t == 0:
                            if i in (2, 3):
                                pe.wait_ge(no_read, i - 1)
                            if 4 <= i < 8:
                                pe.wait_ge(evac, E_END)
                            if i == 7:
                                pe.wait_ge(rt_ready, 6)
                            if i >= 8:
                                pe.wait_ge(y_read[i % 2], (i - 8) // 2 + 1)
                        n = NB * NS if s == 2 else P
                        m_ = pe.transpose(YB[i % 8][0:n, t * P:(t + 1) * P], x[:, kt, META + s * P:META + s * P + n], ident[:, :])
                        if t == 3:
                            m_.then_inc(y_mm, 1)

        @block.scalar
        def _(act):
            def hi(c, k):
                s = k % SLOTS
                if isinstance(c, int) and c + k >= C_END:
                    return
                act.wait_ge(raw_landed[s], c * 8 + 32 * (k // SLOTS + 1))
                if not (isinstance(c, int) and c + k < SLOTS):
                    act.wait_ge(chunk_used, c + (k - SLOTS + 1))
                nc.scalar.activation(w_hi[:, s], w_raw[:, s], ACT.Copy).then_inc(hi_done, 1)

            def his(c, k0, k1):
                for k in range(k0, k1):
                    hi(c, k)

            def hand_over(stage, n, chunks=None, root=None):
                e = (0, E_FFN0, E_POOL, E_FFN1, E_END)[stage] - 16
                gain = (0, 2, 1, 3, 4)[stage] * KT
                for kt in range(4 * n, 4 * n + 4):
                    act.wait_ge(evac, e + kt + 1)
                    if stage in (1, 3):
                        c0 = G0[stage // 2]
                        nc.scalar.activation(xh[:, kt, c0:], x[:, kt, c0:], ACT.Copy,
                                             scale=par[:, gain + kt:gain + kt + 1]).then_inc(xh_done, 1)
                    act.wait_ge(st_squ, stage * KT + kt - 3)
                    nc.scalar.activation(sqf[:, kt % 4], x[:, kt], ACT.Square).then_inc(st_sq, 1)
                if chunks:
                    chunks()
                if root:
                    root()
                for kt in range(4 * n, 4 * n + 4):
                    g = par[:, gain + kt:gain + kt + 1]
                    if stage == 2:
                        nc.scalar.activation(U[:, kt, PADW:PADW + NP], x[:, kt, 0:NP], ACT.Copy, scale=g)
                        nc.scalar.activation(seqs(U[:, kt, PADW + NP:], PADW), seqs(x[:, kt, NP:]), ACT.Copy,
                                             scale=g).then_inc(gx_ready, 1)
                    if stage == 4:
                        act.wait_ge(st_sq, stage * KT + kt + 1)
                        nc.scalar.activation(x[:, kt, META:], x[:, kt, META:], ACT.Copy, scale=g).then_inc(y_ready, 1)

            def rms(ps, k):
                act.wait_ge(rms_mm, k)
                nc.scalar.activation(rt[:, :], ps[:, 0:T], ACT.Sqrt, bias=eps[:, :], scale=1.0 / D).then_inc(rt_ready, 1)

            def sqrt_table():
                nc.scalar.activation(warm[:, :], eps[:, :], ACT.Sqrt).then_inc(warmed, 1)

            his(0, 0, SLOTS)
            act.wait_ge(st_ev, 13)
            for kt in range(KT):
                nc.scalar.activation(xh[:, kt], x[:, kt], ACT.Copy, scale=par[:, kt:kt + 1]).then_inc(xh_done, 1)
                if kt >= 4:
                    act.wait_ge(st_squ, kt - 3)
                nc.scalar.activation(sqr[:, kt % 4], x[:, kt], ACT.Square).then_inc(st_sq, 1)
            act.wait_ge(st_squ, KT)
            nc.scalar.activation(rt[:, :], SB[1][:, 0:T], ACT.Sqrt, bias=eps[:, :], scale=1.0 / D).then_inc(rt_ready, 1)
            act.wait_ge(row_abs, 1)
            nc.scalar.activation(row[5][0:H], row[4][0:H], ACT.Exp).then_inc(row_exp, 1)
            act.wait_ge(row_exp, 1)
            nc.scalar.activation(row[6][0:H], row[5][0:H], ACT.Ln, bias=ones[0:H, 0:1]).then_inc(row_ln, 1)

            def head(h, c, e):
                first = isinstance(h, int) and h == 0
                his(c, 4, 9)
                if first:
                    act.wait_ge(gcol_a, 1)
                    nc.scalar.activation(gcol[:, :, 1], gcol[:, :, 1], ACT.Exp, scale=-1.0).then_inc(gcol_em, 1)
                act.wait_ge(mb_read, h + 1)
                nc.scalar.activation(X, X, ACT.Exp)
                nc.scalar.activation(WI, WI, ACT.Exp).then_inc(x_exp, 1)
                his(c, 9, 14)
                act.wait_ge(kt_ready, h + 1)
                for k in range(2):
                    nc.scalar.activation(ktok[:, 0:2, k * P:(k + 1) * P],
                                         SA[1 + k][:, 0:2 * P].rearrange("p (s n) -> p s n", n=P), ACT.Copy)
                    m_ = nc.scalar.activation(ktok[0:TL, 2, k * P:(k + 1) * P], SA[1 + k][0:TL, 2 * P:3 * P], ACT.Copy)
                m_.then_inc(ktok_ready, 1)
                his(c, 14, 22)
                for f in range(2):
                    act.wait_ge(vt_ready, 4 * h + f + 1)
                    nc.scalar.activation(vtok[:, 0:2, f * P:(f + 1) * P],
                                         SA[f][:, 0:2 * P].rearrange("p (s n) -> p s n", n=P), ACT.Copy)
                    m_ = nc.scalar.activation(vtok[0:TL, 2, f * P:(f + 1) * P], SA[f][0:TL, 2 * P:3 * P], ACT.Copy)
                m_.then_inc(vtok_a, 1)
                his(c, 22, 23)
                act.wait_ge(vtok_a, h + 1)
                act.wait_ge(vtok_v, h + 1)
                nc.scalar.activation(vh[0:TL, :], vtok[0:TL, 2, :], ACT.Copy).then_inc(vh_ready, 1)

                def keys_high(b0, b1):
                    for b in range(b0, b1):
                        act.wait_ge(wkb_ready, NB * h + b + 1)
                        nc.scalar.activation(wkbh[0:TL, b % 2], wkb[0:TL, b % 2], ACT.Copy).then_inc(wkbh_ready, 1)

                keys_high(0, 2)
                his(c, 23, 28)
                act.wait_ge(evac, e + 12)
                nc.scalar.activation(o, o, ACT.Sigmoid).then_inc(sig_done, 1)
                sqrt_table()
                for s, (t0, n) in enumerate(TOK):
                    if s == 2:
                        keys_high(2, NB)
                    act.wait_ge(num_ready, 3 * h + s + 1)
                    nc.scalar.activation(junk[0:n], SA[s][0:n, :], ACT.Square,
                                         accum_out=stat[0:n, 3, s:s + 1]).then_inc(ss_done, 1)
                    act.wait_ge(ss_done, 3 * h + s + 1)
                act.wait_ge(z_ready, h + 1)
                nc.scalar.activation(stat[:, 5], stat[:, 4], ACT.Sqrt, bias=eps[:, :], scale=1.0 / DV).then_inc(z_sqrt, 1)
                for k in range(2):
                    act.wait_ge(cp_ready, 2 * h + k + 1)
                    if not first:
                        act.wait_ge(cst_stored, 16 * h)
                    nc.scalar.activation(Cst[:, k], SA[k][:, :], ACT.Copy).then_inc(cst_ready, 1)
                    if k == 0:
                        for f in range(4):
                            act.wait_ge(hf_ready, 4 * h + f + 1)
                            nc.scalar.activation(hh[:, f], hf[:, f], ACT.Copy).then_inc(hh_ready, 1)
                act.wait_ge(cst_ready, 2 * h + 2)
                act.dma_start(O["C_prompt"][0, 0].rearrange("h (k p) v -> p (h k) v", p=P)[:, bass.ds(2 * h, 2), :],
                              Cst).then_inc(cst_stored, 16)
                for n in range(4):
                    his(c, 28 + 2 * n, 30 + 2 * n)
                    if isinstance(h, int) and h == H - 1:
                        hand_over(1, n)

            def ffn(i, c, e, j, nq, nt):
                first = isinstance(j, int) and j == 0
                a0 = A0[i]
                eb = k0 = 0
                for q in range(nq):
                    hj = i * HB + 2 * j + q
                    pooled = i == 1 and first and q == 0
                    if pooled:
                        his(c, 4, 6)
                        act.wait_ge(pt_mm, 1)
                        act.wait_ge(hrow_ready, KT)
                        for n in range(4):
                            nc.scalar.activation(pstp[:, n * 512:(n + 1) * 512], SB[n][0:PADW, :], ACT.Copy).then_inc(pt_read, 1)
                        his(c, 6, 9)
                        act.wait_ge(pt_mm, 2)
                        for n in range(4):
                            nc.scalar.activation(psto[:, n * 512:(n + 1) * 512], SB[n][0:NB * PADW, :],
                                                 ACT.Copy).then_inc(pt_read, 1)
                        act.wait_ge(pt_read, 8)
                        act.dma_start(O["pool_prompt"][0, 0], pstp).then_inc(pool_stored, 16)
                        act.dma_start(O["pool_sample"][0].rearrange("b r d -> (b r) d"), psto).then_inc(pool_stored, 16)
                        his(c, 9, 11)
                    else:
                        his(c, k0 + 4, k0 + 8)
                    act.wait_ge(hist_mm, hj + 1)
                    if not (i == 0 and first and q == 0):
                        act.wait_ge(last_ready, hj)
                        act.wait_ge(taps_ready, i * FT + 8 * j + 4 * q)
                    else:
                        act.wait_ge(e_zero, 1)
                    nc.scalar.activation(E[:, 0:nt, 2 + NP:].rearrange("p f (b s) -> p f b s", s=NS + 2)[:, :, :, 0:2],
                                         SB[2][:, 0:nt * 2 * NB].rearrange("p (f b s) -> p f b s", b=NB, s=2),
                                         ACT.Copy).then_inc(hist_read, 1)
                    his(c, k0 + (11 if pooled else 8), k0 + 12)
                    if first and q == 0:
                        rms(SB[3], (1, 3)[i])
                    for t in range(nt):
                        act.wait_ge(evac, e + (eb + t + 1))
                        nc.scalar.activation(Tt[:, t, a0:GW - 2], E[:, t, a0 + 2:GW], ACT.Identity,
                                             bias=cp[:, 3, 4 * q + t:4 * q + t + 1],
                                             scale=cp[:, 2, 4 * q + t:4 * q + t + 1]).then_inc(tap0_ready, 1)
                    for t in range(nt):
                        act.wait_ge(taps_ready, i * FT + 8 * j + (4 * q + t + 1))
                        nc.scalar.activation(Tt[:, t, a0:GW - 2], Tt[:, t, a0:GW - 2], ACT.Silu).then_inc(silu_ready, 1)
                    his(c, k0 + 12, k0 + 16)
                    tails(i, j, q, nt, hj + 1)
                    his(c, k0 + 16, k0 + 19)
                    for t in range(nt):
                        act.wait_ge(evac, e + (eb + nt + t + 1))
                        nc.scalar.activation(hh[:, 4 * q + t, a0:], fh[:, t, a0:], ACT.Copy).then_inc(hh_ready, 1)
                    hi(c, k0 + 19)
                    k0 += KT
                    eb += 2 * nt
                nd = (nq * nt + 1) // 2
                if nt < 4:
                    if i == 0:
                        act.wait_ge(u_pads, 1)
                    for n in range(4):
                        if i == 0 and n == 3:
                            def root():
                                sqrt_table()
                                rms(SB[3], 2)
                            hand_over(2, n, lambda: his(c, k0 + 4 + n * nd, k0 + 4 + (n + 1) * nd), root)
                            continue
                        his(c, k0 + 4 + n * nd, k0 + 4 + (n + 1) * nd)
                        hand_over((2, 4)[i], n)
                        if i == 1 and n == 2:
                            act.wait_ge(no_mm, 2)
                            nc.scalar.activation(nsto, SA[0][0:NB * H, 0:DK], ACT.Copy).then_inc(no_read, 1)
                            nc.scalar.activation(npst, SA[1][0:H, 0:DK], ACT.Copy).then_inc(no_read, 1)
                else:
                    his(c, k0 + 4, k0 + 4 + 4 * nd)

            def tails(i, j, q, nt, n):
                act.wait_ge(tail_mm, n)
                if not (i == 0 and isinstance(j, int) and j == 0):
                    act.wait_ge(tail_stored[q], 32 * (j + i * (N_PASS + 1 - q)))
                nc.scalar.activation(tst[:, q, 0:nt * P], SA[2][0:2 * NB + 2, 0:nt * P], ACT.Copy).then_inc(tail_read, 1)
                act.wait_ge(tail_read, n)
                cols = bass.ds((j * 8 + 4 * q) * P, nt * P)
                act.dma_start(O["conv_prompt"][i, 0][:, cols], tst[0:2, q, 0:nt * P]).then_inc(tail_stored[q], 16)
                act.dma_start(O["conv_sample"][i].rearrange("b r f -> (b r) f")[:, cols],
                              tst[2:2 * NB + 2, q, 0:nt * P]).then_inc(tail_stored[q], 16)

            def pooling():
                act.wait_ge(ph_mm, 1)
                for g in range(4):
                    nc.scalar.activation(
                        U[:, 4 * g:4 * g + 4, PADW + NP:].rearrange("p f (b s) -> p f b s", s=SEQW)[:, :, :, 0:PADW],
                        SA[g][:, 0:480].rearrange("p (f b s) -> p f b s", f=4, b=NB), ACT.Copy).then_inc(ph_read, 1)
                for g in range(4):
                    for t in range(4):
                        act.wait_ge(pd_ready, 2 * g + t // 2 + 1)
                        nc.scalar.activation(xh[:, 4 * g + t], PD[:, t], ACT.Copy).then_inc(xh_done, 1)
                    if g:
                        his(C_POOL, 2 + 2 * g, 4 + 2 * g)
                for n in range(4):
                    if n == 2:
                        his(C_POOL, 10, 12)
                    hand_over(3, n)

            head(0, 0, 0)
            with act.Fori(1, H - 1) as h:
                head(h, h * C_HEAD, h * E_HEAD)
            head(H - 1, (H - 1) * C_HEAD, (H - 1) * E_HEAD)
            for i, c, e in ((0, C_FFN0, E_FFN0), (1, C_FFN1, E_FFN1)):
                ffn(i, c, e, 0, 2, 4)
                with act.Fori(1, N_PASS) as j:
                    ffn(i, c + j * C_PASS, e + j * E_PASS, j, 2, 4)
                ffn(i, c + N_PASS * C_PASS, e + N_PASS * E_PASS, N_PASS, 1, TAIL_T)
                if i == 0:
                    pooling()
            sqrt_table()
            act.wait_ge(rms_mm, 4)
            nc.scalar.activation(stat[:, 5, 0:2], SB[3][:, 0:2], ACT.Sqrt, bias=eps[:, :], scale=1.0 / D).then_inc(rt_ready, 1)
            nc.scalar.activation(stat[0:64, 5, 2:3], SB[3][0:64, 2:3], ACT.Sqrt, bias=eps[0:64, :], scale=1.0 / D).then_inc(rt_ready, 1)
            act.wait_ge(pool_stored, 32)
            act.wait_ge(r_ready, 5)
            for i in range(0, 12, 2):
                s, q = i % 3, i // 3
                n = NB * NS if s == 2 else P
                act.wait_ge(y_mm, i + 1)
                nc.scalar.activation(ytok[0:n, s, q * 512:(q + 1) * 512], YB[i % 8][0:n, :], ACT.Copy,
                                     scale=stat[0:n, 6, s:s + 1]).then_inc(y_read[0], 1)

        @block.vector
        def _(dve):
            step = Chain(dve, dve_step)
            V = nc.vector

            def lo(c, k):
                s = k % SLOTS
                if isinstance(c, int) and c + k >= C_END:
                    return
                dve.wait_ge(hi_done, c + (k + 1))
                V.tensor_tensor(w_lo[:, s], w_raw[:, s], w_hi[:, s].bitcast(F32), ALU.subtract).then_inc(lo_done, 1)

            def los(c, k0, k1):
                for k in range(k0, k1):
                    lo(c, k)

            def x_low(stage, gain, c0, k0, k1):
                for kt in range(k0, k1):
                    dve.wait_ge(xh_done, stage * KT + kt + 1)
                    V.scalar_tensor_tensor(xl[:, kt, c0:], x[:, kt, c0:], par[:, gain * KT + kt:gain * KT + kt + 1],
                                           xh[:, kt, c0:].bitcast(F32), ALU.mult, ALU.subtract).then_inc(xl_done, 1)

            def inv_rms(k):
                dve.wait_ge(rt_ready, k)
                V.reciprocal(rbc[:, :], rt[:, :]).then_inc(r_ready, 1)
                dve.wait_ge(r_ready, k)

            def add_to_x(banks, n, c0):
                for t in range(4):
                    V.tensor_tensor(x[:, 4 * n + t, c0:], banks[t][:, c0:T], x[:, 4 * n + t, c0:], ALU.add).then_inc(evac, 1)

            for s, (t0, n) in enumerate(TOK):
                for q in range(4):
                    dve.wait_ge(st_tr, 4 * s + q + 1)
                    V.tensor_copy(x[:, 4 * q:4 * q + 4, t0:t0 + n],
                                  bank[(4 * s + q) % 8][:, :].rearrange("p (f t) -> p f t", t=P)[:, :, 0:n]).then_inc(st_ev, 1)
            dve.wait_ge(st_tr, 13)
            V.tensor_copy(par[:, :], SB[0][:, 0:7 * KT]).then_inc(st_ev, 1)
            for i in range(2):
                dve.wait_ge(st_tr, 14 + i)
                V.tensor_copy(cpar[:, i].rearrange("p a f -> p (a f)"), SB[1 + i][:, 0:4 * FT]).then_inc(st_ev, 1)
            dve.wait_ge(st_tr, 16)
            V.tensor_copy(nT[:, :, :, :].rearrange("p k b h -> p (k b h)"), SB[3][:, 0:64]).then_inc(st_ev, 1)
            dve.wait_ge(in_gate, 16 * 5)
            dve.wait_ge(consts, 2)
            dve.wait_ge(st_ev, 13)
            gain = par[:, 0:KT].unsqueeze(2).to_broadcast([P, KT, 4])
            V.tensor_tensor(wgg[:, :, 0:4], wgr[:, :, 0:4], gain, ALU.mult)
            V.tensor_tensor(wgg[:, :, 32:36], wgr[:, :, 4:8], gain, ALU.mult).then_inc(wgg_ready, 1)
            los(0, 0, SLOTS)
            x_low(0, 0, 0, 0, KT)
            inv_rms(1)
            dve.wait_ge(gates_mm, 1)
            h4 = slice(0, H)
            step(V.tensor_tensor(row[0], SB[0][0:36, 0:T], rbc[0:36, :], ALU.mult))
            V.tensor_scalar(row[1][h4], row[0][h4], bg[0:H, :], None, ALU.add)
            step(V.tensor_scalar(row[2][h4], row[0][32:36], bg[32:36, :], None, ALU.add))
            V.scalar_tensor_tensor(row[4][h4], row[2][h4], -1.0, row[2][h4], ALU.mult, ALU.min).then_inc(row_abs, 1)
            dve.wait_ge(row_ln, 1)
            step(V.scalar_tensor_tensor(row[3][h4], row[2][h4], 0.0, row[6][h4], ALU.min, ALU.subtract))
            step(V.tensor_tensor_scan(row[7][h4], row[9][h4], row[3][h4], 0.0, ALU.mult, ALU.add))
            step(V.tensor_tensor(row[8][h4], row[1][h4], row[7][h4], ALU.subtract))
            step(V.tensor_copy(row[4][h4], row[8][h4]))
            V.tensor_scalar(row[4][h4, 0:1], row[8][h4, 0:1], 0.0, None, ALU.max)
            step(V.tensor_tensor(row[4][h4, NP:T:NS], row[8][h4, NP:T:NS], row[11][h4, 0:NB], ALU.max))
            step(V.tensor_tensor_scan(mrow[:, :], row[10][h4], row[4][h4], 0.0, ALU.add, ALU.max))
            V.tensor_tensor(mtrow[:, :], row[7][h4], mrow[:, :], ALU.add).then_inc(rows_ready, 1)

            def head(h, c, e):
                first = isinstance(h, int) and h == 0
                if not first:
                    dve.wait_ge(mb_ready, h)
                V.tensor_scalar(mm[:, :], mrow[:, :], negeye[:, bass.ds(h, 1)], None, ALU.mult).then_inc(mrow_ready, 1)
                los(c, 4, 9)
                if first:
                    dve.wait_ge(gcol_mm, 1)
                    V.tensor_copy(gcol[:, 0:2].rearrange("p s a h -> p (s a h)"), SB[2][:, 0:16])
                    V.tensor_copy(gcol[0:TL, 2].rearrange("p a h -> p (a h)"), SB[2][0:TL, 16:24]).then_inc(gcol_a, 1)
                    dve.wait_ge(gcol_em, 1)
                V.tensor_copy(hcol[:, :, :].unsqueeze(3), gcol[:, :, :, bass.ds(h, 1)])
                V.tensor_copy(mbh[:, :].unsqueeze(2), mb[:, :, bass.ds(h, 1)])
                V.tensor_copy(nh[:, :, :].unsqueeze(3), nT[:, :, :, bass.ds(h, 1)])
                step(V.tensor_copy(gh[:, :], par[:, bass.ds(5 * KT + 4 * h, 4)]))
                dve.wait_ge(mb_ready, h + 1)
                nM = SB[3]
                V.tensor_scalar(X[:, X0:X1], nM[:, 0:NP], hcol[:, 0, 0:1], 0.0, ALU.add, ALU.min)
                V.tensor_scalar(X[:, X1:X2], nM[:, P:NP], hcol[:, 1, 0:1], 0.0, ALU.add, ALU.min)
                V.tensor_scalar(X[0:TL, X2:XW], nM[0:TL, 2 * P:T], hcol[0:TL, 2, 0:1], 0.0, ALU.add, ALU.min)
                V.tensor_tensor(seqs(WI), seqs(nM[:, NP:T]), mbh[:, :].unsqueeze(2).to_broadcast([P, NB, NS]),
                                ALU.add).then_inc(mb_read, 1)
                los(c, 9, 11)
                dve.wait_ge(chunk_used, c + 8)
                for t in range(2):
                    V.scalar_tensor_tensor(qk[:, t], SA[t][:, 0:T], DK ** -0.5, rbc[:, :], ALU.mult, ALU.mult).then_inc(evac, 1)
                for t in range(2, 4):
                    V.tensor_tensor(qk[:, t], SA[t][:, 0:T], rbc[:, :], ALU.mult).then_inc(evac, 1)
                lo(c, 11)
                dve.wait_ge(x_exp, h + 1)
                V.tensor_tensor(X, X, mask[:, :], ALU.mult).then_inc(pm_ready, 1)
                dve.wait_ge(evac, e + 2)
                for k in range(2):
                    step.mark(V.tensor_tensor(qmb(k), seqs(qk[:, k, NP:T]), seqs(WI), ALU.mult))
                step.sync()
                for k in range(2):
                    m_ = V.tensor_tensor(seqs(qn[:, k, META:TL]), qmb(k), nh[:, k, :].unsqueeze(2).to_broadcast([P, NB, NS]),
                                         ALU.mult)
                m_.then_inc(qm_ready, 1)
                los(c, 12, 14)
                dve.wait_ge(s_ready, h + 1)
                dve.wait_ge(pm_ready, h + 1)
                V.tensor_tensor(PS0[:, 0:NP], SA[0][:, X0:X1], X[:, X0:X1], ALU.mult)
                V.tensor_tensor(PS1[:, 0:NP - P], SA[0][:, X1:X2], X[:, X1:X2], ALU.mult)
                V.tensor_tensor(PS2[0:TL, :], SA[0][0:TL, X2:XW], X[0:TL, X2:XW], ALU.mult).then_inc(ps_ready, 1)
                los(c, 14, 19)
                dve.wait_ge(chunk_used, c + 16)
                for t in range(4):
                    V.tensor_tensor(v[:, t], SB[t][:, 0:T], rbc[:, :], ALU.mult).then_inc(evac, 1)
                los(c, 19, 22)
                for f in range(2, 4):
                    dve.wait_ge(vt_ready, 4 * h + f + 1)
                    V.tensor_copy(vtok[:, 0:2, f * P:(f + 1) * P], SA[f][:, 0:2 * P].rearrange("p (s n) -> p s n", n=P))
                    m_ = V.tensor_copy(vtok[0:TL, 2, f * P:(f + 1) * P], SA[f][0:TL, 2 * P:3 * P])
                m_.then_inc(vtok_v, 1)
                los(c, 22, 24)
                dve.wait_ge(vh_ready, h + 1)
                V.tensor_tensor(vl[0:TL, :], vtok[0:TL, 2, :], vh[0:TL, :].bitcast(F32), ALU.subtract).then_inc(vl_ready, 1)
                los(c, 24, 27)
                dve.wait_ge(chunk_used, c + 24)
                for t in range(4):
                    V.tensor_tensor(o[:, t], SB[t][:, 0:T], rbc[:, :], ALU.mult).then_inc(evac, 1)
                lo(c, 27)
                dve.wait_ge(den_ready, h + 1)
                V.tensor_copy(stat[:, 0, 0:2], SA[3][:, 0:2])
                V.tensor_copy(stat[0:TL, 0, 2:3], SA[3][0:TL, 2:3]).then_inc(den_read, 1)
                dve.wait_ge(den_read, h + 1)
                step(V.scalar_tensor_tensor(stat[:, 1], stat[:, 0], -1.0, stat[:, 0], ALU.mult, ALU.max))
                step(V.tensor_tensor(stat[:, 1], stat[:, 1], hcol[:, :, 1], ALU.max))
                step(V.reciprocal(stat[:, 2], stat[:, 1]))
                step(V.tensor_tensor(stat[:, 1], stat[:, 2], stat[:, 2], ALU.mult))

                def new_states(b0, b1):
                    for b in range(b0, b1):
                        dve.wait_ge(cnew_ready, NB * h + b + 1)
                        for k in range(2):
                            m_ = V.scalar_tensor_tensor(Cr[:, b % 4, k], Cr[:, b % 4, k], WI[:, NS * b + NS - 1:NS * b + NS],
                                                        SB[2 * (b % 2) + k][:, :], ALU.mult, ALU.add)
                        m_.then_inc(c_updated, 1)

                new_states(0, NB - 1)
                dve.wait_ge(ss_done, 3 * h + 3)
                V.tensor_tensor(stat[:, 4], stat[:, 1], stat[:, 3], ALU.mult).then_inc(z_ready, 1)
                dve.wait_ge(z_sqrt, h + 1)
                step(V.reciprocal(stat[:, 6], stat[:, 5]))
                step(V.tensor_tensor(stat[:, 7], stat[:, 6], stat[:, 2], ALU.mult))
                for s, (t0, n) in enumerate(TOK):
                    V.tensor_scalar(hn[0:n, s], SA[s][0:n, :], stat[0:n, 7, s:s + 1], None, ALU.mult).then_inc(hn_ready, 1)
                new_states(NB - 1, NB)
                dve.wait_ge(ht_ready, h + 1)
                dve.wait_ge(sig_done, h + 1)
                for f in range(4):
                    V.scalar_tensor_tensor(hf[:, f], SB[f][:, 0:T], gh[:, f:f + 1], o[:, f], ALU.mult, ALU.mult).then_inc(hf_ready, 1)
                for f in range(4):
                    dve.wait_ge(hh_ready, 4 * h + f + 1)
                    V.tensor_tensor(hl[:, f], hf[:, f], hh[:, f].bitcast(F32), ALU.subtract).then_inc(hl_ready, 1)
                dve.wait_ge(n_ready, h + 1)
                for k in range(2):
                    step.mark(V.tensor_tensor(nt2[:, k], nh[:, k], WI[:, NS - 1::NS], ALU.mult))
                step.sync()
                for k in range(2):
                    V.tensor_tensor(nT[:, k, :, bass.ds(h, 1)], nt2[:, k].unsqueeze(2), SA[3][:, 16 * k + 1:16 * k + 9].unsqueeze(2),
                                    ALU.add)
                    m_ = V.tensor_copy(nP[:, k, bass.ds(h, 1)], SA[3][:, 16 * k:16 * k + 1])
                m_.then_inc(n_read, 1)
                for n in range(4):
                    los(c, 28 + 2 * n, 30 + 2 * n)
                    dve.wait_ge(chunk_used, c + (26 + 2 * n))
                    add_to_x((SA, SB)[n % 2], n, 0)
                    if isinstance(h, int) and h == H - 1:
                        x_low(1, 2, G0[0], 4 * n, 4 * n + 4)

            def qmb(k):
                return qm[:, k].rearrange("p (b s) -> p b s", s=TL + NS)[:, :, META:META + NS]

            def ffn(i, c, e, j, nq, nt):
                first = isinstance(j, int) and j == 0
                a0, g0 = A0[i], G0[i]
                eb = k0 = 0
                V.tensor_copy(cp[:, :, 0:nq * nt], cpar[:, i, :, bass.ds(8 * j, nq * nt)])
                for q in range(nq):
                    los(c, k0 + 4, k0 + 11)
                    if first and q == 0:
                        inv_rms((2, 4)[i])
                    dve.wait_ge(chunk_used, c + (k0 + 8))
                    if not (i == 0 and first and q == 0):
                        dve.wait_ge(last_ready, i * HB + 2 * j + q)
                    if i == 1 and first and q == 0:
                        dve.wait_ge(pt_mm, 2)
                    for t in range(nt):
                        V.tensor_tensor(E[:, t, 2 + g0:2 + NP], SA[t][:, g0:NP], rbc[:, g0:NP], ALU.mult)
                        V.tensor_tensor(seqs(E[:, t, 2 + NP:], 2), seqs(SA[t][:, NP:T]), seqs(rbc[:, NP:T]), ALU.mult).then_inc(evac, 1)
                    lo(c, k0 + 11)
                    dve.wait_ge(hist_read, i * HB + 2 * j + q + 1)
                    for t in range(nt):
                        f = 4 * q + t
                        dve.wait_ge(tap0_ready, i * FT + 8 * j + (f + 1))
                        step(V.scalar_tensor_tensor(Tt[:, t, a0:GW - 2], E[:, t, a0 + 1:GW - 1], cp[:, 1, f:f + 1],
                                                    Tt[:, t, a0:GW - 2], ALU.mult, ALU.add))
                        V.scalar_tensor_tensor(Tt[:, t, a0:GW - 2], E[:, t, a0:GW - 2], cp[:, 0, f:f + 1],
                                               Tt[:, t, a0:GW - 2], ALU.mult, ALU.add).then_inc(taps_ready, 1)
                    for t in range(nt):
                        dve.wait_ge(silu_ready, i * FT + 8 * j + (4 * q + t + 1))
                        V.tensor_tensor(Sp[:, t, a0:NP], Tt[:, t, a0:NP], rbc[:, a0:NP], ALU.mult)
                        m_ = V.tensor_tensor(seqs(Sp[:, t, NP:T]),
                                             Tt[:, t, 2 + NP:].rearrange("p (b s) -> p b s", s=NS + 2)[:, :, 0:NS],
                                             seqs(rbc[:, NP:T]), ALU.mult)
                        step.mark(m_)
                    los(c, k0 + 12, k0 + 19)
                    dve.wait_ge(chunk_used, c + (k0 + 16))
                    step.sync()
                    for t in range(nt):
                        V.tensor_tensor(fh[:, t, a0:], SB[t][:, a0:T], Sp[:, t, a0:], ALU.mult).then_inc(evac, 1)
                    for t in range(nt):
                        dve.wait_ge(hh_ready, 4 * H + i * FT + 8 * j + (4 * q + t + 1))
                        V.tensor_tensor(hl[:, 4 * q + t, a0:], fh[:, t, a0:], hh[:, 4 * q + t, a0:].bitcast(F32),
                                        ALU.subtract).then_inc(hl_ready, 1)
                    lo(c, k0 + 19)
                    k0 += KT
                    eb += 2 * nt
                nd = (nq * nt + 1) // 2
                for n in range(4):
                    early = nd - 1 if nt == 4 else 0
                    los(c, k0 + 4, k0 + 4 + early)
                    dve.wait_ge(chunk_used, c + (k0 + nd))
                    add_to_x((SA, SB)[n % 2], n, a0)
                    los(c, k0 + 4 + early, k0 + 4 + nd)
                    k0 += nd

            def pooling():
                inv_rms(3)

                def out(g):
                    los(C_POOL, 4 + 2 * g, 6 + 2 * g)
                    dve.wait_ge(chunk_used, C_POOL + 2 * g + 2)
                    for t in range(4):
                        f = 4 * g + t
                        V.scalar_tensor_tensor(x[:, f], (SA, SB)[g % 2][t][:, 0:T], par[:, 6 * KT + f:6 * KT + f + 1], x[:, f],
                                               ALU.mult, ALU.add).then_inc(evac, 1)

                def prompt(ap):
                    return ap[:, :, PADW:PADW + NP]

                def samples(ap):
                    return ap[:, :, PADW + NP:].rearrange("p f (b s) -> p f b s", s=SEQW)[:, :, :, PADW:]

                dve.wait_ge(tail_stored[0], 32 * (N_PASS + 1))
                dve.wait_ge(tail_stored[1], 32 * N_PASS)
                for p in range(KT // 2):
                    g = p // 2
                    w = 2 << g
                    u = U[:, 2 * p:2 * p + 2]
                    pd = PD[:, p % 2 * 2:p % 2 * 2 + 2]
                    if p == 0:
                        dve.wait_ge(gx_ready, 2)
                        step.mark(V.tensor_tensor(prompt(u), prompt(u), rbc[:, 0:NP].unsqueeze(1).to_broadcast([P, 2, NP]),
                                                  ALU.mult))
                        step(V.tensor_tensor(samples(u), samples(u),
                                             seqs(rbc[:, NP:]).unsqueeze(1).to_broadcast([P, 2, NB, NS]), ALU.mult))
                    else:
                        dve.wait_ge(u_ready, p)
                    dve.wait_ge(ph_read, g + 1)
                    src, n, at = u, 1, 0
                    while n < w:
                        at += n
                        to = (Wa, Wb)[n in (2, 8)]
                        step(V.tensor_tensor(to[:, :, at:], src[:, :, at:], src[:, :, at - n:UW - n], ALU.add))
                        src, n = to, 2 * n
                    if p >= 2:
                        dve.wait_ge(pd_low, 2 * p - 2)
                    step.mark(V.scalar_tensor_tensor(pd[:, :, 0:NP], prompt(src), 1.0 / w, prompt(u), ALU.mult, ALU.subtract))
                    for t in range(2):
                        V.scalar_tensor_tensor(seqs(pd[:, t, NP:]), seqs(src[:, t, PADW + NP:], PADW), 1.0 / w,
                                               seqs(u[:, t, PADW + NP:], PADW), ALU.mult, ALU.subtract)
                    step.sync()
                    few = pd[:, :, 0:w - 1]
                    step(V.tensor_tensor(few, prompt(src)[:, :, 0:w - 1], rc[:, 0:w - 1].unsqueeze(1).to_broadcast([P, 2, w - 1]),
                                         ALU.mult))
                    V.tensor_tensor(few, few, prompt(u)[:, :, 0:w - 1], ALU.subtract).then_inc(pd_ready, 1)
                    if g and p % 2:
                        out(g - 1)
                x_low(3, 3, G0[1], 0, KT // 2)
                out(3)
                x_low(3, 3, G0[1], KT // 2, KT)

            step.base, step.n, before = 0, step.n, step.n
            head(0, 0, 0)
            per, step.n = step.n - before, before
            with dve.Fori(1, H - 1) as h:
                step.base = h * per
                head(h, h * C_HEAD, h * E_HEAD)
            step.base, step.n = (H - 1) * per, before
            head(H - 1, (H - 1) * C_HEAD, (H - 1) * E_HEAD)
            dve.wait_ge(hl_ready, 4 * H)
            V.memset(E[:, :, 0:2], 0.0).then_inc(e_zero, 1)
            for i, c, e in ((0, C_FFN0, E_FFN0), (1, C_FFN1, E_FFN1)):
                before, base = step.n, step.base
                ffn(i, c, e, 0, 2, 4)
                per, step.n = step.n - before, before
                with dve.Fori(1, N_PASS) as j:
                    step.base = j * per + base
                    ffn(i, c + j * C_PASS, e + j * E_PASS, j, 2, 4)
                step.base = (N_PASS - 1) * per + base
                ffn(i, c + N_PASS * C_PASS, e + N_PASS * E_PASS, N_PASS, 1, TAIL_T)
                if i == 0:
                    pooling()
            dve.wait_ge(rt_ready, 6)
            V.reciprocal(stat[:, 6], stat[:, 5]).then_inc(r_ready, 1)
            dve.wait_ge(pool_stored, 32)
            dve.wait_ge(r_ready, 5)
            for i in range(1, 12, 2):
                s, q = i % 3, i // 3
                n = NB * NS if s == 2 else P
                dve.wait_ge(y_mm, i + 1)
                V.tensor_scalar(ytok[0:n, s, q * 512:(q + 1) * 512], YB[i % 8][0:n, :], stat[0:n, 6, s:s + 1], None,
                                ALU.mult).then_inc(y_read[1], 1)

        @block.gpsimd
        def _(pool):
            step = Chain(pool, pool_step)
            G = nc.gpsimd
            G.memset(ones[:, :], 1.0)
            step(G.memset(ident[:, :], 0.0))
            G.affine_select(out=ident[:, :], in_=ident[:, :], compare_op=ALU.not_equal, fill=1.0, base=0,
                            pattern=[[-1, P]], channel_multiplier=1).then_inc(consts, 1)
            G.memset(eps[:, :], EPS)
            G.memset(stat[:, :, :], 1.0)
            G.memset(gcol[:, :, :, :], 0.0)
            G.memset(row[9][0:H], 1.0)
            G.memset(row[10][0:H], 0.0)
            G.memset(negeye[:, :], 0.0)
            for t in range(16):
                G.memset(rc[:, t:t + 1], 1.0 / (t + 1))
            step(G.memset(wgg, 0.0))
            for s, value in ((9, 0.0), (10, BIG)):
                G.memset(row[s][0:H, 0:1], value)
                G.memset(row[s][0:H, NP:T:NS], value)
            step(G.affine_select(out=negeye[:, :], in_=negeye[:, :], compare_op=ALU.not_equal, fill=-1.0, base=0,
                                 pattern=[[-1, H]], channel_multiplier=1))
            step(G.memset(mask[:, :], 1.0))
            for x0, x1 in ((X0, X1), (X1, X2)):
                G.affine_select(out=mask[:, x0:x1], in_=mask[:, x0:x1], compare_op=ALU.is_ge, fill=0.0, base=0,
                                pattern=[[1, x1 - x0]], channel_multiplier=-1)
            step(G.affine_select(out=mask[:, X2:XW], in_=mask[:, X2:XW], compare_op=ALU.is_ge, fill=0.0, base=0,
                                 pattern=[[1, TL]], channel_multiplier=-1))
            own = mask[:, X2 + META:XW].rearrange("p (b s) -> p b s", s=NS)
            G.affine_select(out=own, in_=own, compare_op=ALU.is_ge, fill=0.0, base=-META,
                            pattern=[[-NS, NB], [0, NS]], channel_multiplier=1)
            pool.wait_ge(st_tr, 16)
            G.memset(area[:, 6528:9216], 0.0).then_inc(consts, 1)

            def sum_of_squares(k):
                if k > 1:
                    pool.wait_ge(rms_mm, k - 1)
                for kt in range(KT):
                    pool.wait_ge(st_sq, k * KT + kt + 1)
                    if kt:
                        pool.wait_ge(st_squ, k * KT + kt)
                        m_ = G.tensor_tensor(acc[:, :], acc[:, :], sqf[:, kt % 4], ALU.add)
                    else:
                        m_ = G.tensor_copy(acc[:, :], sqf[:, 0])
                    m_.then_inc(st_squ, 1)
                pool.wait_ge(st_squ, k * KT + KT)
                pool.sem_inc(ssq_ready, 1)

            def head(h):
                first = isinstance(h, int)
                pool.wait_ge(pm_ready, h + 1)
                pool.wait_ge(ktok_ready, h + 1)
                for b in range(NB):
                    if not (first and b < 2):
                        wait_apart(pool, pool_passed, cnew_ready, NB * h + b - 1)
                    col = X2 + META + NS * b + NS - 1
                    G.tensor_scalar(wkb[0:TL, b % 2], ktok[0:TL, 2], X[0:TL, col:col + 1], None, ALU.mult).then_inc(wkb_ready, 1)
                    wait_apart(pool, pool_passed, wkbh_ready, NB * h + b + 1)
                    G.tensor_tensor(wkbl[0:TL, b % 2], wkb[0:TL, b % 2], wkbh[0:TL, b % 2].bitcast(F32),
                                    ALU.subtract).then_inc(wkbl_ready, 1)
                    if b == 1:
                        G.tensor_scalar(wkp[:, 0], ktok[:, 0], X[:, X1 - 1:X1], None, ALU.mult)
                        G.tensor_scalar(wkp[:, 1], ktok[:, 1], X[:, X2 - 1:X2], None, ALU.mult)
                        G.tensor_scalar(wkp[0:TL, 2], ktok[0:TL, 2], X[0:TL, X2 + META - 1:X2 + META], None,
                                        ALU.mult).then_inc(wkp_ready, 1)

            head(0)
            with pool.Fori(1, H) as h:
                head(h)

            def last_rows(i, e, j, nq, nt):
                for q in range(nq):
                    n = i * HB + 2 * j + q
                    if not (isinstance(j, int) and j == 0):
                        pool.wait_ge(tail_mm, n - 1)
                    elif i:
                        pool.wait_ge(tail_mm, HB)
                    for t in range(nt):
                        wait_apart(pool, pool_passed, evac, e + (2 * nt * q + t + 1))
                        m_ = G.tensor_copy(last[:, q, t].rearrange("p (b s) -> p b s", s=2),
                                           E[:, t, NP - NS:].rearrange("p (b s) -> p b s", s=NS + 2)[:, :, NS:])
                    m_.then_inc(last_ready, 1)

            sum_of_squares(1)
            for b in range(4):
                pool.wait_ge(c_stored[b], 2 * H * 16)
            pool.wait_ge(cst_stored, 16 * H)
            G.memset(U[:, :, 0:PADW], 0.0).then_inc(u_pads, 1)
            for i, e in ((0, E_FFN0), (1, E_FFN1)):
                last_rows(i, e, 0, 2, 4)
                with pool.Fori(1, N_PASS) as j:
                    last_rows(i, e + j * E_PASS, j, 2, 4)
                last_rows(i, e + N_PASS * E_PASS, N_PASS, 1, TAIL_T)
                if i == 0:
                    sum_of_squares(2)
                    pool.wait_ge(r_ready, 3)

                    def times_r(p):
                        u = U[:, 2 * p:2 * p + 2]
                        pool.wait_ge(gx_ready, 2 * p + 2)
                        G.tensor_tensor(u[:, :, PADW:PADW + NP], u[:, :, PADW:PADW + NP],
                                        rbc[:, 0:NP].unsqueeze(1).to_broadcast([P, 2, NP]), ALU.mult)
                        own = u[:, :, PADW + NP:].rearrange("p f (b s) -> p f b s", s=SEQW)[:, :, :, PADW:]
                        G.tensor_tensor(own, own, seqs(rbc[:, NP:]).unsqueeze(1).to_broadcast([P, 2, NB, NS]),
                                        ALU.mult).then_inc(u_ready, 1)

                    times_r(1)
                    for p in range(KT // 2):
                        if p + 2 < KT // 2:
                            times_r(p + 2)
                        for kt in range(2 * p, 2 * p + 2):
                            pool.wait_ge(xh_done, 2 * KT + kt + 1)
                            G.tensor_tensor(xl[:, kt], PD[:, kt % 4], xh[:, kt].bitcast(F32), ALU.subtract).then_inc(pd_low, 1)
                        G.tensor_copy(hrow[:, 2 * p:2 * p + 2].rearrange("p f (b s) -> p f b s", s=PADW),
                                      U[:, 2 * p:2 * p + 2, PADW + NP:].rearrange("p f (b s) -> p f b s", s=SEQW)[:, :, :, NS:]
                                      ).then_inc(hrow_ready, 2)
                    sum_of_squares(3)
            sum_of_squares(4)


INPUTS = ["x_prompt", "x_sample", "state_mlstm_C", "state_mlstm_n", "state_mlstm_m", "state_pool", "state_ffn_conv",
          "meta_tokens", "norm_mix", "norm_ffn", "norm_final", "w_mlstm_in", "b_mlstm_gate", "g_mlstm_out",
          "w_mlstm_out", "w_pool", "pool_scale", "w_up", "conv_w", "conv_b", "w_down"]
OUTPUTS = [("y_prompt", (1, SEQ, D)), ("y_sample", (NB, NS, D)), ("C_prompt", (1, 1, H, DK, DV)), ("n_prompt", (1, 1, H, DK)),
           ("m_prompt", (1, 1, H)), ("pool_prompt", (1, 1, PADW, D)), ("conv_prompt", (2, 1, 2, F)),
           ("C_sample", (1, NB, H, DK, DV)), ("n_sample", (1, NB, H, DK)), ("m_sample", (1, NB, H)),
           ("pool_sample", (1, NB, PADW, D)), ("conv_sample", (2, NB, 2, F))]


def kernel(**inputs):
    import numpy as np
    from concourse import bacc
    from concourse.bass_utils import run_bass_kernel_spmd

    nc = bacc.Bacc("TRN2", target_bir_lowering=False, num_devices=1)
    arrays, I, O = {}, {}, {}
    for name in INPUTS:
        a = np.ascontiguousarray(inputs[name])
        arrays[f"in_{name}"] = a
        I[name] = nc.dram_tensor(f"in_{name}", a.shape, mybir.dt.from_np(a.dtype), kind="ExternalInput").ap()
    for name, shape in OUTPUTS:
        O[name] = nc.dram_tensor(f"out_{name}", shape, F32, kind="ExternalOutput").ap()
    program(nc, I, O)
    r = run_bass_kernel_spmd(nc, [arrays], core_ids=[0])
    return tuple(r.results[0][f"out_{name}"] for name, _ in OUTPUTS)
```
